# Optimizing a Trainium2 kernel written in Bass

```python
import jax
import jax.numpy as jnp
from jax import lax
import numpy as np

D_MODEL = 1024
BATCH = 1
SEQ = 512
DEPTH = 1

GRID_W = 64
CTX_LEN = 256
D_MIX = D_MODEL
D_FOURIER = D_MIX // 2
FOURIER_GROUPS = 4
FOURIER_GD = D_FOURIER // FOURIER_GROUPS
D_RG = D_MIX - D_FOURIER
RG_HEADS = 8
RG_HD = D_RG // RG_HEADS
D_IN = D_FOURIER + 2 * D_RG
CONV_W = 4
CONV_PAD_LO = 2
CONV_PAD_HI = CONV_W - 1 - CONV_PAD_LO
RG_C = 8.0
N_EXPERTS = 32
TOP_K = 4
D_FF = D_MODEL
SWIGLU_LIMIT = 7.0
SWIGLU_ALPHA = 1.702
MOE_BLOCK = 256
N_MOD = 6
EPS = 1e-6

kernel_name = 'hybrid_fourier_rglru_moe_dit'

def rmsnorm(x, g):
    xf = x.astype(jnp.float32)
    y = xf * lax.rsqrt(jnp.mean(xf * xf, axis=-1, keepdims=True) + EPS)
    return (y * g.astype(jnp.float32)).astype(x.dtype)

def modulate(h, shift, scale):
    return h * (1 + scale) + shift

def adaln_params(cond, w_mod, b_mod):
    m = jax.nn.silu(cond) @ w_mod + b_mod
    return [t[..., None, :] for t in jnp.split(m, N_MOD, axis=-1)]

def serpentine(t):
    b, n, ch = t.shape
    rows = n // GRID_W
    g = t.reshape(b, rows, GRID_W, ch)
    odd = (jnp.arange(rows) % 2 == 1)[None, :, None, None]
    return jnp.where(odd, g[:, :, ::-1], g).reshape(b, n, ch)

def dwconv_centred(t, w, bias):
    n = t.shape[1]
    tp = jnp.pad(t, ((0, 0), (CONV_PAD_LO, CONV_PAD_HI), (0, 0)))
    out = tp[:, 0:n] * w[0]
    for k in range(1, CONV_W):
        out = out + tp[:, k:k + n] * w[k]
    return out + bias

def blockdiag(t, w, bias):
    b, n, _ = t.shape
    th = t.reshape(b, n, RG_HEADS, RG_HD)
    return jnp.einsum('bnhi,hij->bnhj', th, w).reshape(b, n, D_RG) + bias

def rglru_coeffs(xc, w_a, b_a, w_x, b_x, lam):
    f32 = jnp.float32
    r = jax.nn.sigmoid(blockdiag(xc, w_a.astype(f32), b_a.astype(f32)))
    i = jax.nn.sigmoid(blockdiag(xc, w_x.astype(f32), b_x.astype(f32)))
    log_a = -RG_C * r * jax.nn.softplus(-lam.astype(f32))
    a = jnp.exp(log_a)
    drive = jnp.sqrt(-jnp.expm1(2.0 * log_a)) * (i * xc)
    return a, drive

def linear_recurrence(a, drive, h0):
    drive = drive.at[:, 0].add(a[:, 0] * h0)

    def combine(left, right):
        return (left[0] * right[0], right[0] * left[1] + right[1])

    _, h = lax.associative_scan(combine, (a, drive), axis=1)
    return h

def rglru_bidirectional(xr_lat, xr_ctx, conv_w, conv_b, w_a, b_a, w_x, b_x, lam):
    xc_lat = dwconv_centred(xr_lat, conv_w, conv_b).astype(jnp.float32)
    xc_ctx = dwconv_centred(xr_ctx, conv_w, conv_b).astype(jnp.float32)
    h0 = jnp.zeros((xr_ctx.shape[0], D_RG), jnp.float32)
    ys_lat = []
    ys_ctx = []
    for d in range(2):
        flip = (lambda t: t[:, ::-1]) if d == 1 else (lambda t: t)
        a_c, u_c = rglru_coeffs(flip(xc_ctx), w_a[d], b_a[d], w_x[d], b_x[d], lam[d])
        a_l, u_l = rglru_coeffs(flip(xc_lat), w_a[d], b_a[d], w_x[d], b_x[d], lam[d])
        h_c = linear_recurrence(a_c, u_c, h0)
        h_l = linear_recurrence(a_l, u_l, h_c[:, -1])
        ys_ctx.append(flip(h_c))
        ys_lat.append(flip(h_l))
    return ys_lat[0] + ys_lat[1], ys_ctx[0] + ys_ctx[1]

def fourier_mix(u, w_f):
    b, n, _ = u.shape
    g = u.astype(jnp.float32).reshape(b, n, FOURIER_GROUPS, FOURIER_GD)
    f = jnp.fft.fft2(g, axes=(1, 3), norm='ortho').real
    out = jnp.einsum('bngi,gij->bngj', f, w_f.astype(jnp.float32))
    return out.reshape(b, n, D_FOURIER).astype(u.dtype)

def merge_heads(fourier_out, rg_out, g_out_f, g_out_r, w_out):
    cat = jnp.concatenate([rmsnorm(fourier_out, g_out_f), rmsnorm(rg_out, g_out_r)], axis=-1)
    return cat @ w_out

def token_mixer(h_lat, h_ctx, w_in, w_fourier, conv_w, conv_b, rg_w_a, rg_b_a, rg_w_x, rg_b_x,
                rg_lam, g_out_f, g_out_r, w_out, with_ctx_out):
    cuts = [D_FOURIER, D_FOURIER + D_RG]
    f_lat, xr_lat, gr_lat = jnp.split(h_lat @ w_in, cuts, axis=-1)
    f_ctx, xr_ctx, gr_ctx = jnp.split(h_ctx @ w_in, cuts, axis=-1)
    rg_lat_s, rg_ctx = rglru_bidirectional(serpentine(xr_lat), xr_ctx, conv_w, conv_b,
                                           rg_w_a, rg_b_a, rg_w_x, rg_b_x, rg_lam)
    rg_lat = serpentine(rg_lat_s).astype(h_lat.dtype) * jax.nn.gelu(gr_lat)
    out_lat = merge_heads(fourier_mix(f_lat, w_fourier), rg_lat, g_out_f, g_out_r, w_out)
    if not with_ctx_out:
        return out_lat, None
    rg_c = rg_ctx.astype(h_ctx.dtype) * jax.nn.gelu(gr_ctx)
    out_ctx = merge_heads(fourier_mix(f_ctx, w_fourier), rg_c, g_out_f, g_out_r, w_out)
    return out_lat, out_ctx

def moe_ffn(h, w_router, b_router, w_gu, b_gu, w_down, b_down):
    shp = h.shape
    hf = h.reshape(-1, D_MODEL)
    n_tok = hf.shape[0]
    logits = (hf @ w_router).astype(jnp.float32) + b_router.astype(jnp.float32)
    top_val, top_idx = lax.top_k(logits, TOP_K)
    gates = jax.nn.softmax(top_val, axis=-1)
    n_assign = n_tok * TOP_K
    e_flat = top_idx.reshape(-1).astype(jnp.int32)
    tok_flat = jnp.arange(n_assign, dtype=jnp.int32) // TOP_K
    g_flat = gates.reshape(-1)
    order = jnp.argsort(e_flat)
    e_sorted = e_flat[order]
    counts = jnp.bincount(e_flat, length=N_EXPERTS).astype(jnp.int32)
    padded = (counts + MOE_BLOCK - 1) // MOE_BLOCK * MOE_BLOCK
    pad_end = jnp.cumsum(padded)
    pad_start = pad_end - padded
    grp_start = jnp.cumsum(counts) - counts
    dest = pad_start[e_sorted] + jnp.arange(n_assign, dtype=jnp.int32) - grp_start[e_sorted]
    n_blocks = -(-n_assign // MOE_BLOCK) + N_EXPERTS
    cap = n_blocks * MOE_BLOCK
    row_tok = jnp.zeros((cap,), jnp.int32).at[dest].set(tok_flat[order])
    row_gate = jnp.zeros((cap,), jnp.float32).at[dest].set(g_flat[order])
    blk_start = jnp.arange(n_blocks, dtype=jnp.int32) * MOE_BLOCK
    blk_expert = jnp.minimum(jnp.searchsorted(pad_end, blk_start, side='right'), N_EXPERTS - 1)

    def run_block(args):
        tok, gate, e = args
        xb = hf[tok]
        gu = xb @ w_gu[e] + b_gu[e]
        gt = jnp.minimum(gu[:, :D_FF], SWIGLU_LIMIT)
        up = jnp.clip(gu[:, D_FF:], -SWIGLU_LIMIT, SWIGLU_LIMIT)
        act = (up + 1) * (gt * jax.nn.sigmoid(SWIGLU_ALPHA * gt))
        out = act @ w_down[e] + b_down[e]
        return (out * gate[:, None]).astype(hf.dtype)

    outs = lax.map(run_block, (row_tok.reshape(n_blocks, MOE_BLOCK),
                               row_gate.reshape(n_blocks, MOE_BLOCK), blk_expert))
    y = jnp.zeros_like(hf).at[row_tok].add(outs.reshape(cap, D_MODEL))
    return y.reshape(shp)

def setup_inputs(seed: int = 0) -> dict:
    key = jax.random.key(seed)
    ks = jax.random.split(key, 32)

    def nrm(k, shape, scale):
        return jax.random.normal(k, shape, jnp.float32) * scale

    u = jax.random.uniform(ks[14], (DEPTH, 2, D_RG), jnp.float32, 0.9, 0.999)
    a0 = u ** (1.0 / RG_C)
    rg_lam = jnp.log(a0) - jnp.log1p(-a0)
    return {
        'x': nrm(ks[0], (BATCH, SEQ, D_MODEL), 1.0),
        'c': nrm(ks[1], (BATCH, D_MODEL), 1.0),
        'ctx': nrm(ks[2], (BATCH, CTX_LEN, D_MODEL), 1.0),
        'c_ctx': nrm(ks[3], (D_MODEL,), 1.0),
        'w_mod': nrm(ks[4], (DEPTH, D_MODEL, N_MOD * D_MODEL), 0.5 * D_MODEL ** -0.5),
        'b_mod': nrm(ks[5], (DEPTH, N_MOD * D_MODEL), 0.02),
        'g_norm_mix': 1.0 + nrm(ks[6], (DEPTH, D_MODEL), 0.02),
        'g_norm_ffn': 1.0 + nrm(ks[7], (DEPTH, D_MODEL), 0.02),
        'w_in': nrm(ks[8], (DEPTH, D_MODEL, D_IN), D_MODEL ** -0.5),
        'w_fourier': nrm(ks[9], (DEPTH, FOURIER_GROUPS, FOURIER_GD, FOURIER_GD), FOURIER_GD ** -0.5),
        'conv_w': nrm(ks[10], (DEPTH, CONV_W, D_RG), CONV_W ** -0.5),
        'conv_b': nrm(ks[11], (DEPTH, D_RG), 0.02),
        'rg_w_a': nrm(ks[12], (DEPTH, 2, RG_HEADS, RG_HD, RG_HD), RG_HD ** -0.5),
        'rg_b_a': nrm(ks[13], (DEPTH, 2, D_RG), 0.02),
        'rg_w_x': nrm(ks[15], (DEPTH, 2, RG_HEADS, RG_HD, RG_HD), RG_HD ** -0.5),
        'rg_b_x': nrm(ks[16], (DEPTH, 2, D_RG), 0.02),
        'rg_lam': rg_lam,
        'g_out_fourier': 1.0 + nrm(ks[17], (DEPTH, D_FOURIER), 0.02),
        'g_out_rg': 1.0 + nrm(ks[18], (DEPTH, D_RG), 0.02),
        'w_out': nrm(ks[19], (DEPTH, D_MIX, D_MODEL), D_MIX ** -0.5),
        'w_router': nrm(ks[20], (DEPTH, D_MODEL, N_EXPERTS), D_MODEL ** -0.5),
        'b_router': nrm(ks[21], (DEPTH, N_EXPERTS), 0.01),
        'w_gate_up': nrm(ks[22], (DEPTH, N_EXPERTS, D_MODEL, 2 * D_FF), D_MODEL ** -0.5),
        'b_gate_up': nrm(ks[23], (DEPTH, N_EXPERTS, 2 * D_FF), 0.01),
        'w_down': nrm(ks[24], (DEPTH, N_EXPERTS, D_FF, D_MODEL), D_FF ** -0.5),
        'b_down': nrm(ks[25], (DEPTH, N_EXPERTS, D_MODEL), 0.01),
        'g_final': 1.0 + nrm(ks[26], (D_MODEL,), 0.02),
    }

def reference(x, c, ctx, c_ctx, w_mod, b_mod, g_norm_mix, g_norm_ffn, w_in, w_fourier, conv_w,
              conv_b, rg_w_a, rg_b_a, rg_w_x, rg_b_x, rg_lam, g_out_fourier, g_out_rg, w_out,
              w_router, b_router, w_gate_up, b_gate_up, w_down, b_down, g_final):
    y = ctx
    for i in range(DEPTH):
        last = i == DEPTH - 1
        sh_m, sc_m, gt_m, sh_f, sc_f, gt_f = adaln_params(c, w_mod[i], b_mod[i])
        csh_m, csc_m, cgt_m, csh_f, csc_f, cgt_f = adaln_params(c_ctx, w_mod[i], b_mod[i])
        h_lat = modulate(rmsnorm(x, g_norm_mix[i]), sh_m, sc_m)
        h_ctx = modulate(rmsnorm(y, g_norm_mix[i]), csh_m, csc_m)
        mix_lat, mix_ctx = token_mixer(h_lat, h_ctx, w_in[i], w_fourier[i], conv_w[i], conv_b[i],
                                       rg_w_a[i], rg_b_a[i], rg_w_x[i], rg_b_x[i], rg_lam[i],
                                       g_out_fourier[i], g_out_rg[i], w_out[i], not last)
        x = x + gt_m * mix_lat
        h = modulate(rmsnorm(x, g_norm_ffn[i]), sh_f, sc_f)
        x = x + gt_f * moe_ffn(h, w_router[i], b_router[i], w_gate_up[i], b_gate_up[i],
                               w_down[i], b_down[i])
        if not last:
            y = y + cgt_m * mix_ctx
            hc = modulate(rmsnorm(y, g_norm_ffn[i]), csh_f, csc_f)
            y = y + cgt_f * moe_ffn(hc, w_router[i], b_router[i], w_gate_up[i], b_gate_up[i],
                                    w_down[i], b_down[i])
    return rmsnorm(x, g_final)


_drawn_inputs = setup_inputs


def setup_inputs(seed=0):
    import zlib

    import numpy as np

    out = dict(_drawn_inputs(seed))
    spreads = {}
    factors = {'g_norm_mix': 5.076,
     'g_norm_ffn': 3.339,
     'rg_b_a': 8.0,
     'rg_b_x': 8.0,
     'g_out_fourier': 6.766,
     'g_out_rg': 7.54,
     'b_router': 21.202,
     'b_gate_up': 22.649,
     'b_down': 64.0,
     'g_final': 7.827}
    for name, (base, spread) in spreads.items():
        noise = np.random.default_rng([zlib.crc32(name.encode()), seed]).standard_normal(out[name].shape)
        drawn = base * np.exp(spread * noise) if base else spread * noise
        out[name] = jnp.asarray(drawn.astype(out[name].dtype))
    for name, factor in factors.items():
        out[name] = (out[name] * factor).astype(out[name].dtype)
    return out
```

```python
import numpy as np
import concourse.bass as bass
from concourse import mybir
from contextlib import ExitStack

F32 = mybir.dt.float32
F32R = mybir.dt.float32r
BF16 = mybir.dt.bfloat16
I32 = mybir.dt.int32
U32 = mybir.dt.uint32
ALU = mybir.AluOpType
ACT = mybir.ActivationFunctionType
AX = mybir.AxisListType

P = 128
D = 1024
KD = D // P
NL, NC = 512, 256
TL, TC = NL // P, NC // P
DF = 512
DR = 512
GT = DF // P
RT = DR // P
GRID_W = 64
TAPS, PAD_LO = 4, 2
NE, TOPK = 32, 4
FF = 1024
CH = 512
EPS = 1e-6
LIMIT, ALPHA = 7.0, 1.702
RG_C = 8.0
NS = NL // P - 1 + NL * TOPK // P
NS = NL * TOPK // P
NI = NE + NS
OUT_OF_RANGE = 4096
KB = 1024

COLS = {}
_at = 0
for _name, _n in (("c", KD), ("c_ctx", KD), ("g_mix", KD), ("b_shift", KD), ("b_scale", KD),
                  ("conv_w", TAPS * RT), ("conv_b", RT), ("b_a", 2 * RT), ("b_x", 2 * RT),
                  ("lam", 2 * RT), ("g_f", GT), ("g_r", RT)):
    COLS[_name] = (_at, _at + _n)
    _at += _n
NCOL = _at

CST = {}
_at = 0
for _name, _n in (("ident", P), ("cd", P), ("neg_sd", P), ("ones", P), ("slot", P), ("before", P),
                  ("expert", NE), ("expert_of_row", 1), ("token", 2 * TL), ("extra", NS)):
    CST[_name] = (_at, _at + _n)
    _at += _n
NCST = _at


def serpentine_order():
    t = np.arange(NL).reshape(NL // GRID_W, GRID_W)
    t[1::2] = t[1::2, ::-1]
    return t.reshape(-1)


def constants():
    p = np.arange(P)
    c = np.zeros((P, NCST), np.float32)

    def put(name, a):
        c[:, CST[name][0]:CST[name][1]] = a

    put("ident", np.eye(P))
    ang = 2 * np.pi * ((p[:, None] * p[None]) % P) / P
    put("cd", np.cos(ang) / np.sqrt(P))
    put("neg_sd", -np.sin(ang) / np.sqrt(P))
    put("ones", 1.0)
    put("slot", p[None])
    put("before", (p[:, None] < p[None]).astype(np.float32))
    put("expert", np.arange(NE)[None])
    put("expert_of_row", (p % NE)[:, None])
    put("token", np.stack([np.tile(p[:, None], (1, TL)), np.tile(P * np.arange(TL) - OUT_OF_RANGE, (P, 1))], 2).reshape(P, 2 * TL))
    put("extra", np.arange(NS)[None])
    n = serpentine_order()
    ang = 2 * np.pi * ((n[:, None] * n[None]) % NL) / NL
    dft = np.stack([np.cos(ang), np.sin(ang)]) / np.sqrt(NL)
    return c, dft.astype(np.float32)


def build(nc, x, ctx, w_mod, b_mod, w_in, w_fourier, rg_w_a, rg_w_x, w_out, w_router, b_router,
          w_gate_up, b_gate_up, w_down, b_down, g_norm_ffn, g_final, cols, cst, dft, out):
    h_dram = nc.dram_tensor("h_rows", (NL, D), F32, kind="Internal").ap()
    y_dram = nc.dram_tensor("y_rows", (NL, D), F32, kind="Internal").ap()

    with ExitStack() as stack:
        base = 16512
        RING = base
        SLOT = [RING + 16 * KB * i for i in range(6)]
        ZA = RING + 96 * KB
        ZB = ZA + 24 * KB
        ZD = ZB + 22 * KB
        ZX = ZD + 32 * KB
        SM = ZX + 16 * KB

        def at(name, shape, off, dt=F32):
            return nc.alloc_sbuf_tensor_at(name, shape, dt, offset=off)

        small_at = [SM]

        def small(name, shape, dt=F32):
            n = int(np.prod(shape[1:])) * mybir.dt.size(dt)
            t = at(name, shape, small_at[0], dt)
            small_at[0] += -(-n // 32) * 32
            assert small_at[0] <= 229344, name
            return t

        ps = stack.enter_context(nc.psum_tensor("ps", [P, 8, 512], F32))

        def sem(name):
            return stack.enter_context(nc.semaphore(name))

        wm_first = [at("wm_0", [P, KD, CH], ZD), at("wm_1", [P, KD, CH], ZD + 16 * KB),
                    at("wm_2", [P, KD, CH], SLOT[3]), at("wm_3", [P, KD, CH], SLOT[4])]
        wm_rest = [at("wm_a", [P, KD, CH], ZD), at("wm_b", [P, KD, CH], ZD + 16 * KB)]
        x_in = at("x_in", [P, TL, D], ZX)
        c_in = at("c_in", [P, TC, D], ZB)
        xs_c = at("xs_c", [P, TC, D], ZB + 8 * KB)
        junk = at("junk", [P, D], ZB + 16 * KB)
        wf = at("wf", [P, GT, P], ZB + 20 * KB)
        xs_l = at("xs_l", [P, TL, D], SLOT[5])
        win = [at(f"win_{i}", [P, KD, CH], SLOT[i]) for i in range(3)]
        hT_l = at("hT_l", [P, KD, NL], ZA)
        hT_c = at("hT_c", [P, KD, NC], ZA + 16 * KB)
        z_buf = [at(f"z_{i}", [P, CH], SLOT[5] + (8 + 2 * i) * KB) for i in range(2)]
        gnf = at("gnf", [P, D], SLOT[5] + 12 * KB)
        bc = at("bc", [P, 4, D], ZX)
        fT = at("fT", [P, GT, NL], SLOT[5])
        dft_sb = at("dft_sb", [P, 2, TL, NL], SLOT[4])
        Y = at("Y", [P, TL, 2, DF], ZA)
        catF = at("catF", [P, GT, NL], SLOT[5])
        NX = PAD_LO + NC + 1 + PAD_LO + NL + 1
        LAT0 = NC + 3
        xp = [at(f"xp_{i}", [P, NX], ZB + 3200 * i) for i in range(2)]
        cv = at("cv", [P, NX - 3], ZB + 6400)
        NB = NC + NL
        xc = at("xc", [P, RT, NB], ZB + 9600)
        gelu = at("gelu", [P, RT, NL], ZA + 16 * KB)
        Am = at("Am", [P, 2, RT, NB], SLOT[0])
        Um = at("Um", [P, 2, RT, NB], SLOT[1] + 8 * KB)
        Rm = at("Rm", [P, RT, NB], SLOT[3])
        Qm = [at(f"Qm_{i}", [P, NB], ZB + 3200 * i) for i in range(2)]
        sqF = at("sqF", [P, GT, NL], ZB + 9600)
        wo = [at("wo_f", [P, GT, D], ZD), at("wo_r", [P, RT, D], ZD + 16 * KB)]
        xl = at("xl", [P, TL, D], ZA)
        Fb = at("Fb", [P, TL, D], SLOT[4])
        h_sb = at("h_sb", [P, TL, D], SLOT[3])
        hT2 = at("hT2", [P, KD, P], SLOT[5])
        junk2 = at("junk2", [P, D], ZA + 16 * KB)
        RA = ZB
        lg = at("lg", [P, TL, NE], RA)
        ex = at("ex", [P, TL, NE], RA + 512)
        one = at("one", [P, TL, NE], RA + 1024)
        msk = at("msk", [P, TL, NE], RA + 1536)
        gts = at("gts", [P, TL, NE], RA + 2048)
        gtr = at("gtr", [P, TL, NE], RA + 2560)
        mskb = at("mskb", [P, TL, NE], RA + 3072, BF16)
        gtb = at("gtb", [P, TL, NE], RA + 3328, BF16)
        m8 = at("m8", [P, TL, 8], RA + 3584)
        i8 = at("i8", [P, TL, 8], RA + 3712, U32)
        if8 = at("if8", [P, TL, 8], RA + 3840)
        cnt = at("cnt", [P, NE], RA + 3968)
        ovf = at("ovf", [P, NE], RA + 4096)
        end = at("end", [P, NE], RA + 4224)
        beg = at("beg", [P, NE], RA + 4352)
        mq = at("mq", [P, NS, NE], RA + 4480)
        mq2 = at("mq2", [P, NS, NE], RA + 4480 + 2048)
        rs8 = at("rs8", [P, 8], RA + 4480 + 4096)
        slots = [at(f"slot_{i}", [P, 8 * CH], SLOT[i]) for i in range(6)]
        xg = at("xg", [P, D], ZB + 16 * KB)
        bias_raw = at("bias_raw", [2 * NE, 3 * D], ZD)
        bias_w = at("bias_w", [P, 3 * D], ZD + 12 * KB, F32R)
        gfin = at("gfin", [P, D], ZD + 24 * KB)
        osb = at("osb", [P, D], ZD + 28 * KB)
        gb = at("gb", [P, CH], ZD)
        ub = at("ub", [P, CH], ZD + 2 * KB)
        sg = at("sg", [P, CH], ZD + 4 * KB)
        ab = at("ab", [P, CH], ZD + 6 * KB)
        aT = at("aT", [P, 8, P], ZD + 8 * KB)
        xT = at("xT", [P, KD, P], ZX)
        y_sb = at("y_sb", [P, TL, D], SLOT[0])
        o_sb = at("o_sb", [P, TL, D], SLOT[1])
        junk3 = at("junk3", [P, D], SLOT[2])
        zero = at("zero", [P, D], ZA + 20 * KB)

        wbd_at = small_at[0]
        wbd = small("wbd", [P, 2, 2 * RT, P])
        csb = small("csb", [P, NCST])
        pc = small("pc", [P, NCOL])
        MM = at("MM", [P, GT, 2, P], SLOT[5] + 12 * KB)
        csil = small("csil", [P, KD, 2])
        sh = small("sh", [P, KD, 2])
        sc = small("sc", [P, KD, 2])
        ss = small("ss", [P, 6])
        nsp = small("nsp", [P, 3, 2 * RT])
        sp_t = small("sp_t", [P, 6, 2 * RT])
        rsf = small("rsf", [P, 4, TL])
        wr = small("wr", [P, KD, NE])
        br = small("br", [P, NE])
        beforeb = small("beforeb", [P, P], BF16)
        onesb = small("onesb", [P, P], BF16)
        small_at[0], keep = wbd_at, small_at[0]
        posm = small("posm", [P, TL, NE])
        meta = small("meta", [P, TL, NE, 5], BF16)
        item_e = small("item_e", [P, NI + 1])
        item_o = small("item_o", [P, NI + 1])
        item_i = small("item_i", [P, NI + 1], I32)
        n_items = small("n_items", [P, 1], I32)
        sel = small("sel", [P, TL, P], BF16)
        metab = small("metab", [P, TL, 5], BF16)
        pick = small("pick", [P, P], F32R)
        msb = small("msb", [P, 5])
        idx_n = small("idx_n", [P, 1], I32)
        idx_c = small("idx_c", [P, 1], I32)
        gate_n = small("gate_n", [P, 1])
        gate_c = small("gate_c", [P, 1])
        assert small_at[0] <= wbd_at + 8 * KB
        small_at[0] = keep

        def col(name):
            a, b = COLS[name]
            return pc[:, a:b]

        def const(name):
            a, b = CST[name]
            return csb[:, a:b]

        ident, ones = const("ident"), const("ones")

        wm_v = w_mod.rearrange("(k p) n -> p k n", p=P)
        win_v = w_in.rearrange("(k p) n -> p k n", p=P)
        wo_v = w_out.rearrange("(k p) n -> p k n", p=P)
        wgu_v = w_gate_up.rearrange("e (k p) n -> e p k n", p=P)
        wd_v = w_down.rearrange("e (k p) n -> e p k n", p=P)
        rows = lambda a: a.rearrange("(t p) d -> p t d", p=P)

        names = """ld_cols ld_cst ld_wf ld_ctx ld_x ld_wm0 ld_wm1 ld_wm2 ld_wm3 ld_win0 ld_win1 ld_win2
            ld_wbd ld_zm0 ld_zm1 ld_dft ld_bc ld_gnf ld_wo0 ld_wo1 ld_xl ld_wr ld_bias ld_gfin
            dve_step act_step pool_step
            csil_ready mod_done film_ready edges_zero wbd_zero bf_ready rstd_in ssq_in xs_ready tc_done tl_done
            hc_copied hl_by_act hl_by_dve mm_done mm_copied xr_done xr_copied conv_done gr_done gelu_done
            f_done f_copied gate_mm sig_done z_ready z_done bc_ready y_done y_copied dft_done cf_copied
            ssf_done sp_ready ix_ready a_ready th_ready q_ready w_ready root_ready rg_ready sqr_ready
            ssr_done rsf_act rsf_ready pf_done pf_copied pr_done pr_read x2_ready ssq_ffn rt_ffn h_ready h_stored
            ht_done ht_copied lg_done m8_ready ex_ready mask_ready pos_done table_ready y_zero
            bias_ready gate_free xg_zero dve_u
            meta_done at_done xt_done o_done bias_used g_ready act_ready sel_ready idx_ready
            cur_ready pick_ready s_sig aT_copied xT_copied o_copied gathered scattered
            y_loaded ssq_out rt_out out_ready stored"""
        S = {n: sem(n) for n in names.split()}
        w_ld = [sem(f"w_loaded_{c}") for c in range(6)]
        w_free = [sem(f"w_free_{c}") for c in range(6)]

        def chunk_src(c, e):
            if c < 4:
                n0 = (c % 2) * FF + (c // 2) * CH
                return wgu_v[e, :, :, n0:n0 + CH]
            return wd_v[e, :, (c - 4) * 4:(c - 3) * 4, :]

        def chunk_dst(c):
            return slots[c][:, :].rearrange("p (k n) -> p k n", k=8 if c < 4 else 4)

        def pair(i):
            return ps[:, 2 * i:2 * i + 2, :].rearrange("p b n -> p (b n)")

        def z_bank(i):
            return 4 if i == 0 else 2 + i % 2

        block = stack.enter_context(nc.Block())

        @block.sync
        def _(sp):
            def load(dst, src, name, n=16):
                sp.dma_start(dst, src).then_inc(S[name], 16)

            load(pc[:, :], cols, "ld_cols")
            load(csb[:, :], cst, "ld_cst")
            load(wm_first[0][:, :, :], wm_v[:, :, 0:CH], "ld_wm0")
            load(c_in[:, :, :], rows(ctx), "ld_ctx")
            load(wm_first[1][:, :, :], wm_v[:, :, CH:2 * CH], "ld_wm1")
            load(wm_first[2][:, :, :], wm_v[:, :, 2 * CH:3 * CH], "ld_wm2")
            load(wm_first[3][:, :, :], wm_v[:, :, 3 * CH:4 * CH], "ld_wm3")
            load(x_in[:, :, :], rows(x), "ld_x")
            load(wf[:, :, :], w_fourier.rearrange("g i j -> i g j"), "ld_wf")
            for i in (1, 2, 0):
                load(win[i][:, :, :], win_v[:, :, i * CH:(i + 1) * CH], f"ld_win{i}")
            sp.wait_ge(S["wbd_zero"], 1)
            for a, w in enumerate((rg_w_a, rg_w_x)):
                v = w.rearrange("d (t s) i j -> s i (d t) j", s=2)
                for s in range(2):
                    load(wbd[64 * s:64 * s + 64, a, :, 64 * s:64 * s + 64], v[s], "ld_wbd")
            load(wr[:, :, :], w_router.rearrange("(k p) e -> p k e", p=P), "ld_wr")
            load(br[:, :], b_router.partition_broadcast(P), "ld_wr")
            for i in range(8):
                if i < 2:
                    sp.wait_ge(S["mod_done"], i + 1)
                else:
                    sp.wait_ge(S["z_ready"], i - 1)
                load(wm_rest[i % 2][:, :, :], wm_v[:, :, (4 + i) * CH:(5 + i) * CH], f"ld_zm{i % 2}")
                if i == 0:
                    sp.wait_ge(S["xs_ready"], 6)
                    load(bc[:, :, :].rearrange("p a d -> p (a d)"), b_mod[2 * D:6 * D].partition_broadcast(P), "ld_bc")
                if i == 1:
                    sp.wait_ge(S["mod_done"], 4)
                    load(dft_sb[:, 0, :, :], dft[0].rearrange("(m p) n -> p m n", p=P), "ld_dft")
                    load(dft_sb[:, 1, :, :], dft[1].rearrange("(m p) n -> p m n", p=P), "ld_dft")
            sp.wait_ge(S["y_done"], TL)
            load(gnf[:, :], g_norm_ffn.partition_broadcast(P), "ld_gnf")
            for i in range(2):
                sp.wait_ge(S["z_ready"], 7 + i)
                load(wo[i][:, :, :], wo_v[:, 4 * i:4 * i + 4, :], f"ld_wo{i}")
            sp.wait_ge(S["dft_done"], GT)
            load(xl[:, :, :], rows(x), "ld_xl")
            sp.wait_ge(S["ssr_done"], 1)
            sp.dma_start(chunk_dst(0), chunk_src(0, 0)).then_inc(w_ld[0], 16)
            sp.wait_ge(S["pr_done"], TL)
            sp.dma_start(chunk_dst(1), chunk_src(1, 0)).then_inc(w_ld[1], 16)
            sp.dma_start(chunk_dst(2), chunk_src(2, 0)).then_inc(w_ld[2], 16)
            load(bias_raw[0:NE, 0:2 * FF], b_gate_up, "ld_bias")
            load(bias_raw[NE:2 * NE, 0:2 * FF], b_gate_up, "ld_bias")
            load(bias_raw[0:NE, 2 * FF:], b_down, "ld_bias")
            load(bias_raw[NE:2 * NE, 2 * FF:], b_down, "ld_bias")
            load(gfin[:, :], g_final.partition_broadcast(P), "ld_gfin")
            for t in range(TL):
                sp.wait_ge(S["h_ready"], t + 1)
                sp.dma_start(h_dram[t * P:(t + 1) * P, :], h_sb[:, t, :]).then_inc(S["h_stored"], 16)
            sp.wait_ge(S["x2_ready"], TL)
            sp.dma_start(chunk_dst(4), chunk_src(4, 0)).then_inc(w_ld[4], 16)
            sp.wait_ge(S["lg_done"], TL)
            sp.dma_start(chunk_dst(5), chunk_src(5, 0)).then_inc(w_ld[5], 16)
            sp.wait_ge(S["h_stored"], 16 * TL)
            sp.dma_start(chunk_dst(3), chunk_src(3, 0)).then_inc(w_ld[3], 16)
            sp.wait_ge(S["table_ready"], 1)
            n = sp.value_load(n_items[0:1, 0:1], min_val=NE, max_val=NI)
            with sp.Fori(1, NI) as b:
                with sp.If(b < n):
                    e = sp.value_load(item_i[0:1, bass.ds(b, 1)], min_val=0, max_val=NE - 1)
                    for c in range(6):
                        sp.wait_ge(w_free[c], b)
                        sp.dma_start(chunk_dst(c), chunk_src(c, e)).then_inc(w_ld[c], 16)
            sp.wait_ge(S["gathered"], 16 * (n + 1))
            sp.wait_ge(S["scattered"], 16 * (n + 1))
            for t in range(TL):
                sp.dma_start(y_sb[:, t, :], y_dram[t * P:(t + 1) * P, :]).then_inc(S["y_loaded"], 16)
                sp.wait_ge(S["y_loaded"], 16 * (t + 1))
            for t in range(TL):
                sp.wait_ge(S["out_ready"], t + 1)
                sp.dma_start(out[t * P:(t + 1) * P, :], o_sb[:, t, :]).then_inc(S["stored"], 16)
            sp.wait_ge(S["stored"], 16 * TL)

        @block.gpsimd
        def _(pool):
            nc.gpsimd.memset(wbd[:, :, :, :], 0.0).then_inc(S["wbd_zero"], 1)
            pool.wait_ge(S["ld_cst"], 16)
            nc.gpsimd.tensor_copy(beforeb[:, :], const("before"))
            nc.gpsimd.tensor_copy(onesb[:, :], ones).then_inc(S["bf_ready"], 1)
            pool.wait_ge(S["tc_done"], 4)
            for i in range(2):
                nc.gpsimd.memset(xp[i][:, 0:PAD_LO], 0.0)
                nc.gpsimd.memset(xp[i][:, PAD_LO + NC:PAD_LO + NC + 3], 0.0)
                last = nc.gpsimd.memset(xp[i][:, NX - 1:NX], 0.0)
            last.then_inc(S["edges_zero"], 1)
            for n in range(2 * RT):
                d, t = n // RT, n % RT
                pool.wait_ge(S["a_ready"], n + 1)
                if n == 0:
                    pool.wait_ge(S["conv_done"], RT)
                if n >= 2:
                    pool.wait_ge(S["w_ready"], n - 1)
                nc.gpsimd.tensor_tensor(Qm[n % 2][:, :], Am[:, d, t, :], Am[:, d, t, :], ALU.mult).then_inc(S["q_ready"], 1)
            pool.wait_ge(S["rg_ready"], RT)
            nc.gpsimd.memset(zero[:, :], 0.0).then_inc(S["y_zero"], 1)
            pool.wait_ge(S["y_zero"], 1)
            pool.dma_start(rows(y_dram), zero[:, :].unsqueeze(1).to_broadcast([P, TL, D])).then_inc(S["scattered"], 16)
            pool.wait_ge(S["ld_bias"], 64)
            nc.gpsimd.memset(bias_w[2 * NE:P, :].bitcast(F32), 0.0)
            nc.gpsimd.tensor_copy(bias_w[0:2 * NE, :], bias_raw[:, :]).then_inc(S["pool_step"], 1)
            pool.wait_ge(S["pool_step"], 1)
            nc.gpsimd.tensor_tensor(bias_w[NE:2 * NE, :], bias_raw[NE:2 * NE, :], bias_w[NE:2 * NE, :].bitcast(F32),
                                    ALU.subtract).then_inc(S["bias_ready"], 1)
            pool.wait_ge(S["cf_copied"], GT)
            pool.wait_ge(S["ssf_done"], 1)
            pool.wait_ge(S["bias_ready"], 1)
            nc.gpsimd.memset(osb[:, :], 0.0).then_inc(S["o_copied"], 2)
            nc.gpsimd.memset(xg[:, :], 0.0).then_inc(S["xg_zero"], 1)
            pool.wait_ge(S["xg_zero"], 1)
            pool.wait_ge(S["h_stored"], 16 * TL)

            last_row = pool.to_reg(NL - 1)

            def gather():
                pool.indirect_dma_start(xg[:, :], None, h_dram, bass.IndirectOffsetOnAxis(ap=idx_n[:, 0:1], axis=0),
                                        bounds_check=last_row, oob_is_err=False).then_inc(S["gathered"], 16)

            pool.wait_ge(S["idx_ready"], 1)
            gather()
            n = pool.value_load(n_items[0:1, 0:1], min_val=NE, max_val=NI)
            with pool.Fori(0, NI) as b:
                with pool.If(b < n):
                    pool.wait_ge(S["idx_ready"], b + 2)
                    pool.wait_ge(S["xt_done"], 2 * b + 2)
                    pool.nop(nofuse=True)
                    gather()
                    pool.wait_ge(S["cur_ready"], b + 1)
                    pool.wait_ge(S["o_copied"], 2 * b + 4)
                    pool.wait_ge(S["scattered"], 16 * b + 16)
                    pool.nop(nofuse=True)
                    pool.indirect_dma_start(y_dram, bass.IndirectOffsetOnAxis(ap=idx_c[:, 0:1], axis=0), osb[:, :], None,
                                            bounds_check=last_row, oob_is_err=False, compute_op=ALU.add
                                            ).then_inc(S["scattered"], 16)

        @block.scalar
        def _(act):
            A = nc.scalar.activation
            act.wait_ge(S["ld_cols"], 16)
            a0 = COLS["c"][0]
            A(sp_t[:, 0:2, :].rearrange("p a b -> p (a b)"), pc[:, a0:a0 + 2 * KD], ACT.Sigmoid).then_inc(S["act_step"], 1)
            act.wait_ge(S["ld_ctx"], 16)
            for t in range(TC):
                A(junk[:, :], c_in[:, t, :], ACT.Square, accum_out=ss[:, t:t + 1]).then_inc(S["ssq_in"], 1)
                act.wait_ge(S["ssq_in"], t + 1)
            act.wait_ge(S["ld_x"], 16)
            for t in range(TL):
                A(junk[:, :], x_in[:, t, :], ACT.Square, accum_out=ss[:, TC + t:TC + t + 1]).then_inc(S["ssq_in"], 1)
                act.wait_ge(S["ssq_in"], TC + t + 1)
            act.wait_ge(S["rstd_in"], 1)
            A(ss[:, :], ss[:, :], ACT.Sqrt).then_inc(S["rstd_in"], 1)
            act.wait_ge(S["film_ready"], 1)
            for i in range(4):
                act.wait_ge(S["tc_done"], i + 1)
                for k in (2 * i, 2 * i + 1):
                    last = A(hT_c[:, k, :], ps[:, 1 + i, (k % 2) * NC:(k % 2 + 1) * NC], ACT.Identity,
                             bias=sh[:, k, 1:2], scale=sc[:, k, 1:2])
                last.then_inc(S["hc_copied"], 1)
            for k in range(0, KD, 2):
                act.wait_ge(S["tl_done"], k + 1)
                A(hT_l[:, k, :], ps[:, (5 + k) % 8, :], ACT.Identity, bias=sh[:, k, 0:1], scale=sc[:, k, 0:1]).then_inc(S["hl_by_act"], 1)
            act.wait_ge(S["edges_zero"], 1)
            for t in range(RT):
                act.wait_ge(S["xr_done"], t + 1)
                if t >= 2:
                    act.wait_ge(S["conv_done"], t - 1)
                A(xp[t % 2][:, PAD_LO:PAD_LO + NC], ps[:, t % 2, 0:NC], ACT.Copy)
                A(xp[t % 2][:, NC + 5:NC + 5 + NL], ps[:, 2 + t % 2, :], ACT.Copy).then_inc(S["xr_copied"], 1)
            for t in range(RT):
                act.wait_ge(S["gr_done"], t + 1)
                A(gelu[:, t, :], ps[:, 4 + t, :], ACT.Gelu_apprx_tanh).then_inc(S["gelu_done"], 1)
            act.wait_ge(S["sp_ready"], 1)
            A(sp_t[:, 2, :], sp_t[:, 1, :], ACT.Exp, scale=-1.0).then_inc(S["sp_ready"], 1)
            for d in range(2):
                for t in range(RT):
                    n = 2 * (RT * d + t)
                    act.wait_ge(S["gate_mm"], n + 1)
                    if d == 1 and t == 0:
                        act.wait_ge(S["root_ready"], RT)
                        act.wait_ge(S["ix_ready"], 2 * RT)
                    A(Rm[:, t, :], pair(n % 2)[:, NC:NC + NB], ACT.Sigmoid,
                      bias=pc[:, COLS["b_a"][0] + RT * d + t:COLS["b_a"][0] + RT * d + t + 1]).then_inc(S["sig_done"], 1)
                    act.wait_ge(S["gate_mm"], n + 2)
                    A(Um[:, d, t, :], pair((n + 1) % 2)[:, NC:NC + NB], ACT.Sigmoid,
                      bias=pc[:, COLS["b_x"][0] + RT * d + t:COLS["b_x"][0] + RT * d + t + 1]).then_inc(S["sig_done"], 1)
                if d == 0:
                    act.wait_ge(S["sp_ready"], 3)
                for t in range(RT):
                    m = RT * d + t
                    act.wait_ge(S["sig_done"], 2 * m + 1)
                    A(Am[:, d, t, :], Rm[:, t, :], ACT.Exp, scale=nsp[:, 0, m:m + 1]).then_inc(S["a_ready"], 1)
                for t in range(RT):
                    m = RT * d + t
                    act.wait_ge(S["a_ready"], m + 1)
                    A(Rm[:, t, :], Rm[:, t, :], ACT.Tanh, scale=nsp[:, 1, m:m + 1]).then_inc(S["th_ready"], 1)
                for t in range(RT):
                    m = RT * d + t
                    act.wait_ge(S["w_ready"], m + 1)
                    A(Rm[:, t, :], Rm[:, t, :], ACT.Sqrt).then_inc(S["root_ready"], 1)
            act.wait_ge(S["ix_ready"], 3 * RT)
            for g in range(GT):
                act.wait_ge(S["dft_done"], g + 1)
                A(sqF[:, g, :], ps[:, 4 + g, :], ACT.Square)
                A(catF[:, g, :], ps[:, 4 + g, :], ACT.Copy, scale=pc[:, COLS["g_f"][0] + g:COLS["g_f"][0] + g + 1]).then_inc(S["cf_copied"], 1)
            act.wait_ge(S["rsf_act"], 1)
            A(rsf[:, 1, :], rsf[:, 0, :], ACT.Sqrt).then_inc(S["rsf_act"], 1)
            act.wait_ge(S["rsf_ready"], 1)
            for t in range(TL):
                act.wait_ge(S["pf_done"], t + 1)
                A(Fb[:, t, :], pair(1 + t % 3), ACT.Copy, scale=rsf[:, 0, t:t + 1]).then_inc(S["pf_copied"], 1)
            for t in range(RT):
                act.wait_ge(S["rg_ready"], t + 1)
                A(Um[:, 1, t, NC:], Um[:, 0, t, NC:], ACT.Square).then_inc(S["act_step"], 1)
                act.wait_ge(S["act_step"], t + 2)
                A(Um[:, 0, t, NC:], Um[:, 0, t, NC:], ACT.Copy, scale=pc[:, COLS["g_r"][0] + t:COLS["g_r"][0] + t + 1]).then_inc(S["sqr_ready"], 1)
            act.wait_ge(S["rsf_act"], 3)
            A(rsf[:, 3, :], rsf[:, 2, :], ACT.Sqrt).then_inc(S["rsf_act"], 1)
            for t in range(TL):
                act.wait_ge(S["x2_ready"], t + 1)
                if t:
                    act.wait_ge(S["ssq_ffn"], 2 * t - 1)
                A(junk2[:, :], xl[:, t, :], ACT.Square, accum_out=ss[:, t:t + 1]).then_inc(S["ssq_ffn"], 1)
                act.wait_ge(S["ssq_ffn"], 2 * t + 2)
                A(rsf[:, 1, t:t + 1], rsf[:, 0, t:t + 1], ACT.Sqrt).then_inc(S["rt_ffn"], 1)
            for t in range(TL):
                act.wait_ge(S["ht_done"], 2 * t + 2)
                if t:
                    act.wait_ge(S["lg_done"], t)
                A(hT2[:, :, :].rearrange("p k n -> p (k n)"), pair(1 + t % 2), ACT.Copy).then_inc(S["ht_copied"], 1)
            act.wait_ge(S["m8_ready"], 1)
            for t in range(TL):
                last = A(ex[:, t, :], lg[:, t, :], ACT.Exp, bias=rs8[:, t:t + 1])
            last.then_inc(S["ex_ready"], 1)

            def copy_xT(h, v):
                act.wait_ge(S["xt_done"], v)
                A(xT[:, 4 * h:4 * h + 4, :].rearrange("p k n -> p (k n)"), ps[:, h, :], ACT.Copy).then_inc(S["xT_copied"], 1)

            copy_xT(0, 1)
            copy_xT(1, 2)
            n = act.value_load(n_items[0:1, 0:1], min_val=NE, max_val=NI)
            with act.Fori(0, NI) as b:
                with act.If(b < n):
                    act.wait_ge(S["g_ready"], 2 * b + 1)
                    A(sg[:, :], gb[:, :], ACT.Sigmoid, scale=ALPHA).then_inc(S["s_sig"], 1)
                    act.wait_ge(S["at_done"], 2 * b + 1)
                    A(aT[:, 0:4, :].rearrange("p k n -> p (k n)"), ps[:, 6, :], ACT.Copy).then_inc(S["aT_copied"], 1)
                    act.wait_ge(S["g_ready"], 2 * b + 2)
                    A(sg[:, :], gb[:, :], ACT.Sigmoid, scale=ALPHA).then_inc(S["s_sig"], 1)
                    copy_xT(0, 2 * b + 3)
                    copy_xT(1, 2 * b + 4)
                    act.wait_ge(S["at_done"], 2 * b + 2)
                    A(aT[:, 4:8, :].rearrange("p k n -> p (k n)"), ps[:, 6, :], ACT.Copy).then_inc(S["aT_copied"], 1)
                    act.wait_ge(S["cur_ready"], b + 1)
                    act.wait_ge(S["scattered"], 16 * b + 16)
                    for h in range(2):
                        act.wait_ge((S["o_done"], w_free[5])[h], b + 1)
                        A(osb[:, h * CH:(h + 1) * CH], ps[:, 4 + h, :], ACT.Copy, scale=gate_c[:, 0:1]).then_inc(S["o_copied"], 1)
            for t in range(TL):
                act.wait_ge(S["rt_out"], 3 * t + 1)
                A(junk3[:, :], xl[:, t, :], ACT.Square, accum_out=ss[:, t:t + 1]).then_inc(S["ssq_out"], 1)
                act.wait_ge(S["rt_out"], 3 * t + 2)
                act.wait_ge(S["ssq_out"], t + 1)
                A(rsf[:, 1, t:t + 1], rsf[:, 0, t:t + 1], ACT.Sqrt).then_inc(S["rt_out"], 1)

        @block.vector
        def _(dve):
            V = nc.vector
            steps = [0]

            def link(ins):
                steps[0] += 1
                ins.then_inc(S["dve_step"], 1)
                dve.wait_ge(S["dve_step"], steps[0])

            dve.wait_ge(S["act_step"], 1)
            for s, name in enumerate(("c", "c_ctx")):
                last = V.tensor_tensor(csil[:, :, s], col(name), sp_t[:, s, :], ALU.mult)
            last.then_inc(S["csil_ready"], 1)
            dve.wait_ge(S["csil_ready"], 1)
            link(V.tensor_scalar(sp_t[:, 0, :], col("lam"), -1.0, None, ALU.mult))
            V.tensor_tensor(sp_t[:, 1, :], sp_t[:, 0, :], col("lam"), ALU.max).then_inc(S["sp_ready"], 1)
            dve.wait_ge(S["ssq_in"], TC + TL)
            V.tensor_scalar(ss[:, :], ss[:, :], 1.0 / D, EPS, ALU.mult, ALU.add).then_inc(S["rstd_in"], 1)
            dve.wait_ge(S["rstd_in"], 2)
            link(V.reciprocal(ss[:, :], ss[:, :]))
            for t in range(TC):
                V.tensor_scalar(xs_c[:, t, :], c_in[:, t, :], ss[:, t:t + 1], None, ALU.mult).then_inc(S["xs_ready"], 1)
            for t in range(TL):
                V.tensor_scalar(xs_l[:, t, :], x_in[:, t, :], ss[:, TC + t:TC + t + 1], None, ALU.mult).then_inc(S["xs_ready"], 1)
            dve.wait_ge(S["mod_done"], 4)
            mod = ps[:, 0, 0:4 * KD].rearrange("p (m s) -> p m s", s=2)
            for s in range(2):
                V.tensor_tensor(sh[:, :, s], mod[:, 0:KD, s], col("b_shift"), ALU.add)
                link(V.tensor_tensor(sc[:, :, s], mod[:, KD:2 * KD, s], col("b_scale"), ALU.add))
                last = V.scalar_tensor_tensor(sc[:, :, s], sc[:, :, s], 1.0, col("g_mix"), ALU.add, ALU.mult)
            last.then_inc(S["film_ready"], 1)
            dve.wait_ge(S["film_ready"], 1)
            for k in range(1, KD, 2):
                dve.wait_ge(S["tl_done"], k + 1)
                V.tensor_scalar(hT_l[:, k, :], ps[:, (5 + k) % 8, :], sc[:, k, 0:1], sh[:, k, 0:1], ALU.mult, ALU.add).then_inc(S["hl_by_dve"], 1)
            dve.wait_ge(S["mm_done"], 1)
            for s in range(2):
                last = V.tensor_copy(MM[:, :, s, :], ps[:, 6 + s, :].rearrange("p (g j) -> p g j", g=GT))
            last.then_inc(S["mm_copied"], 1)
            for t in range(RT):
                dve.wait_ge(S["xr_copied"], t + 1)
                w = [pc[:, COLS["conv_w"][0] + RT * k + t:COLS["conv_w"][0] + RT * k + t + 1] for k in range(TAPS)]
                X = xp[t % 2]
                link(V.tensor_scalar(cv[:, :], X[:, 0:NX - 3], w[0], pc[:, COLS["conv_b"][0] + t:COLS["conv_b"][0] + t + 1], ALU.mult, ALU.add))
                for k in (1, 2):
                    link(V.scalar_tensor_tensor(cv[:, :], X[:, k:k + NX - 3], w[k], cv[:, :], ALU.mult, ALU.add))
                V.scalar_tensor_tensor(xc[:, t, 0:NC], X[:, 3:3 + NC], w[3], cv[:, 0:NC], ALU.mult, ALU.add)
                V.scalar_tensor_tensor(xc[:, t, NC:], X[:, 3 + LAT0:3 + LAT0 + NL], w[3], cv[:, LAT0:LAT0 + NL], ALU.mult, ALU.add
                                       ).then_inc(S["conv_done"], 1)
                dve.wait_ge(S["conv_done"], t + 1)
            dve.wait_ge(S["sp_ready"], 2)
            e_, s_, s2, q_ = sp_t[:, 2, :], sp_t[:, 3, :], sp_t[:, 4, :], sp_t[:, 5, :]
            link(V.tensor_scalar(s_, e_, 2.0, None, ALU.add))
            link(V.reciprocal(s_, s_))
            link(V.tensor_tensor(s_, s_, e_, ALU.mult))
            link(V.tensor_tensor(s2, s_, s_, ALU.mult))
            link(V.tensor_scalar(q_, s2, 1.0 / 17, None, ALU.mult))
            for k in (15, 13, 11, 9, 7, 5, 3):
                link(V.scalar_tensor_tensor(q_, q_, 1.0 / k, s2, ALU.add, ALU.mult))
            link(V.scalar_tensor_tensor(q_, q_, 1.0, s_, ALU.add, ALU.mult))
            link(V.tensor_scalar(s_, sp_t[:, 0, :], 0.0, None, ALU.max))
            link(V.scalar_tensor_tensor(q_, q_, 2.0, s_, ALU.mult, ALU.add))
            V.tensor_scalar(nsp[:, 0, :], q_, -RG_C, None, ALU.mult)
            V.tensor_scalar(nsp[:, 1, :], q_, RG_C, None, ALU.mult).then_inc(S["sp_ready"], 1)
            for g in range(GT):
                dve.wait_ge(S["f_done"], g + 1)
                if g == 0:
                    dve.wait_ge(S["tl_done"], KD)
                V.tensor_copy(fT[:, g, :], ps[:, g, :]).then_inc(S["f_copied"], 1)

            zn = [0]

            def z_chunk():
                i = zn[0]
                zn[0] += 1
                dve.wait_ge(S[f"ld_zm{i % 2}"], 16 * (i // 2 + 1))
                if i == 0:
                    dve.wait_ge(S["tl_done"], KD)
                if i >= 2:
                    dve.wait_ge(S["z_done"], i - 1)
                W, Z = wm_rest[i % 2], z_buf[i % 2]
                link(V.tensor_scalar(Z[:, :], W[:, 0, :], csil[:, 0, 0:1], None, ALU.mult))
                for k in range(1, KD):
                    ins = V.scalar_tensor_tensor(Z[:, :], W[:, k, :], csil[:, k, 0:1], Z[:, :], ALU.mult, ALU.add)
                    if k < KD - 1:
                        link(ins)
                ins.then_inc(S["z_ready"], 1)

            def z_add():
                i = zn[0] - 1
                dve.wait_ge(S["z_done"], i + 1)
                if i == 0:
                    dve.wait_ge(S["ld_bc"], 16)
                v = bc[:, i // 2, (i % 2) * CH:(i % 2 + 1) * CH]
                V.tensor_tensor(v, ps[:, z_bank(i), :], v, ALU.add).then_inc(S["bc_ready"], 1)

            def y_copy(m):
                dve.wait_ge(S["y_done"], m + 1)
                v = pair(2 + m % 2).rearrange("p (g s j) -> p g s j", g=GT, s=2)
                for s in range(2):
                    last = V.tensor_copy(Y[:, m, s, :].rearrange("p (g j) -> p g j", g=GT), v[:, :, s, :])
                last.then_inc(S["y_copied"], 1)

            def ix(d):
                for t in range(RT):
                    dve.wait_ge(S["sig_done"], 2 * (RT * d + t) + 2)
                    V.tensor_tensor(Um[:, d, t, :], Um[:, d, t, :], xc[:, t, :], ALU.mult).then_inc(S["ix_ready"], 1)

            def drive(d):
                for t in range(RT):
                    m = RT * d + t
                    dve.wait_ge(S["q_ready"], m + 1)
                    dve.wait_ge(S["th_ready"], m + 1)
                    V.scalar_tensor_tensor(Rm[:, t, :], Qm[m % 2][:, :], 1.0, Rm[:, t, :], ALU.add, ALU.mult).then_inc(S["w_ready"], 1)
                for t in range(RT):
                    m = RT * d + t
                    dve.wait_ge(S["root_ready"], m + 1)
                    V.tensor_tensor(Um[:, d, t, :], Um[:, d, t, :], Rm[:, t, :], ALU.mult).then_inc(S["ix_ready"], 1)

            def scan(d):
                for t in range(RT):
                    a, u = Am[:, d, t, :], Um[:, d, t, :]
                    if t == 0:
                        dve.wait_ge(S["ix_ready"], 2 * RT * (d + 1))
                        if d == 1:
                            dve.wait_ge(S["a_ready"], 2 * RT)
                    if d == 0:
                        link(V.tensor_tensor_scan(u[:, 0:NC], a[:, 0:NC], u[:, 0:NC], 0.0, ALU.mult, ALU.add))
                        link(V.tensor_tensor_scan(u[:, NC:], a[:, NC:], u[:, NC:], u[:, NC - 1:NC], ALU.mult, ALU.add))
                    else:
                        link(V.tensor_tensor_scan(u[:, 0:NC][:, ::-1], a[:, 0:NC][:, ::-1], u[:, 0:NC][:, ::-1], 0.0, ALU.mult, ALU.add))
                        link(V.tensor_tensor_scan(u[:, NC:][:, ::-1], a[:, NC:][:, ::-1], u[:, NC:][:, ::-1], u[:, 0:1], ALU.mult, ALU.add))

            ix(0)
            z_chunk()
            z_add()
            for m in range(TL):
                y_copy(m)
            drive(0)
            ix(1)
            z_chunk()
            scan(0)
            z_add()
            z_chunk()
            drive(1)
            z_add()
            scan(1)
            dve.wait_ge(S["gelu_done"], RT)
            for t in range(RT):
                link(V.tensor_tensor(Um[:, 0, t, NC:], Um[:, 0, t, NC:], Um[:, 1, t, NC:], ALU.add))
                V.tensor_tensor(Um[:, 0, t, NC:], Um[:, 0, t, NC:], gelu[:, t, :], ALU.mult).then_inc(S["rg_ready"], 1)
            dve.wait_ge(S["ssf_done"], 1)
            V.tensor_scalar(rsf[:, 0, :], ps[:, 0, 0:TL], 1.0 / DF, EPS, ALU.mult, ALU.add).then_inc(S["rsf_act"], 1)
            dve.wait_ge(S["rsf_act"], 2)
            V.reciprocal(rsf[:, 0, :], rsf[:, 1, :]).then_inc(S["rsf_ready"], 1)
            while zn[0] < 8:
                z_chunk()
                z_add()
            dve.wait_ge(S["bc_ready"], 8)
            dve.wait_ge(S["ld_gnf"], 16)
            V.scalar_tensor_tensor(bc[:, 2, :], bc[:, 2, :], 1.0, gnf[:, :], ALU.add, ALU.mult).then_inc(S["bc_ready"], 1)
            dve.wait_ge(S["ssr_done"], 1)
            V.tensor_scalar(rsf[:, 2, :], ps[:, 1, 0:TL], 1.0 / DR, EPS, ALU.mult, ALU.add).then_inc(S["rsf_act"], 1)
            dve.wait_ge(S["rsf_act"], 4)
            link(V.reciprocal(rsf[:, 2, :], rsf[:, 3, :]))
            dve.wait_ge(S["ld_xl"], 16)
            dve.wait_ge(S["bc_ready"], 9)
            for t in range(TL):
                dve.wait_ge(S["pr_done"], t + 1)
                dve.wait_ge(S["pf_copied"], t + 1)
                V.scalar_tensor_tensor(Fb[:, t, :], pair(1 + t % 3), rsf[:, 2, t:t + 1], Fb[:, t, :], ALU.mult, ALU.add).then_inc(S["pr_read"], 1)
                dve.wait_ge(S["pr_read"], t + 1)
                link(V.tensor_tensor(Fb[:, t, :], Fb[:, t, :], bc[:, 0, :], ALU.mult))
                V.tensor_tensor(xl[:, t, :], xl[:, t, :], Fb[:, t, :], ALU.add).then_inc(S["x2_ready"], 1)
                dve.wait_ge(S["ssq_ffn"], 2 * t + 1)
                V.tensor_scalar(rsf[:, 0, t:t + 1], ss[:, t:t + 1], 1.0 / D, EPS, ALU.mult, ALU.add).then_inc(S["ssq_ffn"], 1)
                dve.wait_ge(S["rt_ffn"], t + 1)
                link(V.reciprocal(rsf[:, 1, t:t + 1], rsf[:, 1, t:t + 1]))
                link(V.scalar_tensor_tensor(h_sb[:, t, :], xl[:, t, :], rsf[:, 1, t:t + 1], bc[:, 2, :], ALU.mult, ALU.mult))
                V.tensor_tensor(h_sb[:, t, :], h_sb[:, t, :], bc[:, 1, :], ALU.add).then_inc(S["h_ready"], 1)
            dve.wait_ge(S["ld_wr"], 32)
            dve.wait_ge(S["lg_done"], TL)
            link(V.tensor_tensor(lg[:, :, :], ps[:, 0, 0:TL * NE].rearrange("p (t e) -> p t e", t=TL),
                                 br[:, :].unsqueeze(1).to_broadcast([P, TL, NE]), ALU.add))
            for t in range(TL):
                link(V.max(m8[:, t, :], lg[:, t, :]))
                last = V.max_index(i8[:, t, :], m8[:, t, :], lg[:, t, :])
            V.tensor_scalar(rs8[:, 0:TL], m8[:, :, 0], -1.0, None, ALU.mult).then_inc(S["m8_ready"], 1)
            dve.wait_ge(S["m8_ready"], 1)
            link(V.tensor_copy(if8[:, :, :], i8[:, :, :]))
            exp_bc = const("expert").unsqueeze(1).to_broadcast([P, TL, NE])
            link(V.tensor_tensor(msk[:, :, :], exp_bc, if8[:, :, 0:1].to_broadcast([P, TL, NE]), ALU.is_equal))
            for k in range(1, TOPK):
                link(V.tensor_tensor(one[:, :, :], exp_bc, if8[:, :, k:k + 1].to_broadcast([P, TL, NE]), ALU.is_equal))
                link(V.tensor_tensor(msk[:, :, :], msk[:, :, :], one[:, :, :], ALU.add))
            V.tensor_copy(mskb[:, :, :], msk[:, :, :]).then_inc(S["mask_ready"], 1)
            dve.wait_ge(S["ex_ready"], 1)
            link(V.tensor_tensor(ex[:, :, :], ex[:, :, :], msk[:, :, :], ALU.mult))
            link(V.tensor_reduce(rs8[:, 4:4 + TL], ex[:, :, :], AX.X, ALU.add))
            link(V.reciprocal(rs8[:, 4:4 + TL], rs8[:, 4:4 + TL]))
            link(V.tensor_tensor(gts[:, :, :], ex[:, :, :], rs8[:, 4:4 + TL].unsqueeze(2).to_broadcast([P, TL, NE]), ALU.mult))
            link(V.tensor_copy(meta[:, :, :, 2], gts[:, :, :]))
            link(V.tensor_tensor(gtr[:, :, :], gts[:, :, :], meta[:, :, :, 2], ALU.subtract))
            link(V.tensor_copy(meta[:, :, :, 3], gtr[:, :, :]))
            link(V.tensor_tensor(gts[:, :, :], gtr[:, :, :], meta[:, :, :, 3], ALU.subtract))
            link(V.tensor_copy(meta[:, :, :, 4], gts[:, :, :]))
            tok = const("token").rearrange("p (t s) -> p t s", s=2).unsqueeze(2).to_broadcast([P, TL, NE, 2])
            link(V.tensor_copy(meta[:, :, :, 0:2], tok))
            dve.wait_ge(S["pos_done"], 1)
            link(V.scalar_tensor_tensor(posm[:, :, :], ps[:, 1, 0:TL * NE].rearrange("p (t e) -> p t e", t=TL), 1.0,
                                        msk[:, :, :], ALU.add, ALU.mult))
            link(V.tensor_scalar(posm[:, :, :], posm[:, :, :], -1.0, None, ALU.add))
            link(V.tensor_copy(cnt[:, :], ps[:, 2, 0:NE]))
            link(V.tensor_scalar(ovf[:, :], cnt[:, :], float(P), None, ALU.is_gt))
            for j in range(2, NL // P):
                link(V.scalar_tensor_tensor(ovf[:, :], cnt[:, :], float(P * j), ovf[:, :], ALU.is_gt, ALU.add))
            link(V.tensor_tensor_scan(end[:, :], ones[:, 0:NE], ovf[:, :], 0.0, ALU.mult, ALU.add))
            link(V.tensor_tensor(beg[:, :], end[:, :], ovf[:, :], ALU.subtract))
            q_bc = const("extra").unsqueeze(2).to_broadcast([P, NS, NE])
            link(V.tensor_tensor(mq[:, :, :], q_bc, beg[:, :].unsqueeze(1).to_broadcast([P, NS, NE]), ALU.is_ge))
            link(V.tensor_tensor(mq2[:, :, :], end[:, :].unsqueeze(1).to_broadcast([P, NS, NE]), q_bc, ALU.is_gt))
            link(V.tensor_tensor(mq[:, :, :], mq[:, :, :], mq2[:, :, :], ALU.mult))
            link(V.tensor_tensor(mq2[:, :, :], mq[:, :, :], const("expert").unsqueeze(1).to_broadcast([P, NS, NE]), ALU.mult))
            V.memset(item_e[:, NI:], 0.0)
            V.memset(item_o[:, :], 0.0)
            V.tensor_copy(item_e[:, 0:NE], const("expert"))
            link(V.tensor_reduce(item_e[:, NE:NI], mq2[:, :, :], AX.X, ALU.add))
            link(V.tensor_tensor(mq2[:, :, :], mq[:, :, :], beg[:, :].unsqueeze(1).to_broadcast([P, NS, NE]), ALU.mult))
            link(V.tensor_reduce(item_o[:, NE:NI], mq2[:, :, :], AX.X, ALU.add))
            link(V.tensor_tensor(item_o[:, NE:NI], const("extra"), item_o[:, NE:NI], ALU.subtract))
            link(V.tensor_scalar(item_o[:, NE:NI], item_o[:, NE:NI], 1.0, float(P), ALU.add, ALU.mult))
            V.tensor_copy(item_i[:, :], item_e[:, :])
            V.tensor_scalar(n_items[:, :], end[:, NE - 1:NE], float(NE), None, ALU.add).then_inc(S["table_ready"], 1)
            dve.wait_ge(S["table_ready"], 1)

            def pick_tokens(b, e):
                V.tensor_copy(metab[:, :, :], meta[:, :, bass.ds(e, 1), :].rearrange("p t e s -> p t (e s)"))
                V.scalar_tensor_tensor(sel[:, :, :], const("slot").unsqueeze(1).to_broadcast([P, TL, P]),
                                       item_o[:, bass.ds(b, 1)], posm[:, :, bass.ds(e, 1)].to_broadcast([P, TL, P]),
                                       ALU.add, ALU.is_equal).then_inc(S["sel_ready"], 1)

            def pick_expert(b):
                V.tensor_tensor(pick[:, :], const("expert_of_row").to_broadcast([P, P]),
                                item_e[:, bass.ds(b, 1)].to_broadcast([P, P]), ALU.is_equal).then_inc(S["pick_ready"], 1)

            def numbers(v):
                dve.wait_ge(S["meta_done"], v)
                V.tensor_copy(msb[:, :], ps[:, 7, 0:5]).then_inc(S["gate_free"], 1)
                dve.wait_ge(S["gate_free"], v)
                V.tensor_reduce(gate_n[:, :], msb[:, 2:5], AX.X, ALU.add)
                V.scalar_tensor_tensor(idx_n[:, :], msb[:, 0:1], float(OUT_OF_RANGE), msb[:, 1:2], ALU.add, ALU.add).then_inc(S["idx_ready"], 1)

            pick_tokens(0, 0)
            pick_expert(0)
            numbers(1)

            def swiglu(j, b):
                dve.wait_ge(w_free[2 * j + 1], b + 1)
                V.tensor_scalar(gb[:, :], ps[:, 2 * j, :], LIMIT, None, ALU.min).then_inc(S["g_ready"], 1)
                V.tensor_scalar(ub[:, :], ps[:, 2 * j + 1, :], LIMIT, -LIMIT, ALU.min, ALU.max).then_inc(S["dve_u"], 1)
                dve.wait_ge(S["g_ready"], 2 * b + 1 + j)
                dve.wait_ge(S["dve_u"], 4 * b + 2 * j + 1)
                V.scalar_tensor_tensor(ub[:, :], ub[:, :], 1.0, gb[:, :], ALU.add, ALU.mult).then_inc(S["dve_u"], 1)
                dve.wait_ge(S["dve_u"], 4 * b + 2 * j + 2)
                dve.wait_ge(S["s_sig"], 2 * b + 1 + j)
                V.tensor_tensor(ab[:, :], ub[:, :], sg[:, :], ALU.mult).then_inc(S["act_ready"], 1)

            n = dve.value_load(n_items[0:1, 0:1], min_val=NE, max_val=NI)
            with dve.Fori(0, NI) as b:
                with dve.If(b < n):
                    e = dve.value_load(item_i[0:1, bass.ds(b + 1, 1)], min_val=0, max_val=NE - 1)
                    dve.wait_ge(S["meta_done"], b + 1)
                    pick_tokens(b + 1, e)
                    swiglu(0, b)
                    dve.wait_ge(S["scattered"], 16 * b + 16)
                    dve.wait_ge(S["o_copied"], 2 * b + 2)
                    V.tensor_copy(idx_c[:, :], idx_n[:, :])
                    V.tensor_copy(gate_c[:, :], gate_n[:, :]).then_inc(S["cur_ready"], 1)
                    dve.wait_ge(S["cur_ready"], b + 1)
                    dve.wait_ge(S["gathered"], 16 * b + 16)
                    numbers(b + 2)
                    swiglu(1, b)
                    dve.wait_ge(S["bias_used"], b + 1)
                    pick_expert(b + 1)
            dve.wait_ge(S["ld_gfin"], 16)
            for t in range(TL):
                dve.wait_ge(S["y_loaded"], 16 * (t + 1))
                link(V.tensor_tensor(y_sb[:, t, :], y_sb[:, t, :], bc[:, 3, :], ALU.mult))
                V.tensor_tensor(xl[:, t, :], xl[:, t, :], y_sb[:, t, :], ALU.add).then_inc(S["rt_out"], 1)
                dve.wait_ge(S["ssq_out"], t + 1)
                V.tensor_scalar(rsf[:, 0, t:t + 1], ss[:, t:t + 1], 1.0 / D, EPS, ALU.mult, ALU.add).then_inc(S["rt_out"], 1)
                dve.wait_ge(S["rt_out"], 3 * t + 3)
                link(V.reciprocal(rsf[:, 1, t:t + 1], rsf[:, 1, t:t + 1]))
                V.scalar_tensor_tensor(o_sb[:, t, :], xl[:, t, :], rsf[:, 1, t:t + 1], gfin[:, :], ALU.mult, ALU.mult).then_inc(S["out_ready"], 1)

        @block.tensor
        def _(pe):
            MMUL = nc.tensor.matmul
            pe.wait_ge(S["ld_cst"], 16)
            pe.wait_ge(S["csil_ready"], 1)
            for q in range(4):
                pe.wait_ge(S[f"ld_wm{q}"], 16)
                for m in range(4):
                    c0 = 2 * (4 * q + m)
                    for k in range(KD):
                        last = MMUL(ps[:, 0, c0:c0 + 2], wm_first[q][:, k, m * P:(m + 1) * P], csil[:, k, :],
                                    start=(k == 0), stop=(k == KD - 1))
                last.then_inc(S["mod_done"], 1)
            pe.wait_ge(S["xs_ready"], TC)
            for k in range(KD):
                for t in range(TC):
                    last = nc.tensor.transpose(ps[:, 1 + k // 2, (k % 2) * NC + t * P:(k % 2) * NC + (t + 1) * P],
                                               xs_c[:, t, k * P:(k + 1) * P], ident)
                if k % 2:
                    last.then_inc(S["tc_done"], 1)
            pe.wait_ge(S["xs_ready"], TC + TL)
            for k in range(KD):
                if k == 3:
                    pe.wait_ge(S["film_ready"], 1)
                if k > 3:
                    pe.wait_ge(S["hc_copied"], k - 3)
                for t in range(TL):
                    last = nc.tensor.transpose(ps[:, (5 + k) % 8, t * P:(t + 1) * P], xs_l[:, t, k * P:(k + 1) * P], ident)
                last.then_inc(S["tl_done"], 1)
            pe.wait_ge(S["ld_wf"], 16)
            pe.wait_ge(S["hl_by_dve"], 1)
            pe.wait_ge(S["hl_by_act"], 2)
            for s, name in enumerate(("cd", "neg_sd")):
                last = MMUL(ps[:, 6 + s, :], const(name), wf[:, :, :].rearrange("p g j -> p (g j)"), start=True, stop=True)
            last.then_inc(S["mm_done"], 1)
            pe.wait_ge(S["hl_by_act"], KD // 2)
            pe.wait_ge(S["hl_by_dve"], KD // 2)
            pe.wait_ge(S["hc_copied"], 4)
            pe.wait_ge(S["ld_win1"], 16)
            for t in range(RT):
                if t >= 2:
                    pe.wait_ge(S["xr_copied"], t - 1)
                for k in range(KD):
                    MMUL(ps[:, t % 2, 0:NC], win[1][:, k, t * P:(t + 1) * P], hT_c[:, k, :], start=(k == 0), stop=(k == KD - 1))
                for k in range(KD):
                    last = MMUL(ps[:, 2 + t % 2, :], win[1][:, k, t * P:(t + 1) * P], hT_l[:, k, :], start=(k == 0), stop=(k == KD - 1))
                last.then_inc(S["xr_done"], 1)
            pe.wait_ge(S["ld_win2"], 16)
            pe.wait_ge(S["mm_copied"], 1)
            for t in range(RT):
                for k in range(KD):
                    last = MMUL(ps[:, 4 + t, :], win[2][:, k, t * P:(t + 1) * P], hT_l[:, k, :], start=(k == 0), stop=(k == KD - 1))
                last.then_inc(S["gr_done"], 1)
            pe.wait_ge(S["ld_win0"], 16)
            pe.wait_ge(S["xr_copied"], RT)
            for g in range(GT):
                for k in range(KD):
                    last = MMUL(ps[:, g, :], win[0][:, k, g * P:(g + 1) * P], hT_l[:, k, :], start=(k == 0), stop=(k == KD - 1))
                last.then_inc(S["f_done"], 1)

            def gates(d):
                for t in range(RT):
                    for a in range(2):
                        n = 2 * (RT * d + t) + a
                        if n == 0:
                            pe.wait_ge(S["ld_wbd"], 64)
                            pe.wait_ge(S["conv_done"], RT)
                            pe.wait_ge(S["f_copied"], GT)
                        if n >= 2:
                            pe.wait_ge(S["sig_done"], n - 1)
                        v = pair(n % 2)
                        MMUL(v[:, NC:2 * NC], wbd[:, a, RT * d + t, :], xc[:, t, 0:NC], start=True, stop=True)
                        MMUL(v[:, 2 * NC:], wbd[:, a, RT * d + t, :], xc[:, t, NC:], start=True, stop=True).then_inc(S["gate_mm"], 1)

            zc = [0]

            def z_sum():
                i = zc[0]
                zc[0] += 1
                pe.wait_ge(S["z_ready"], i + 1)
                if i >= 2:
                    pe.wait_ge(S["bc_ready"], i - 1)
                MMUL(ps[:, z_bank(i), :], ones, z_buf[i % 2][:, :], start=True, stop=True).then_inc(S["z_done"], 1)

            gates(0)
            pe.wait_ge(S["gelu_done"], RT)
            z_sum()
            pe.wait_ge(S["bc_ready"], 1)
            for m in range(TL):
                if m >= 2:
                    pe.wait_ge(S["y_copied"], m - 1)
                for g in range(GT):
                    last = MMUL(pair(2 + m % 2)[:, g * 2 * P:(g + 1) * 2 * P], fT[:, g, m * P:(m + 1) * P],
                                MM[:, g, :, :].rearrange("p s j -> p (s j)"), start=True, stop=True)
                last.then_inc(S["y_done"], 1)
            gates(1)
            pe.wait_ge(S["y_copied"], TL)
            pe.wait_ge(S["ld_dft"], 32)
            for g in range(GT):
                for m in range(TL):
                    for s in range(2):
                        last = MMUL(ps[:, 4 + g, :], Y[:, m, s, g * P:(g + 1) * P], dft_sb[:, s, m, :],
                                    start=(m == 0 and s == 0), stop=(m == TL - 1 and s == 1))
                last.then_inc(S["dft_done"], 1)
                if g < 2:
                    pe.wait_ge(S["sig_done"], 4 * RT)
                    z_sum()
            pe.wait_ge(S["cf_copied"], GT)
            pe.wait_ge(S["sig_done"], 4 * RT)
            for t in range(TL):
                for g in range(GT):
                    last = MMUL(ps[:, 0, t:t + 1], sqF[:, g, t * P:(t + 1) * P], ones[:, 0:1], start=(g == 0), stop=(g == GT - 1))
            last.then_inc(S["ssf_done"], 1)
            while zc[0] < 8:
                z_sum()
            pe.wait_ge(S["bc_ready"], 8)
            pe.wait_ge(S["ld_wo0"], 16)
            for t in range(TL):
                if t >= 3:
                    pe.wait_ge(S["pf_copied"], t - 2)
                for n in range(2):
                    for k in range(GT):
                        last = MMUL(ps[:, 2 * (1 + t % 3) + n, :], catF[:, k, t * P:(t + 1) * P], wo[0][:, k, n * CH:(n + 1) * CH],
                                    start=(k == 0), stop=(k == GT - 1))
                last.then_inc(S["pf_done"], 1)
            pe.wait_ge(S["sqr_ready"], RT)
            for t in range(TL):
                for g in range(RT):
                    last = MMUL(ps[:, 1, t:t + 1], Um[:, 1, g, NC + t * P:NC + (t + 1) * P], ones[:, 0:1], start=(g == 0), stop=(g == RT - 1))
            last.then_inc(S["ssr_done"], 1)
            pe.wait_ge(S["ld_wo1"], 16)
            pe.wait_ge(S["pf_copied"], TL)
            for t in range(TL):
                if t >= 3:
                    pe.wait_ge(S["pr_read"], t - 2)
                for n in range(2):
                    for k in range(RT):
                        last = MMUL(ps[:, 2 * (1 + t % 3) + n, :], Um[:, 0, k, NC + t * P:NC + (t + 1) * P], wo[1][:, k, n * CH:(n + 1) * CH],
                                    start=(k == 0), stop=(k == RT - 1))
                last.then_inc(S["pr_done"], 1)
            pe.wait_ge(S["ld_wr"], 32)
            for t in range(TL):
                pe.wait_ge(S["h_ready"], t + 1)
                if t == 0:
                    pe.wait_ge(S["pr_read"], TL)
                if t >= 2:
                    pe.wait_ge(S["ht_copied"], t - 1)
                for k in range(KD):
                    last = nc.tensor.transpose(pair(1 + t % 2)[:, k * P:(k + 1) * P], h_sb[:, t, k * P:(k + 1) * P], ident)
                    if k % 4 == 3:
                        last.then_inc(S["ht_done"], 1)
                pe.wait_ge(S["ht_copied"], t + 1)
                for k in range(KD):
                    last = MMUL(ps[:, 0, t * NE:(t + 1) * NE], hT2[:, k, :], wr[:, k, :], start=(k == 0), stop=(k == KD - 1))
                last.then_inc(S["lg_done"], 1)
            pe.wait_ge(S["bf_ready"], 1)
            pe.wait_ge(S["mask_ready"], 1)
            for t in range(TL):
                for u in range(t):
                    MMUL(ps[:, 1, t * NE:(t + 1) * NE], onesb[:, :], mskb[:, u, :], start=(u == 0), stop=False)
                MMUL(ps[:, 1, t * NE:(t + 1) * NE], beforeb[:, :], mskb[:, t, :], start=(t == 0), stop=True)
            for t in range(TL):
                last = MMUL(ps[:, 2, 0:NE], onesb[:, :], mskb[:, t, :], start=(t == 0), stop=(t == TL - 1))
            last.then_inc(S["pos_done"], 1)

            def slots_meta(v):
                pe.wait_ge(S["sel_ready"], v)
                for t in range(TL):
                    last = MMUL(ps[:, 7, 0:5], sel[:, t, :], metab[:, t, :], start=(t == 0), stop=(t == TL - 1))
                last.then_inc(S["meta_done"], 1)

            def rows_to_channels(v):
                pe.wait_ge(S["gathered"], v)
                for k in range(KD):
                    last = nc.tensor.transpose(ps[:, k // 4, (k % 4) * P:(k % 4 + 1) * P], xg[:, k * P:(k + 1) * P], ident)
                    if k % 4 == 3:
                        last.then_inc(S["xt_done"], 1)

            slots_meta(1)
            rows_to_channels(16)
            pe.wait_ge(S["bias_ready"], 1)

            def bias(bank, n0):
                MMUL(ps[:, bank, :], pick[:, :], bias_w[:, n0:n0 + CH], start=True, stop=False)

            def gate_up(j, b):
                bias(2 * j, j * CH)
                bias(2 * j + 1, FF + j * CH)
                for s in range(2):
                    c = 2 * j + s
                    pe.wait_ge(w_ld[c], 16 * b + 16)
                    W = chunk_dst(c)
                    for k in range(KD):
                        last = MMUL(ps[:, c, :], xT[:, k, :], W[:, k, :], start=False, stop=(k == KD - 1))
                    last.then_inc(w_free[c], 1)

            n = pe.value_load(n_items[0:1, 0:1], min_val=NE, max_val=NI)
            with pe.Fori(0, NI) as b:
                with pe.If(b < n):
                    pe.wait_ge(S["xT_copied"], 2 * b + 2)
                    pe.wait_ge(S["pick_ready"], b + 1)
                    gate_up(0, b)
                    pe.wait_ge(S["gate_free"], b + 1)
                    slots_meta(b + 2)
                    gate_up(1, b)

                    def act_to_channels(j):
                        pe.wait_ge(S["act_ready"], 2 * b + 1 + j)
                        for k in range(4):
                            last = nc.tensor.transpose(ps[:, 6, k * P:(k + 1) * P], ab[:, k * P:(k + 1) * P], ident)
                        last.then_inc(S["at_done"], 1)

                    def down(j):
                        pe.wait_ge(w_ld[4 + j], 16 * b + 16)
                        pe.wait_ge(S["aT_copied"], 2 * b + 1 + j)
                        W = chunk_dst(4 + j)
                        for m in range(2):
                            for k in range(4):
                                last = MMUL(ps[:, 4 + m, :], aT[:, 4 * j + k, :], W[:, k, m * CH:(m + 1) * CH],
                                            start=False, stop=(j == 1 and k == 3))
                            if j == 1 and m == 0:
                                last.then_inc(S["o_done"], 1)
                        last.then_inc(w_free[4 + j], 1)

                    act_to_channels(0)
                    pe.wait_ge(S["o_copied"], 2 * b + 2)
                    for m in range(2):
                        last = MMUL(ps[:, 4 + m, :], pick[:, :], bias_w[:, 2 * FF + m * CH:2 * FF + (m + 1) * CH], start=True, stop=False)
                    last.then_inc(S["bias_used"], 1)
                    down(0)
                    rows_to_channels(16 * b + 32)
                    act_to_channels(1)
                    down(1)


_PERM = serpentine_order()


def kernel(x, c, ctx, c_ctx, w_mod, b_mod, g_norm_mix, g_norm_ffn, w_in, w_fourier, conv_w,
           conv_b, rg_w_a, rg_b_a, rg_w_x, rg_b_x, rg_lam, g_out_fourier, g_out_rg, w_out,
           w_router, b_router, w_gate_up, b_gate_up, w_down, b_down, g_final):
    import concourse.bacc as bacc
    from concourse.bass_utils import run_bass_kernel_spmd

    a = lambda t: np.ascontiguousarray(np.asarray(t))
    tiles = lambda v: np.asarray(v).reshape(-1, P).T
    bm = np.asarray(b_mod)[0]
    cols = {"c": tiles(c), "c_ctx": tiles(c_ctx), "g_mix": tiles(g_norm_mix), "b_shift": tiles(bm[:D]),
            "b_scale": tiles(bm[D:2 * D]), "conv_w": tiles(conv_w), "conv_b": tiles(conv_b), "b_a": tiles(rg_b_a),
            "b_x": tiles(rg_b_x), "lam": tiles(rg_lam), "g_f": tiles(g_out_fourier), "g_r": tiles(g_out_rg)}
    cst, dft = constants()
    arrays = {
        "x": a(np.asarray(x)[0][_PERM]), "ctx": a(ctx)[0], "w_mod": a(w_mod)[0], "b_mod": a(bm), "w_in": a(w_in)[0],
        "w_fourier": a(w_fourier)[0], "rg_w_a": a(rg_w_a)[0], "rg_w_x": a(rg_w_x)[0], "w_out": a(w_out)[0],
        "w_router": a(w_router)[0], "b_router": a(b_router)[0], "w_gate_up": a(w_gate_up)[0],
        "b_gate_up": a(b_gate_up)[0], "w_down": a(w_down)[0], "b_down": a(b_down)[0],
        "g_norm_ffn": a(g_norm_ffn)[0], "g_final": a(g_final),
        "cols": a(np.concatenate([cols[k] for k in COLS], axis=1)), "cst": cst, "dft": dft,
    }
    nc = bacc.Bacc("TRN2", target_bir_lowering=False, num_devices=1)
    args = [nc.dram_tensor(f"in_{k}", v.shape, mybir.dt.from_np(v.dtype), kind="ExternalInput").ap()
            for k, v in arrays.items()]
    out = nc.dram_tensor("out_rows", (NL, D), F32, kind="ExternalOutput").ap()
    build(nc, *args, out)
    r = run_bass_kernel_spmd(nc, [{f"in_{k}": v for k, v in arrays.items()}], core_ids=[0])
    got = np.empty((1, NL, D), np.float32)
    got[0, _PERM] = r.results[0]["out_rows"]
    return got
```

```python
import numpy as np
import concourse.bass as bass
from concourse import mybir
from contextlib import ExitStack

F32 = mybir.dt.float32
F32R = mybir.dt.float32r
BF16 = mybir.dt.bfloat16
I32 = mybir.dt.int32
U32 = mybir.dt.uint32
ALU = mybir.AluOpType
ACT = mybir.ActivationFunctionType
AX = mybir.AxisListType

P = 128
D = 1024
KD = D // P
NL, NC = 512, 256
TL, TC = NL // P, NC // P
DF = 512
DR = 512
GT = DF // P
RT = DR // P
GRID_W = 64
TAPS, PAD_LO = 4, 2
NE, TOPK = 32, 4
FF = 1024
CH = 512
EPS = 1e-6
LIMIT, ALPHA = 7.0, 1.702
RG_C = 8.0
NS = NL * TOPK // P
NI = NE + NS
PIECE = 1024
NPC = 6 * 8 * CH // PIECE
PPC = 8 * CH // PIECE
RS = 4
BY_POOL = (5, 11, 17, 23)
LO_POOL = len(BY_POOL)
LO_DVE = NPC - LO_POOL


def lo_count(i):
    pool = i in BY_POOL
    return pool, sum((j in BY_POOL) == pool for j in range(i + 1))
OUT_OF_RANGE = 4096
KB = 1024

COLS = {}
_at = 0
for _name, _n in (("c", KD), ("c_ctx", KD), ("g_mix", KD), ("b_shift", KD), ("b_scale", KD),
                  ("conv_w", TAPS * RT), ("conv_b", RT), ("b_a", 2 * RT), ("b_x", 2 * RT),
                  ("lam", 2 * RT), ("g_f", GT), ("g_r", RT)):
    COLS[_name] = (_at, _at + _n)
    _at += _n
NCOL = _at

CST = {}
_at = 0
for _name, _n in (("ident", P), ("cd", P), ("neg_sd", P), ("ones", P), ("slot", P), ("before", P),
                  ("expert", NE), ("expert_of_row", 1), ("token", 2 * TL)):
    CST[_name] = (_at, _at + _n)
    _at += _n
NCST = _at


def serpentine_order():
    t = np.arange(NL).reshape(NL // GRID_W, GRID_W)
    t[1::2] = t[1::2, ::-1]
    return t.reshape(-1)


def constants():
    p = np.arange(P)
    c = np.zeros((P, NCST), np.float32)

    def put(name, a):
        c[:, CST[name][0]:CST[name][1]] = a

    put("ident", np.eye(P))
    ang = 2 * np.pi * ((p[:, None] * p[None]) % P) / P
    put("cd", np.cos(ang) / np.sqrt(P))
    put("neg_sd", -np.sin(ang) / np.sqrt(P))
    put("ones", 1.0)
    put("slot", p[None])
    put("before", (p[:, None] < p[None]).astype(np.float32))
    put("expert", np.arange(NE)[None])
    put("expert_of_row", (p % NE)[:, None])
    put("token", np.stack([np.tile(p[:, None], (1, TL)), np.tile(P * np.arange(TL) - OUT_OF_RANGE, (P, 1))], 2).reshape(P, 2 * TL))
    n = serpentine_order()
    ang = 2 * np.pi * ((n[:, None] * n[None]) % NL) / NL
    dft = np.stack([np.cos(ang), np.sin(ang)]) / np.sqrt(NL)
    return c, dft.astype(np.float32)


def build(nc, x, ctx, w_mod, b_mod, w_in, w_fourier, rg_w_a, rg_w_x, w_out, w_router, b_router,
          w_gate_up, b_gate_up, w_down, b_down, g_norm_ffn, g_final, cols, cst, dft, out):
    h_dram = nc.dram_tensor("h_rows", (NL, D), F32, kind="Internal").ap()
    y_dram = nc.dram_tensor("y_rows", (NL, D), F32, kind="Internal").ap()

    with ExitStack() as stack:
        base = 16512
        RING = base
        SLOT = [RING + 16 * KB * i for i in range(6)]
        ZA = RING + 96 * KB
        ZB = ZA + 24 * KB
        ZD = ZB + 22 * KB
        ZX = ZD + 32 * KB
        SM = ZX + 16 * KB
        STAGE_LAST = 229344 - 4 * KB

        def at(name, shape, off, dt=F32):
            return nc.alloc_sbuf_tensor_at(name, shape, dt, offset=off)

        small_at = [SM]

        def small(name, shape, dt=F32):
            n = int(np.prod(shape[1:])) * mybir.dt.size(dt)
            t = at(name, shape, small_at[0], dt)
            small_at[0] += -(-n // 32) * 32
            assert small_at[0] <= STAGE_LAST, name
            return t

        ps = stack.enter_context(nc.psum_tensor("ps", [P, 8, 512], F32))

        def sem(name):
            return stack.enter_context(nc.semaphore(name))

        wm_first = [at("wm_0", [P, KD, CH], ZD), at("wm_1", [P, KD, CH], ZD + 16 * KB),
                    at("wm_2", [P, KD, CH], SLOT[3]), at("wm_3", [P, KD, CH], SLOT[4])]
        wm_rest = [at("wm_a", [P, KD, CH], ZD), at("wm_b", [P, KD, CH], ZD + 16 * KB)]
        x_in = at("x_in", [P, TL, D], ZX)
        c_in = at("c_in", [P, TC, D], ZB)
        xs_c = at("xs_c", [P, TC, D], ZB + 8 * KB)
        junk = at("junk", [P, D], ZB + 16 * KB)
        wf = at("wf", [P, GT, P], ZB + 20 * KB)
        xs_l = at("xs_l", [P, TL, D], SLOT[5])
        win = [at(f"win_{i}", [P, KD, CH], SLOT[i]) for i in range(3)]
        hT_l = at("hT_l", [P, KD, NL], ZA)
        hT_c = at("hT_c", [P, KD, NC], ZA + 16 * KB)
        z_buf = [at(f"z_{i}", [P, CH], SLOT[5] + (8 + 2 * i) * KB) for i in range(2)]
        gnf = at("gnf", [P, D], SLOT[5] + 12 * KB)
        bc = at("bc", [P, 4, D], ZX)
        fT = at("fT", [P, GT, NL], SLOT[5])
        dft_sb = at("dft_sb", [P, 2, TL, NL], SLOT[4])
        Y = at("Y", [P, TL, 2, DF], ZA)
        catF = at("catF", [P, GT, NL], SLOT[5])
        NX = PAD_LO + NC + 1 + PAD_LO + NL + 1
        LAT0 = NC + 3
        xp = [at(f"xp_{i}", [P, NX], ZB + 3200 * i) for i in range(2)]
        cv = at("cv", [P, NX - 3], ZB + 6400)
        NB = NC + NL
        xc = at("xc", [P, RT, NB], ZB + 9600)
        gelu = at("gelu", [P, RT, NL], ZA + 16 * KB)
        Am = at("Am", [P, 2, RT, NB], SLOT[0])
        Um = at("Um", [P, 2, RT, NB], SLOT[1] + 8 * KB)
        Rm = at("Rm", [P, RT, NB], SLOT[3])
        Qm = [at(f"Qm_{i}", [P, NB], ZB + 3200 * i) for i in range(2)]
        sqF = at("sqF", [P, GT, NL], ZB + 9600)
        wo = [at("wo_f", [P, GT, D], ZD), at("wo_r", [P, RT, D], ZD + 16 * KB)]
        xl = at("xl", [P, TL, D], ZA)
        Fb = at("Fb", [P, TL, D], SLOT[4])
        h_sb = at("h_sb", [P, TL, D], SLOT[3])
        hT2 = at("hT2", [P, KD, P], SLOT[5])
        junk2 = at("junk2", [P, D], ZA + 16 * KB)
        RA = ZB
        lg = at("lg", [P, TL, NE], RA)
        ex = at("ex", [P, TL, NE], RA + 512)
        one = at("one", [P, TL, NE], RA + 1024)
        msk = at("msk", [P, TL, NE], RA + 1536)
        gts = at("gts", [P, TL, NE], RA + 2048)
        gtr = at("gtr", [P, TL, NE], RA + 2560)
        mskb = at("mskb", [P, TL, NE], RA + 3072, BF16)
        gtb = at("gtb", [P, TL, NE], RA + 3328, BF16)
        m8 = at("m8", [P, TL, 8], RA + 3584)
        i8 = at("i8", [P, TL, 8], RA + 3712, U32)
        if8 = at("if8", [P, TL, 8], RA + 3840)
        cnt = at("cnt", [P, NE], RA + 3968)
        ovf = at("ovf", [P, NE], RA + 4096)
        end = at("end", [P, NE], RA + 4224)
        beg = at("beg", [P, NE], RA + 4352)
        rs8 = at("rs8", [P, 8], RA + 4480)
        mq = at("mq", [P, NI, NE], RA + 4608)
        slots = [at(f"slot_{i}", [P, 8 * CH], SLOT[i]) for i in range(6)]
        xg = at("xg", [P, D], ZB + 16 * KB)
        bias_raw = at("bias_raw", [2 * NE, 3 * D], ZD)
        bias_w = at("bias_w", [P, 3 * D], ZD + 12 * KB, F32R)
        gfin = at("gfin", [P, D], SLOT[3])
        osb = at("osb", [P, D], ZD + 28 * KB)
        gb = at("gb", [P, CH], ZD)
        ub = at("ub", [P, CH], ZD + 2 * KB)
        sg = at("sg", [P, CH], ZD + 4 * KB)
        ab = at("ab", [P, CH], ZD + 6 * KB)
        aT = [at("aT_hi", [P, 8, P], ZD + 8 * KB, F32R), at("aT_lo", [P, 8, P], ZD + 24 * KB, F32R)]
        xT = [at("xT_hi", [P, KD, P], ZX, F32R), at("xT_lo", [P, KD, P], ZX + 4 * KB, F32R)]
        stage_at = [ZB, ZB + 4 * KB, ZB + 8 * KB, ZB + 12 * KB, ZA + 16 * KB, ZA + 20 * KB, ZX + 8 * KB, STAGE_LAST]
        w_hi = [at(f"w_hi_{i}", [P, PIECE], stage_at[2 * i], F32R) for i in range(RS)]
        w_lo = [at(f"w_lo_{i}", [P, PIECE], stage_at[2 * i + 1], F32R) for i in range(RS)]
        y_sb = at("y_sb", [P, TL, D], SLOT[0])
        o_sb = at("o_sb", [P, TL, D], SLOT[1])
        junk3 = at("junk3", [P, D], SLOT[2])
        zero = at("zero", [P, D], ZA + 20 * KB)

        wbd_at = small_at[0]
        wbd = small("wbd", [P, 2, 2 * RT, P])
        csb = small("csb", [P, NCST])
        pc = small("pc", [P, NCOL])
        MM = at("MM", [P, GT, 2, P], SLOT[5] + 12 * KB)
        csil = small("csil", [P, KD, 2])
        sh = small("sh", [P, KD, 2])
        sc = small("sc", [P, KD, 2])
        ss = small("ss", [P, 6])
        nsp = small("nsp", [P, 3, 2 * RT])
        sp_t = small("sp_t", [P, 6, 2 * RT])
        rsf = small("rsf", [P, 4, TL])
        wr = small("wr", [P, KD, NE])
        br = small("br", [P, NE])
        beforeb = small("beforeb", [P, P], BF16)
        onesb = small("onesb", [P, P], BF16)
        small_at[0], keep = wbd_at, small_at[0]
        posm = small("posm", [P, TL, NE])
        meta = small("meta", [P, TL, NE, 5], BF16)
        item_e = small("item_e", [P, NI + 1])
        item_o = small("item_o", [P, NI + 1])
        item_i = small("item_i", [P, NI + 1], I32)
        before_i = small("before_i", [P, NE], I32)
        n_items = small("n_items", [P, 1], I32)
        sel = small("sel", [P, TL, P], BF16)
        metab = small("metab", [P, TL, 5], BF16)
        pick = small("pick", [P, P], F32R)
        msb = small("msb", [P, 5])
        idx_n = small("idx_n", [P, 1], I32)
        idx_c = small("idx_c", [P, 1], I32)
        gate_n = small("gate_n", [P, 1])
        gate_c = small("gate_c", [P, 1])
        assert small_at[0] <= wbd_at + 8 * KB
        small_at[0] = keep

        def col(name):
            a, b = COLS[name]
            return pc[:, a:b]

        def const(name):
            a, b = CST[name]
            return csb[:, a:b]

        ident, ones = const("ident"), const("ones")
        item_no = const("slot")[:, 0:NI]

        wm_v = w_mod.rearrange("(k p) n -> p k n", p=P)
        win_v = w_in.rearrange("(k p) n -> p k n", p=P)
        wo_v = w_out.rearrange("(k p) n -> p k n", p=P)
        wgu_v = w_gate_up.rearrange("e (k p) n -> e p k n", p=P)
        wd_v = w_down.rearrange("e (k p) n -> e p k n", p=P)
        rows = lambda a: a.rearrange("(t p) d -> p t d", p=P)

        names = """ld_cols ld_cst ld_wf ld_ctx ld_x ld_wm0 ld_wm1 ld_wm2 ld_wm3 ld_win0 ld_win1 ld_win2
            ld_wbd ld_zm0 ld_zm1 ld_dft ld_bc ld_gnf ld_wo0 ld_wo1 ld_xl ld_wr ld_bias ld_gfin
            dve_step act_step pool_step
            csil_ready mod_done film_ready edges_zero wbd_zero bf_ready rstd_in ssq_in xs_ready tc_done tl_done
            hc_copied hl_by_act hl_by_dve mm_done mm_copied xr_done xr_copied conv_done gr_done gelu_done
            f_done f_copied gate_mm sig_done z_ready z_done bc_ready y_done y_copied dft_done cf_copied
            ssf_done sp_ready ix_ready a_ready th_ready q_ready w_ready root_ready rg_ready sqr_ready
            ssr_done rsf_act rsf_ready pf_done pf_copied pr_done pr_read x2_ready ssq_ffn rt_ffn h_ready h_stored
            ht_done ht_copied lg_done m8_ready ex_ready mask_ready pos_done table_ready y_zero
            bias_ready gate_free xg_zero dve_u hi_ready lo_by_dve lo_by_pool piece_used
            meta_done at_done xt_done bias_used g_ready act_ready sel_ready idx_ready
            cur_ready pick_ready s_sig aT_hi_ready aT_lo_ready xT_hi_ready xT_lo_ready o_copied gathered scattered
            y_loaded ssq_out rt_out out_ready stored"""
        S = {n: sem(n) for n in names.split()}
        w_ld = [sem(f"w_loaded_{c}") for c in range(6)]

        def chunk_src(c, e):
            if c < 4:
                n0 = (c % 2) * FF + (c // 2) * CH
                return wgu_v[e, :, :, n0:n0 + CH]
            return wd_v[e, :, (c - 4) * 4:(c - 3) * 4, :]

        def chunk_dst(c):
            return slots[c][:, :].rearrange("p (k n) -> p k n", k=8 if c < 4 else 4)

        def raw_piece(i):
            q = i % PPC
            return slots[i // PPC][:, q * PIECE:(q + 1) * PIECE]

        def pair(i):
            return ps[:, 2 * i:2 * i + 2, :].rearrange("p b n -> p (b n)")

        def z_bank(i):
            return 4 if i == 0 else 2 + i % 2

        block = stack.enter_context(nc.Block())

        @block.sync
        def _(sp):
            def load(dst, src, name, n=16):
                sp.dma_start(dst, src).then_inc(S[name], 16)

            load(pc[:, :], cols, "ld_cols")
            load(csb[:, :], cst, "ld_cst")
            load(wm_first[0][:, :, :], wm_v[:, :, 0:CH], "ld_wm0")
            load(c_in[:, :, :], rows(ctx), "ld_ctx")
            load(wm_first[1][:, :, :], wm_v[:, :, CH:2 * CH], "ld_wm1")
            load(wm_first[2][:, :, :], wm_v[:, :, 2 * CH:3 * CH], "ld_wm2")
            load(wm_first[3][:, :, :], wm_v[:, :, 3 * CH:4 * CH], "ld_wm3")
            load(x_in[:, :, :], rows(x), "ld_x")
            load(wf[:, :, :], w_fourier.rearrange("g i j -> i g j"), "ld_wf")
            for i in (1, 2, 0):
                load(win[i][:, :, :], win_v[:, :, i * CH:(i + 1) * CH], f"ld_win{i}")
            sp.wait_ge(S["wbd_zero"], 1)
            for a, w in enumerate((rg_w_a, rg_w_x)):
                v = w.rearrange("d (t s) i j -> s i (d t) j", s=2)
                for s in range(2):
                    load(wbd[64 * s:64 * s + 64, a, :, 64 * s:64 * s + 64], v[s], "ld_wbd")
            load(wr[:, :, :], w_router.rearrange("(k p) e -> p k e", p=P), "ld_wr")
            load(br[:, :], b_router.partition_broadcast(P), "ld_wr")
            for i in range(8):
                if i < 2:
                    sp.wait_ge(S["mod_done"], i + 1)
                else:
                    sp.wait_ge(S["z_ready"], i - 1)
                load(wm_rest[i % 2][:, :, :], wm_v[:, :, (4 + i) * CH:(5 + i) * CH], f"ld_zm{i % 2}")
                if i == 0:
                    sp.wait_ge(S["xs_ready"], 6)
                    load(bc[:, :, :].rearrange("p a d -> p (a d)"), b_mod[2 * D:6 * D].partition_broadcast(P), "ld_bc")
                if i == 1:
                    sp.wait_ge(S["mod_done"], 4)
                    load(dft_sb[:, 0, :, :], dft[0].rearrange("(m p) n -> p m n", p=P), "ld_dft")
                    load(dft_sb[:, 1, :, :], dft[1].rearrange("(m p) n -> p m n", p=P), "ld_dft")
            sp.wait_ge(S["y_done"], TL)
            load(gnf[:, :], g_norm_ffn.partition_broadcast(P), "ld_gnf")
            for i in range(2):
                sp.wait_ge(S["z_ready"], 7 + i)
                load(wo[i][:, :, :], wo_v[:, 4 * i:4 * i + 4, :], f"ld_wo{i}")
            sp.wait_ge(S["dft_done"], GT)
            load(xl[:, :, :], rows(x), "ld_xl")
            sp.wait_ge(S["ssr_done"], 1)
            sp.dma_start(chunk_dst(0), chunk_src(0, 0)).then_inc(w_ld[0], 16)
            sp.wait_ge(S["pr_done"], TL)
            sp.dma_start(chunk_dst(1), chunk_src(1, 0)).then_inc(w_ld[1], 16)
            sp.dma_start(chunk_dst(2), chunk_src(2, 0)).then_inc(w_ld[2], 16)
            load(bias_raw[0:NE, 0:2 * FF], b_gate_up, "ld_bias")
            load(bias_raw[NE:2 * NE, 0:2 * FF], b_gate_up, "ld_bias")
            load(bias_raw[0:NE, 2 * FF:], b_down, "ld_bias")
            load(bias_raw[NE:2 * NE, 2 * FF:], b_down, "ld_bias")
            for t in range(TL):
                sp.wait_ge(S["h_ready"], t + 1)
                sp.dma_start(h_dram[t * P:(t + 1) * P, :], h_sb[:, t, :]).then_inc(S["h_stored"], 16)
            sp.wait_ge(S["x2_ready"], TL)
            sp.dma_start(chunk_dst(4), chunk_src(4, 0)).then_inc(w_ld[4], 16)
            sp.wait_ge(S["lg_done"], TL)
            sp.dma_start(chunk_dst(5), chunk_src(5, 0)).then_inc(w_ld[5], 16)
            sp.wait_ge(S["h_stored"], 16 * TL)
            sp.dma_start(chunk_dst(3), chunk_src(3, 0)).then_inc(w_ld[3], 16)
            sp.wait_ge(S["table_ready"], 1)
            n = sp.value_load(n_items[0:1, 0:1], min_val=NE, max_val=NI)
            with sp.Fori(1, NE) as e:
                before = sp.value_load(before_i[0:1, bass.ds(e, 1)], min_val=0, max_val=NI)
                for c in range(6):
                    mine = [i for i in range(PPC * c, PPC * (c + 1)) if i not in BY_POOL]
                    sp.wait_ge(S["lo_by_dve"], LO_DVE * before + lo_count(mine[-1])[1])
                    sp.nop(nofuse=True)
                    theirs = [i for i in range(PPC * c, PPC * (c + 1)) if i in BY_POOL]
                    if theirs:
                        sp.wait_ge(S["lo_by_pool"], LO_POOL * before + lo_count(theirs[-1])[1])
                        sp.nop(nofuse=True)
                    sp.dma_start(chunk_dst(c), chunk_src(c, e)).then_inc(w_ld[c], 16)
            sp.wait_ge(S["gathered"], 16 * (n + 1))
            sp.wait_ge(S["scattered"], 16 * (n + 2))
            load(gfin[:, :], g_final.partition_broadcast(P), "ld_gfin")
            for t in range(TL):
                sp.dma_start(y_sb[:, t, :], y_dram[t * P:(t + 1) * P, :]).then_inc(S["y_loaded"], 16)
                sp.wait_ge(S["y_loaded"], 16 * (t + 1))
            for t in range(TL):
                sp.wait_ge(S["out_ready"], t + 1)
                sp.dma_start(out[t * P:(t + 1) * P, :], o_sb[:, t, :]).then_inc(S["stored"], 16)
            sp.wait_ge(S["stored"], 16 * TL)

        @block.gpsimd
        def _(pool):
            nc.gpsimd.memset(wbd[:, :, :, :], 0.0).then_inc(S["wbd_zero"], 1)
            pool.wait_ge(S["ld_cst"], 16)
            nc.gpsimd.tensor_copy(beforeb[:, :], const("before"))
            nc.gpsimd.tensor_copy(onesb[:, :], ones).then_inc(S["bf_ready"], 1)
            pool.wait_ge(S["tc_done"], 4)
            for i in range(2):
                nc.gpsimd.memset(xp[i][:, 0:PAD_LO], 0.0)
                nc.gpsimd.memset(xp[i][:, PAD_LO + NC:PAD_LO + NC + 3], 0.0)
                last = nc.gpsimd.memset(xp[i][:, NX - 1:NX], 0.0)
            last.then_inc(S["edges_zero"], 1)
            for n in range(2 * RT):
                d, t = n // RT, n % RT
                pool.wait_ge(S["a_ready"], n + 1)
                if n == 0:
                    pool.wait_ge(S["conv_done"], RT)
                if n >= 2:
                    pool.wait_ge(S["w_ready"], n - 1)
                nc.gpsimd.tensor_tensor(Qm[n % 2][:, :], Am[:, d, t, :], Am[:, d, t, :], ALU.mult).then_inc(S["q_ready"], 1)
            pool.wait_ge(S["rg_ready"], RT)
            nc.gpsimd.memset(zero[:, :], 0.0).then_inc(S["y_zero"], 1)
            pool.wait_ge(S["y_zero"], 1)
            pool.dma_start(rows(y_dram), zero[:, :].unsqueeze(1).to_broadcast([P, TL, D])).then_inc(S["scattered"], 16)
            pool.wait_ge(S["ld_bias"], 64)
            nc.gpsimd.memset(bias_w[2 * NE:P, :].bitcast(F32), 0.0)
            nc.gpsimd.tensor_copy(bias_w[0:2 * NE, :], bias_raw[:, :]).then_inc(S["pool_step"], 1)
            pool.wait_ge(S["pool_step"], 1)
            nc.gpsimd.tensor_tensor(bias_w[NE:2 * NE, :], bias_raw[NE:2 * NE, :], bias_w[NE:2 * NE, :].bitcast(F32),
                                    ALU.subtract).then_inc(S["bias_ready"], 1)
            pool.wait_ge(S["cf_copied"], GT)
            pool.wait_ge(S["ssf_done"], 1)
            pool.wait_ge(S["bias_ready"], 1)
            nc.gpsimd.memset(xg[:, :], 0.0).then_inc(S["xg_zero"], 1)
            pool.wait_ge(S["xg_zero"], 1)
            pool.wait_ge(S["h_stored"], 16 * TL)

            last_row = pool.to_reg(NL - 1)

            def gather():
                pool.indirect_dma_start(xg[:, :], None, h_dram, bass.IndirectOffsetOnAxis(ap=idx_n[:, 0:1], axis=0),
                                        bounds_check=last_row, oob_is_err=False).then_inc(S["gathered"], 16)

            pool.wait_ge(S["idx_ready"], 1)
            gather()
            n = pool.value_load(n_items[0:1, 0:1], min_val=NE, max_val=NI)
            def lo_part(b, i):
                pool.wait_ge(S["hi_ready"], NPC * b + i + 1)
                nc.gpsimd.tensor_tensor(w_lo[i % RS][:, :], raw_piece(i), w_hi[i % RS][:, :].bitcast(F32), ALU.subtract
                                        ).then_inc(S["lo_by_pool"], 1)

            def scatter(b):
                pool.wait_ge(S["cur_ready"], b + 1)
                pool.wait_ge(S["o_copied"], 2 * b + 2)
                pool.wait_ge(S["scattered"], 16 * b + 16)
                pool.nop(nofuse=True)
                pool.indirect_dma_start(y_dram, bass.IndirectOffsetOnAxis(ap=idx_c[:, 0:1], axis=0), osb[:, :], None,
                                        bounds_check=last_row, oob_is_err=False, compute_op=ALU.add
                                        ).then_inc(S["scattered"], 16)

            with pool.Fori(0, NI) as b:
                with pool.If(b < n):
                    lo_part(b, BY_POOL[0])
                    scatter(b)
                    lo_part(b, BY_POOL[1])
                    pool.wait_ge(S["idx_ready"], b + 2)
                    pool.wait_ge(S["xt_done"], 2 * b + 2)
                    pool.nop(nofuse=True)
                    gather()
                    lo_part(b, BY_POOL[2])
                    lo_part(b, BY_POOL[3])
            scatter(n)

        @block.scalar
        def _(act):
            A = nc.scalar.activation
            act.wait_ge(S["ld_cols"], 16)
            a0 = COLS["c"][0]
            A(sp_t[:, 0:2, :].rearrange("p a b -> p (a b)"), pc[:, a0:a0 + 2 * KD], ACT.Sigmoid).then_inc(S["act_step"], 1)
            act.wait_ge(S["ld_ctx"], 16)
            for t in range(TC):
                A(junk[:, :], c_in[:, t, :], ACT.Square, accum_out=ss[:, t:t + 1]).then_inc(S["ssq_in"], 1)
                act.wait_ge(S["ssq_in"], t + 1)
            act.wait_ge(S["ld_x"], 16)
            for t in range(TL):
                A(junk[:, :], x_in[:, t, :], ACT.Square, accum_out=ss[:, TC + t:TC + t + 1]).then_inc(S["ssq_in"], 1)
                act.wait_ge(S["ssq_in"], TC + t + 1)
            act.wait_ge(S["rstd_in"], 1)
            A(ss[:, :], ss[:, :], ACT.Sqrt).then_inc(S["rstd_in"], 1)
            act.wait_ge(S["film_ready"], 1)
            for i in range(4):
                act.wait_ge(S["tc_done"], i + 1)
                for k in (2 * i, 2 * i + 1):
                    last = A(hT_c[:, k, :], ps[:, 1 + i, (k % 2) * NC:(k % 2 + 1) * NC], ACT.Identity,
                             bias=sh[:, k, 1:2], scale=sc[:, k, 1:2])
                last.then_inc(S["hc_copied"], 1)
            for k in range(0, KD, 2):
                act.wait_ge(S["tl_done"], k + 1)
                A(hT_l[:, k, :], ps[:, (5 + k) % 8, :], ACT.Identity, bias=sh[:, k, 0:1], scale=sc[:, k, 0:1]).then_inc(S["hl_by_act"], 1)
            act.wait_ge(S["edges_zero"], 1)
            for t in range(RT):
                act.wait_ge(S["xr_done"], t + 1)
                if t >= 2:
                    act.wait_ge(S["conv_done"], t - 1)
                A(xp[t % 2][:, PAD_LO:PAD_LO + NC], ps[:, t % 2, 0:NC], ACT.Copy)
                A(xp[t % 2][:, NC + 5:NC + 5 + NL], ps[:, 2 + t % 2, :], ACT.Copy).then_inc(S["xr_copied"], 1)
            for t in range(RT):
                act.wait_ge(S["gr_done"], t + 1)
                A(gelu[:, t, :], ps[:, 4 + t, :], ACT.Gelu_apprx_tanh).then_inc(S["gelu_done"], 1)
            act.wait_ge(S["sp_ready"], 1)
            A(sp_t[:, 2, :], sp_t[:, 1, :], ACT.Exp, scale=-1.0).then_inc(S["sp_ready"], 1)
            for d in range(2):
                for t in range(RT):
                    n = 2 * (RT * d + t)
                    act.wait_ge(S["gate_mm"], n + 1)
                    if d == 1 and t == 0:
                        act.wait_ge(S["root_ready"], RT)
                        act.wait_ge(S["ix_ready"], 2 * RT)
                    A(Rm[:, t, :], pair(n % 2)[:, NC:NC + NB], ACT.Sigmoid,
                      bias=pc[:, COLS["b_a"][0] + RT * d + t:COLS["b_a"][0] + RT * d + t + 1]).then_inc(S["sig_done"], 1)
                    act.wait_ge(S["gate_mm"], n + 2)
                    A(Um[:, d, t, :], pair((n + 1) % 2)[:, NC:NC + NB], ACT.Sigmoid,
                      bias=pc[:, COLS["b_x"][0] + RT * d + t:COLS["b_x"][0] + RT * d + t + 1]).then_inc(S["sig_done"], 1)
                if d == 0:
                    act.wait_ge(S["sp_ready"], 3)
                for t in range(RT):
                    m = RT * d + t
                    act.wait_ge(S["sig_done"], 2 * m + 1)
                    A(Am[:, d, t, :], Rm[:, t, :], ACT.Exp, scale=nsp[:, 0, m:m + 1]).then_inc(S["a_ready"], 1)
                for t in range(RT):
                    m = RT * d + t
                    act.wait_ge(S["a_ready"], m + 1)
                    A(Rm[:, t, :], Rm[:, t, :], ACT.Tanh, scale=nsp[:, 1, m:m + 1]).then_inc(S["th_ready"], 1)
                for t in range(RT):
                    m = RT * d + t
                    act.wait_ge(S["w_ready"], m + 1)
                    A(Rm[:, t, :], Rm[:, t, :], ACT.Sqrt).then_inc(S["root_ready"], 1)
            act.wait_ge(S["ix_ready"], 3 * RT)
            for g in range(GT):
                act.wait_ge(S["dft_done"], g + 1)
                A(sqF[:, g, :], ps[:, 4 + g, :], ACT.Square)
                A(catF[:, g, :], ps[:, 4 + g, :], ACT.Copy, scale=pc[:, COLS["g_f"][0] + g:COLS["g_f"][0] + g + 1]).then_inc(S["cf_copied"], 1)
            act.wait_ge(S["rsf_act"], 1)
            A(rsf[:, 1, :], rsf[:, 0, :], ACT.Sqrt).then_inc(S["rsf_act"], 1)
            act.wait_ge(S["rsf_ready"], 1)
            for t in range(TL):
                act.wait_ge(S["pf_done"], t + 1)
                A(Fb[:, t, :], pair(1 + t % 3), ACT.Copy, scale=rsf[:, 0, t:t + 1]).then_inc(S["pf_copied"], 1)
            for t in range(RT):
                act.wait_ge(S["rg_ready"], t + 1)
                A(Um[:, 1, t, NC:], Um[:, 0, t, NC:], ACT.Square).then_inc(S["act_step"], 1)
                act.wait_ge(S["act_step"], t + 2)
                A(Um[:, 0, t, NC:], Um[:, 0, t, NC:], ACT.Copy, scale=pc[:, COLS["g_r"][0] + t:COLS["g_r"][0] + t + 1]).then_inc(S["sqr_ready"], 1)
            act.wait_ge(S["rsf_act"], 3)
            A(rsf[:, 3, :], rsf[:, 2, :], ACT.Sqrt).then_inc(S["rsf_act"], 1)
            for t in range(TL):
                act.wait_ge(S["x2_ready"], t + 1)
                if t:
                    act.wait_ge(S["ssq_ffn"], 2 * t - 1)
                A(junk2[:, :], xl[:, t, :], ACT.Square, accum_out=ss[:, t:t + 1]).then_inc(S["ssq_ffn"], 1)
                act.wait_ge(S["ssq_ffn"], 2 * t + 2)
                A(rsf[:, 1, t:t + 1], rsf[:, 0, t:t + 1], ACT.Sqrt).then_inc(S["rt_ffn"], 1)
            for t in range(TL):
                act.wait_ge(S["ht_done"], 2 * t + 2)
                if t:
                    act.wait_ge(S["lg_done"], t)
                A(hT2[:, :, :].rearrange("p k n -> p (k n)"), pair(1 + t % 2), ACT.Copy).then_inc(S["ht_copied"], 1)
            act.wait_ge(S["m8_ready"], 1)
            for t in range(TL):
                last = A(ex[:, t, :], lg[:, t, :], ACT.Exp, bias=rs8[:, t:t + 1])
            last.then_inc(S["ex_ready"], 1)

            def split_xT(h, v):
                act.wait_ge(S["xt_done"], v)
                A(xT[0][:, 4 * h:4 * h + 4, :].rearrange("p k n -> p (k n)"), ps[:, h, :], ACT.Copy).then_inc(S["xT_hi_ready"], 1)

            def split_aT(j, b):
                act.wait_ge(S["at_done"], 2 * b + 1 + j)
                A(aT[0][:, 4 * j:4 * j + 4, :].rearrange("p k n -> p (k n)"), ps[:, 6, :], ACT.Copy).then_inc(S["aT_hi_ready"], 1)

            def hi_parts(b, e, i0, i1):
                for i in range(i0, i1):
                    if i % PPC == 0:
                        act.wait_ge(w_ld[i // PPC], 16 * e + 16)
                    act.wait_ge(S["piece_used"], NPC * b + i + 1)
                    A(w_hi[i % RS][:, :], raw_piece(i), ACT.Copy).then_inc(S["hi_ready"], 1)

            def gated_outputs(b):
                act.wait_ge(S["cur_ready"], b + 1)
                act.wait_ge(S["scattered"], 16 * b + 16)
                act.wait_ge(S["piece_used"], NPC * b + RS)
                for h in range(2):
                    A(osb[:, h * CH:(h + 1) * CH], ps[:, 4 + h, :], ACT.Copy, scale=gate_c[:, 0:1]).then_inc(S["o_copied"], 1)

            def sigmoid(j, b):
                act.wait_ge(S["g_ready"], 2 * b + 1 + j)
                A(sg[:, :], gb[:, :], ACT.Sigmoid, scale=ALPHA).then_inc(S["s_sig"], 1)

            split_xT(0, 1)
            split_xT(1, 2)
            n = act.value_load(n_items[0:1, 0:1], min_val=NE, max_val=NI)
            with act.Fori(0, NI) as b:
                with act.If(b < n):
                    e = act.value_load(item_i[0:1, bass.ds(b, 1)], min_val=0, max_val=NE - 1)
                    hi_parts(b, e, 0, 4)
                    gated_outputs(b)
                    hi_parts(b, e, 4, 12)
                    sigmoid(0, b)
                    hi_parts(b, e, 12, 16)
                    split_aT(0, b)
                    hi_parts(b, e, 16, 20)
                    sigmoid(1, b)
                    hi_parts(b, e, 20, 23)
                    split_aT(1, b)
                    hi_parts(b, e, 23, 24)
                    split_xT(0, 2 * b + 3)
                    split_xT(1, 2 * b + 4)
            gated_outputs(n)
            for t in range(TL):
                act.wait_ge(S["rt_out"], 3 * t + 1)
                A(junk3[:, :], xl[:, t, :], ACT.Square, accum_out=ss[:, t:t + 1]).then_inc(S["ssq_out"], 1)
                act.wait_ge(S["rt_out"], 3 * t + 2)
                act.wait_ge(S["ssq_out"], t + 1)
                A(rsf[:, 1, t:t + 1], rsf[:, 0, t:t + 1], ACT.Sqrt).then_inc(S["rt_out"], 1)

        @block.vector
        def _(dve):
            V = nc.vector
            steps = [0]

            def link(ins):
                steps[0] += 1
                ins.then_inc(S["dve_step"], 1)
                dve.wait_ge(S["dve_step"], steps[0])

            dve.wait_ge(S["act_step"], 1)
            for s, name in enumerate(("c", "c_ctx")):
                last = V.tensor_tensor(csil[:, :, s], col(name), sp_t[:, s, :], ALU.mult)
            last.then_inc(S["csil_ready"], 1)
            dve.wait_ge(S["csil_ready"], 1)
            link(V.tensor_scalar(sp_t[:, 0, :], col("lam"), -1.0, None, ALU.mult))
            V.tensor_tensor(sp_t[:, 1, :], sp_t[:, 0, :], col("lam"), ALU.max).then_inc(S["sp_ready"], 1)
            dve.wait_ge(S["ssq_in"], TC + TL)
            V.tensor_scalar(ss[:, :], ss[:, :], 1.0 / D, EPS, ALU.mult, ALU.add).then_inc(S["rstd_in"], 1)
            dve.wait_ge(S["rstd_in"], 2)
            link(V.reciprocal(ss[:, :], ss[:, :]))
            for t in range(TC):
                V.tensor_scalar(xs_c[:, t, :], c_in[:, t, :], ss[:, t:t + 1], None, ALU.mult).then_inc(S["xs_ready"], 1)
            for t in range(TL):
                V.tensor_scalar(xs_l[:, t, :], x_in[:, t, :], ss[:, TC + t:TC + t + 1], None, ALU.mult).then_inc(S["xs_ready"], 1)
            dve.wait_ge(S["mod_done"], 4)
            mod = ps[:, 0, 0:4 * KD].rearrange("p (m s) -> p m s", s=2)
            for s in range(2):
                V.tensor_tensor(sh[:, :, s], mod[:, 0:KD, s], col("b_shift"), ALU.add)
                link(V.tensor_tensor(sc[:, :, s], mod[:, KD:2 * KD, s], col("b_scale"), ALU.add))
                last = V.scalar_tensor_tensor(sc[:, :, s], sc[:, :, s], 1.0, col("g_mix"), ALU.add, ALU.mult)
            last.then_inc(S["film_ready"], 1)
            dve.wait_ge(S["film_ready"], 1)
            for k in range(1, KD, 2):
                dve.wait_ge(S["tl_done"], k + 1)
                V.tensor_scalar(hT_l[:, k, :], ps[:, (5 + k) % 8, :], sc[:, k, 0:1], sh[:, k, 0:1], ALU.mult, ALU.add).then_inc(S["hl_by_dve"], 1)
            dve.wait_ge(S["mm_done"], 1)
            for s in range(2):
                last = V.tensor_copy(MM[:, :, s, :], ps[:, 6 + s, :].rearrange("p (g j) -> p g j", g=GT))
            last.then_inc(S["mm_copied"], 1)
            for t in range(RT):
                dve.wait_ge(S["xr_copied"], t + 1)
                w = [pc[:, COLS["conv_w"][0] + RT * k + t:COLS["conv_w"][0] + RT * k + t + 1] for k in range(TAPS)]
                X = xp[t % 2]
                link(V.tensor_scalar(cv[:, :], X[:, 0:NX - 3], w[0], pc[:, COLS["conv_b"][0] + t:COLS["conv_b"][0] + t + 1], ALU.mult, ALU.add))
                for k in (1, 2):
                    link(V.scalar_tensor_tensor(cv[:, :], X[:, k:k + NX - 3], w[k], cv[:, :], ALU.mult, ALU.add))
                V.scalar_tensor_tensor(xc[:, t, 0:NC], X[:, 3:3 + NC], w[3], cv[:, 0:NC], ALU.mult, ALU.add)
                V.scalar_tensor_tensor(xc[:, t, NC:], X[:, 3 + LAT0:3 + LAT0 + NL], w[3], cv[:, LAT0:LAT0 + NL], ALU.mult, ALU.add
                                       ).then_inc(S["conv_done"], 1)
                dve.wait_ge(S["conv_done"], t + 1)
            dve.wait_ge(S["sp_ready"], 2)
            e_, s_, s2, q_ = sp_t[:, 2, :], sp_t[:, 3, :], sp_t[:, 4, :], sp_t[:, 5, :]
            link(V.tensor_scalar(s_, e_, 2.0, None, ALU.add))
            link(V.reciprocal(s_, s_))
            link(V.tensor_tensor(s_, s_, e_, ALU.mult))
            link(V.tensor_tensor(s2, s_, s_, ALU.mult))
            link(V.tensor_scalar(q_, s2, 1.0 / 17, None, ALU.mult))
            for k in (15, 13, 11, 9, 7, 5, 3):
                link(V.scalar_tensor_tensor(q_, q_, 1.0 / k, s2, ALU.add, ALU.mult))
            link(V.scalar_tensor_tensor(q_, q_, 1.0, s_, ALU.add, ALU.mult))
            link(V.tensor_scalar(s_, sp_t[:, 0, :], 0.0, None, ALU.max))
            link(V.scalar_tensor_tensor(q_, q_, 2.0, s_, ALU.mult, ALU.add))
            V.tensor_scalar(nsp[:, 0, :], q_, -RG_C, None, ALU.mult)
            V.tensor_scalar(nsp[:, 1, :], q_, RG_C, None, ALU.mult).then_inc(S["sp_ready"], 1)
            for g in range(GT):
                dve.wait_ge(S["f_done"], g + 1)
                if g == 0:
                    dve.wait_ge(S["tl_done"], KD)
                V.tensor_copy(fT[:, g, :], ps[:, g, :]).then_inc(S["f_copied"], 1)

            zn = [0]

            def z_chunk():
                i = zn[0]
                zn[0] += 1
                dve.wait_ge(S[f"ld_zm{i % 2}"], 16 * (i // 2 + 1))
                if i == 0:
                    dve.wait_ge(S["tl_done"], KD)
                if i >= 2:
                    dve.wait_ge(S["z_done"], i - 1)
                W, Z = wm_rest[i % 2], z_buf[i % 2]
                link(V.tensor_scalar(Z[:, :], W[:, 0, :], csil[:, 0, 0:1], None, ALU.mult))
                for k in range(1, KD):
                    ins = V.scalar_tensor_tensor(Z[:, :], W[:, k, :], csil[:, k, 0:1], Z[:, :], ALU.mult, ALU.add)
                    if k < KD - 1:
                        link(ins)
                ins.then_inc(S["z_ready"], 1)

            def z_add():
                i = zn[0] - 1
                dve.wait_ge(S["z_done"], i + 1)
                if i == 0:
                    dve.wait_ge(S["ld_bc"], 16)
                v = bc[:, i // 2, (i % 2) * CH:(i % 2 + 1) * CH]
                V.tensor_tensor(v, ps[:, z_bank(i), :], v, ALU.add).then_inc(S["bc_ready"], 1)

            def y_copy(m):
                dve.wait_ge(S["y_done"], m + 1)
                v = pair(2 + m % 2).rearrange("p (g s j) -> p g s j", g=GT, s=2)
                for s in range(2):
                    last = V.tensor_copy(Y[:, m, s, :].rearrange("p (g j) -> p g j", g=GT), v[:, :, s, :])
                last.then_inc(S["y_copied"], 1)

            def ix(d):
                for t in range(RT):
                    dve.wait_ge(S["sig_done"], 2 * (RT * d + t) + 2)
                    V.tensor_tensor(Um[:, d, t, :], Um[:, d, t, :], xc[:, t, :], ALU.mult).then_inc(S["ix_ready"], 1)

            def drive(d):
                for t in range(RT):
                    m = RT * d + t
                    dve.wait_ge(S["q_ready"], m + 1)
                    dve.wait_ge(S["th_ready"], m + 1)
                    V.scalar_tensor_tensor(Rm[:, t, :], Qm[m % 2][:, :], 1.0, Rm[:, t, :], ALU.add, ALU.mult).then_inc(S["w_ready"], 1)
                for t in range(RT):
                    m = RT * d + t
                    dve.wait_ge(S["root_ready"], m + 1)
                    V.tensor_tensor(Um[:, d, t, :], Um[:, d, t, :], Rm[:, t, :], ALU.mult).then_inc(S["ix_ready"], 1)

            def scan(d):
                for t in range(RT):
                    a, u = Am[:, d, t, :], Um[:, d, t, :]
                    if t == 0:
                        dve.wait_ge(S["ix_ready"], 2 * RT * (d + 1))
                        if d == 1:
                            dve.wait_ge(S["a_ready"], 2 * RT)
                    if d == 0:
                        link(V.tensor_tensor_scan(u[:, 0:NC], a[:, 0:NC], u[:, 0:NC], 0.0, ALU.mult, ALU.add))
                        link(V.tensor_tensor_scan(u[:, NC:], a[:, NC:], u[:, NC:], u[:, NC - 1:NC], ALU.mult, ALU.add))
                    else:
                        link(V.tensor_tensor_scan(u[:, 0:NC][:, ::-1], a[:, 0:NC][:, ::-1], u[:, 0:NC][:, ::-1], 0.0, ALU.mult, ALU.add))
                        link(V.tensor_tensor_scan(u[:, NC:][:, ::-1], a[:, NC:][:, ::-1], u[:, NC:][:, ::-1], u[:, 0:1], ALU.mult, ALU.add))

            ix(0)
            z_chunk()
            z_add()
            for m in range(TL):
                y_copy(m)
            drive(0)
            ix(1)
            z_chunk()
            scan(0)
            z_add()
            z_chunk()
            drive(1)
            z_add()
            scan(1)
            dve.wait_ge(S["gelu_done"], RT)
            for t in range(RT):
                link(V.tensor_tensor(Um[:, 0, t, NC:], Um[:, 0, t, NC:], Um[:, 1, t, NC:], ALU.add))
                V.tensor_tensor(Um[:, 0, t, NC:], Um[:, 0, t, NC:], gelu[:, t, :], ALU.mult).then_inc(S["rg_ready"], 1)
            dve.wait_ge(S["ssf_done"], 1)
            V.tensor_scalar(rsf[:, 0, :], ps[:, 0, 0:TL], 1.0 / DF, EPS, ALU.mult, ALU.add).then_inc(S["rsf_act"], 1)
            dve.wait_ge(S["rsf_act"], 2)
            V.reciprocal(rsf[:, 0, :], rsf[:, 1, :]).then_inc(S["rsf_ready"], 1)
            while zn[0] < 8:
                z_chunk()
                z_add()
            dve.wait_ge(S["bc_ready"], 8)
            dve.wait_ge(S["ld_gnf"], 16)
            V.scalar_tensor_tensor(bc[:, 2, :], bc[:, 2, :], 1.0, gnf[:, :], ALU.add, ALU.mult).then_inc(S["bc_ready"], 1)
            dve.wait_ge(S["ssr_done"], 1)
            V.tensor_scalar(rsf[:, 2, :], ps[:, 1, 0:TL], 1.0 / DR, EPS, ALU.mult, ALU.add).then_inc(S["rsf_act"], 1)
            dve.wait_ge(S["rsf_act"], 4)
            link(V.reciprocal(rsf[:, 2, :], rsf[:, 3, :]))
            dve.wait_ge(S["ld_xl"], 16)
            dve.wait_ge(S["bc_ready"], 9)
            for t in range(TL):
                dve.wait_ge(S["pr_done"], t + 1)
                dve.wait_ge(S["pf_copied"], t + 1)
                V.scalar_tensor_tensor(Fb[:, t, :], pair(1 + t % 3), rsf[:, 2, t:t + 1], Fb[:, t, :], ALU.mult, ALU.add).then_inc(S["pr_read"], 1)
                dve.wait_ge(S["pr_read"], t + 1)
                link(V.tensor_tensor(Fb[:, t, :], Fb[:, t, :], bc[:, 0, :], ALU.mult))
                V.tensor_tensor(xl[:, t, :], xl[:, t, :], Fb[:, t, :], ALU.add).then_inc(S["x2_ready"], 1)
                dve.wait_ge(S["ssq_ffn"], 2 * t + 1)
                V.tensor_scalar(rsf[:, 0, t:t + 1], ss[:, t:t + 1], 1.0 / D, EPS, ALU.mult, ALU.add).then_inc(S["ssq_ffn"], 1)
                dve.wait_ge(S["rt_ffn"], t + 1)
                link(V.reciprocal(rsf[:, 1, t:t + 1], rsf[:, 1, t:t + 1]))
                link(V.scalar_tensor_tensor(h_sb[:, t, :], xl[:, t, :], rsf[:, 1, t:t + 1], bc[:, 2, :], ALU.mult, ALU.mult))
                V.tensor_tensor(h_sb[:, t, :], h_sb[:, t, :], bc[:, 1, :], ALU.add).then_inc(S["h_ready"], 1)
            dve.wait_ge(S["ld_wr"], 32)
            dve.wait_ge(S["lg_done"], TL)
            link(V.tensor_tensor(lg[:, :, :], ps[:, 0, 0:TL * NE].rearrange("p (t e) -> p t e", t=TL),
                                 br[:, :].unsqueeze(1).to_broadcast([P, TL, NE]), ALU.add))
            for t in range(TL):
                link(V.max(m8[:, t, :], lg[:, t, :]))
                last = V.max_index(i8[:, t, :], m8[:, t, :], lg[:, t, :])
            V.tensor_scalar(rs8[:, 0:TL], m8[:, :, 0], -1.0, None, ALU.mult).then_inc(S["m8_ready"], 1)
            dve.wait_ge(S["m8_ready"], 1)
            link(V.tensor_copy(if8[:, :, :], i8[:, :, :]))
            exp_bc = const("expert").unsqueeze(1).to_broadcast([P, TL, NE])
            link(V.tensor_tensor(msk[:, :, :], exp_bc, if8[:, :, 0:1].to_broadcast([P, TL, NE]), ALU.is_equal))
            for k in range(1, TOPK):
                link(V.tensor_tensor(one[:, :, :], exp_bc, if8[:, :, k:k + 1].to_broadcast([P, TL, NE]), ALU.is_equal))
                link(V.tensor_tensor(msk[:, :, :], msk[:, :, :], one[:, :, :], ALU.add))
            V.tensor_copy(mskb[:, :, :], msk[:, :, :]).then_inc(S["mask_ready"], 1)
            dve.wait_ge(S["ex_ready"], 1)
            link(V.tensor_tensor(ex[:, :, :], ex[:, :, :], msk[:, :, :], ALU.mult))
            link(V.tensor_reduce(rs8[:, 4:4 + TL], ex[:, :, :], AX.X, ALU.add))
            link(V.reciprocal(rs8[:, 4:4 + TL], rs8[:, 4:4 + TL]))
            link(V.tensor_tensor(gts[:, :, :], ex[:, :, :], rs8[:, 4:4 + TL].unsqueeze(2).to_broadcast([P, TL, NE]), ALU.mult))
            link(V.tensor_copy(meta[:, :, :, 2], gts[:, :, :]))
            link(V.tensor_tensor(gtr[:, :, :], gts[:, :, :], meta[:, :, :, 2], ALU.subtract))
            link(V.tensor_copy(meta[:, :, :, 3], gtr[:, :, :]))
            link(V.tensor_tensor(gts[:, :, :], gtr[:, :, :], meta[:, :, :, 3], ALU.subtract))
            link(V.tensor_copy(meta[:, :, :, 4], gts[:, :, :]))
            tok = const("token").rearrange("p (t s) -> p t s", s=2).unsqueeze(2).to_broadcast([P, TL, NE, 2])
            link(V.tensor_copy(meta[:, :, :, 0:2], tok))
            dve.wait_ge(S["pos_done"], 1)
            link(V.scalar_tensor_tensor(posm[:, :, :], ps[:, 1, 0:TL * NE].rearrange("p (t e) -> p t e", t=TL), 1.0,
                                        msk[:, :, :], ALU.add, ALU.mult))
            link(V.tensor_scalar(posm[:, :, :], posm[:, :, :], -1.0, None, ALU.add))
            link(V.tensor_copy(cnt[:, :], ps[:, 2, 0:NE]))
            link(V.tensor_scalar(ovf[:, :], cnt[:, :], float(P), 1.0, ALU.is_gt, ALU.add))
            for j in range(2, NL // P):
                link(V.scalar_tensor_tensor(ovf[:, :], cnt[:, :], float(P * j), ovf[:, :], ALU.is_gt, ALU.add))
            link(V.tensor_tensor_scan(end[:, :], ones[:, 0:NE], ovf[:, :], 0.0, ALU.mult, ALU.add))
            V.scalar_tensor_tensor(before_i[:, :], end[:, :], -1.0, ovf[:, :], ALU.add, ALU.subtract)
            V.memset(item_e[:, NI:], 0.0)
            V.memset(item_o[:, :], 0.0)
            link(V.tensor_tensor(mq[:, :, :], end[:, :].unsqueeze(1).to_broadcast([P, NI, NE]),
                                 item_no.unsqueeze(2).to_broadcast([P, NI, NE]), ALU.is_le))
            link(V.tensor_reduce(item_e[:, 0:NI], mq[:, :, :], AX.X, ALU.add))
            link(V.tensor_tensor(mq[:, :, :], mq[:, :, :], ovf[:, :].unsqueeze(1).to_broadcast([P, NI, NE]), ALU.mult))
            link(V.tensor_reduce(item_o[:, 0:NI], mq[:, :, :], AX.X, ALU.add))
            link(V.tensor_tensor(item_o[:, 0:NI], item_no, item_o[:, 0:NI], ALU.subtract))
            link(V.tensor_scalar(item_o[:, 0:NI], item_o[:, 0:NI], float(P), None, ALU.mult))
            link(V.tensor_scalar(item_e[:, 0:NI], item_e[:, 0:NI], float(NE - 1), None, ALU.min))
            V.tensor_copy(item_i[:, :], item_e[:, :])
            V.tensor_copy(n_items[:, :], end[:, NE - 1:NE]).then_inc(S["table_ready"], 1)
            dve.wait_ge(S["table_ready"], 1)

            def pick_tokens(b, e):
                V.tensor_copy(metab[:, :, :], meta[:, :, bass.ds(e, 1), :].rearrange("p t e s -> p t (e s)"))
                V.scalar_tensor_tensor(sel[:, :, :], const("slot").unsqueeze(1).to_broadcast([P, TL, P]),
                                       item_o[:, bass.ds(b, 1)], posm[:, :, bass.ds(e, 1)].to_broadcast([P, TL, P]),
                                       ALU.add, ALU.is_equal).then_inc(S["sel_ready"], 1)

            def pick_expert(b):
                V.tensor_tensor(pick[:, :], const("expert_of_row").to_broadcast([P, P]),
                                item_e[:, bass.ds(b, 1)].to_broadcast([P, P]), ALU.is_equal).then_inc(S["pick_ready"], 1)

            def numbers(v):
                dve.wait_ge(S["meta_done"], v)
                V.tensor_copy(msb[:, :], ps[:, 7, 0:5]).then_inc(S["gate_free"], 1)
                dve.wait_ge(S["gate_free"], v)
                V.tensor_reduce(gate_n[:, :], msb[:, 2:5], AX.X, ALU.add)
                V.scalar_tensor_tensor(idx_n[:, :], msb[:, 0:1], float(OUT_OF_RANGE), msb[:, 1:2], ALU.add, ALU.add).then_inc(S["idx_ready"], 1)

            def split_xT(h, v):
                dve.wait_ge(S["xT_hi_ready"], v)
                V.tensor_tensor(xT[1][:, 4 * h:4 * h + 4, :].rearrange("p k n -> p (k n)"), ps[:, h, :],
                                xT[0][:, 4 * h:4 * h + 4, :].rearrange("p k n -> p (k n)").bitcast(F32), ALU.subtract
                                ).then_inc(S["xT_lo_ready"], 1)

            def split_aT(j, b):
                dve.wait_ge(S["aT_hi_ready"], 2 * b + 1 + j)
                V.tensor_tensor(aT[1][:, 4 * j:4 * j + 4, :].rearrange("p k n -> p (k n)"), ps[:, 6, :],
                                aT[0][:, 4 * j:4 * j + 4, :].rearrange("p k n -> p (k n)").bitcast(F32), ALU.subtract
                                ).then_inc(S["aT_lo_ready"], 1)

            def lo_parts(b, i0, i1):
                for i in range(i0, i1):
                    if i not in BY_POOL:
                        dve.wait_ge(S["hi_ready"], NPC * b + i + 1)
                        V.tensor_tensor(w_lo[i % RS][:, :], raw_piece(i), w_hi[i % RS][:, :].bitcast(F32), ALU.subtract
                                        ).then_inc(S["lo_by_dve"], 1)

            V.memset(gate_c[:, :], 0.0)
            V.memset(idx_c[:, :], OUT_OF_RANGE).then_inc(S["cur_ready"], 1)
            pick_tokens(0, 0)
            pick_expert(0)
            dve.wait_ge(S["scattered"], 16)
            numbers(1)
            V.memset(rs8[:, :], 0.0).then_inc(S["piece_used"], RS)
            split_xT(0, 1)
            split_xT(1, 2)

            def swiglu(j, b):
                dve.wait_ge(S["piece_used"], NPC * b + 2 * PPC * (j + 1) + RS)
                V.tensor_scalar(gb[:, :], ps[:, 2 * j, :], LIMIT, None, ALU.min).then_inc(S["g_ready"], 1)
                V.tensor_scalar(ub[:, :], ps[:, 2 * j + 1, :], LIMIT, -LIMIT, ALU.min, ALU.max).then_inc(S["dve_u"], 1)
                dve.wait_ge(S["g_ready"], 2 * b + 1 + j)
                dve.wait_ge(S["dve_u"], 4 * b + 2 * j + 1)
                V.scalar_tensor_tensor(ub[:, :], ub[:, :], 1.0, gb[:, :], ALU.add, ALU.mult).then_inc(S["dve_u"], 1)
                dve.wait_ge(S["dve_u"], 4 * b + 2 * j + 2)
                dve.wait_ge(S["s_sig"], 2 * b + 1 + j)
                V.tensor_tensor(ab[:, :], ub[:, :], sg[:, :], ALU.mult).then_inc(S["act_ready"], 1)

            n = dve.value_load(n_items[0:1, 0:1], min_val=NE, max_val=NI)
            with dve.Fori(0, NI) as b:
                with dve.If(b < n):
                    e = dve.value_load(item_i[0:1, bass.ds(b + 1, 1)], min_val=0, max_val=NE - 1)
                    lo_parts(b, 0, 4)
                    dve.wait_ge(S["meta_done"], b + 1)
                    pick_tokens(b + 1, e)
                    lo_parts(b, 4, 12)
                    swiglu(0, b)
                    lo_parts(b, 12, 16)
                    split_aT(0, b)
                    dve.wait_ge(S["scattered"], 16 * b + 32)
                    dve.wait_ge(S["o_copied"], 2 * b + 2)
                    V.tensor_copy(idx_c[:, :], idx_n[:, :])
                    V.tensor_copy(gate_c[:, :], gate_n[:, :]).then_inc(S["cur_ready"], 1)
                    dve.wait_ge(S["cur_ready"], b + 2)
                    dve.wait_ge(S["gathered"], 16 * b + 16)
                    numbers(b + 2)
                    lo_parts(b, 16, 20)
                    swiglu(1, b)
                    lo_parts(b, 20, 23)
                    split_aT(1, b)
                    lo_parts(b, 23, 24)
                    dve.wait_ge(S["bias_used"], b + 1)
                    pick_expert(b + 1)
                    split_xT(0, 2 * b + 3)
                    split_xT(1, 2 * b + 4)
            dve.wait_ge(S["ld_gfin"], 16)
            for t in range(TL):
                dve.wait_ge(S["y_loaded"], 16 * (t + 1))
                link(V.tensor_tensor(y_sb[:, t, :], y_sb[:, t, :], bc[:, 3, :], ALU.mult))
                V.tensor_tensor(xl[:, t, :], xl[:, t, :], y_sb[:, t, :], ALU.add).then_inc(S["rt_out"], 1)
                dve.wait_ge(S["ssq_out"], t + 1)
                V.tensor_scalar(rsf[:, 0, t:t + 1], ss[:, t:t + 1], 1.0 / D, EPS, ALU.mult, ALU.add).then_inc(S["rt_out"], 1)
                dve.wait_ge(S["rt_out"], 3 * t + 3)
                link(V.reciprocal(rsf[:, 1, t:t + 1], rsf[:, 1, t:t + 1]))
                V.scalar_tensor_tensor(o_sb[:, t, :], xl[:, t, :], rsf[:, 1, t:t + 1], gfin[:, :], ALU.mult, ALU.mult).then_inc(S["out_ready"], 1)

        @block.tensor
        def _(pe):
            MMUL = nc.tensor.matmul
            pe.wait_ge(S["ld_cst"], 16)
            pe.wait_ge(S["csil_ready"], 1)
            for q in range(4):
                pe.wait_ge(S[f"ld_wm{q}"], 16)
                for m in range(4):
                    c0 = 2 * (4 * q + m)
                    for k in range(KD):
                        last = MMUL(ps[:, 0, c0:c0 + 2], wm_first[q][:, k, m * P:(m + 1) * P], csil[:, k, :],
                                    start=(k == 0), stop=(k == KD - 1))
                last.then_inc(S["mod_done"], 1)
            pe.wait_ge(S["xs_ready"], TC)
            for k in range(KD):
                for t in range(TC):
                    last = nc.tensor.transpose(ps[:, 1 + k // 2, (k % 2) * NC + t * P:(k % 2) * NC + (t + 1) * P],
                                               xs_c[:, t, k * P:(k + 1) * P], ident)
                if k % 2:
                    last.then_inc(S["tc_done"], 1)
            pe.wait_ge(S["xs_ready"], TC + TL)
            for k in range(KD):
                if k == 3:
                    pe.wait_ge(S["film_ready"], 1)
                if k > 3:
                    pe.wait_ge(S["hc_copied"], k - 3)
                for t in range(TL):
                    last = nc.tensor.transpose(ps[:, (5 + k) % 8, t * P:(t + 1) * P], xs_l[:, t, k * P:(k + 1) * P], ident)
                last.then_inc(S["tl_done"], 1)
            pe.wait_ge(S["ld_wf"], 16)
            pe.wait_ge(S["hl_by_dve"], 1)
            pe.wait_ge(S["hl_by_act"], 2)
            for s, name in enumerate(("cd", "neg_sd")):
                last = MMUL(ps[:, 6 + s, :], const(name), wf[:, :, :].rearrange("p g j -> p (g j)"), start=True, stop=True)
            last.then_inc(S["mm_done"], 1)
            pe.wait_ge(S["hl_by_act"], KD // 2)
            pe.wait_ge(S["hl_by_dve"], KD // 2)
            pe.wait_ge(S["hc_copied"], 4)
            pe.wait_ge(S["ld_win1"], 16)
            for t in range(RT):
                if t >= 2:
                    pe.wait_ge(S["xr_copied"], t - 1)
                for k in range(KD):
                    MMUL(ps[:, t % 2, 0:NC], win[1][:, k, t * P:(t + 1) * P], hT_c[:, k, :], start=(k == 0), stop=(k == KD - 1))
                for k in range(KD):
                    last = MMUL(ps[:, 2 + t % 2, :], win[1][:, k, t * P:(t + 1) * P], hT_l[:, k, :], start=(k == 0), stop=(k == KD - 1))
                last.then_inc(S["xr_done"], 1)
            pe.wait_ge(S["ld_win2"], 16)
            pe.wait_ge(S["mm_copied"], 1)
            for t in range(RT):
                for k in range(KD):
                    last = MMUL(ps[:, 4 + t, :], win[2][:, k, t * P:(t + 1) * P], hT_l[:, k, :], start=(k == 0), stop=(k == KD - 1))
                last.then_inc(S["gr_done"], 1)
            pe.wait_ge(S["ld_win0"], 16)
            pe.wait_ge(S["xr_copied"], RT)
            for g in range(GT):
                for k in range(KD):
                    last = MMUL(ps[:, g, :], win[0][:, k, g * P:(g + 1) * P], hT_l[:, k, :], start=(k == 0), stop=(k == KD - 1))
                last.then_inc(S["f_done"], 1)

            def gates(d):
                for t in range(RT):
                    for a in range(2):
                        n = 2 * (RT * d + t) + a
                        if n == 0:
                            pe.wait_ge(S["ld_wbd"], 64)
                            pe.wait_ge(S["conv_done"], RT)
                            pe.wait_ge(S["f_copied"], GT)
                        if n >= 2:
                            pe.wait_ge(S["sig_done"], n - 1)
                        v = pair(n % 2)
                        MMUL(v[:, NC:2 * NC], wbd[:, a, RT * d + t, :], xc[:, t, 0:NC], start=True, stop=True)
                        MMUL(v[:, 2 * NC:], wbd[:, a, RT * d + t, :], xc[:, t, NC:], start=True, stop=True).then_inc(S["gate_mm"], 1)

            zc = [0]

            def z_sum():
                i = zc[0]
                zc[0] += 1
                pe.wait_ge(S["z_ready"], i + 1)
                if i >= 2:
                    pe.wait_ge(S["bc_ready"], i - 1)
                MMUL(ps[:, z_bank(i), :], ones, z_buf[i % 2][:, :], start=True, stop=True).then_inc(S["z_done"], 1)

            gates(0)
            pe.wait_ge(S["gelu_done"], RT)
            z_sum()
            pe.wait_ge(S["bc_ready"], 1)
            for m in range(TL):
                if m >= 2:
                    pe.wait_ge(S["y_copied"], m - 1)
                for g in range(GT):
                    last = MMUL(pair(2 + m % 2)[:, g * 2 * P:(g + 1) * 2 * P], fT[:, g, m * P:(m + 1) * P],
                                MM[:, g, :, :].rearrange("p s j -> p (s j)"), start=True, stop=True)
                last.then_inc(S["y_done"], 1)
            gates(1)
            pe.wait_ge(S["y_copied"], TL)
            pe.wait_ge(S["ld_dft"], 32)
            for g in range(GT):
                for m in range(TL):
                    for s in range(2):
                        last = MMUL(ps[:, 4 + g, :], Y[:, m, s, g * P:(g + 1) * P], dft_sb[:, s, m, :],
                                    start=(m == 0 and s == 0), stop=(m == TL - 1 and s == 1))
                last.then_inc(S["dft_done"], 1)
                if g < 2:
                    pe.wait_ge(S["sig_done"], 4 * RT)
                    z_sum()
            pe.wait_ge(S["cf_copied"], GT)
            pe.wait_ge(S["sig_done"], 4 * RT)
            for t in range(TL):
                for g in range(GT):
                    last = MMUL(ps[:, 0, t:t + 1], sqF[:, g, t * P:(t + 1) * P], ones[:, 0:1], start=(g == 0), stop=(g == GT - 1))
            last.then_inc(S["ssf_done"], 1)
            while zc[0] < 8:
                z_sum()
            pe.wait_ge(S["bc_ready"], 8)
            pe.wait_ge(S["ld_wo0"], 16)
            for t in range(TL):
                if t >= 3:
                    pe.wait_ge(S["pf_copied"], t - 2)
                for n in range(2):
                    for k in range(GT):
                        last = MMUL(ps[:, 2 * (1 + t % 3) + n, :], catF[:, k, t * P:(t + 1) * P], wo[0][:, k, n * CH:(n + 1) * CH],
                                    start=(k == 0), stop=(k == GT - 1))
                last.then_inc(S["pf_done"], 1)
            pe.wait_ge(S["sqr_ready"], RT)
            for t in range(TL):
                for g in range(RT):
                    last = MMUL(ps[:, 1, t:t + 1], Um[:, 1, g, NC + t * P:NC + (t + 1) * P], ones[:, 0:1], start=(g == 0), stop=(g == RT - 1))
            last.then_inc(S["ssr_done"], 1)
            pe.wait_ge(S["ld_wo1"], 16)
            pe.wait_ge(S["pf_copied"], TL)
            for t in range(TL):
                if t >= 3:
                    pe.wait_ge(S["pr_read"], t - 2)
                for n in range(2):
                    for k in range(RT):
                        last = MMUL(ps[:, 2 * (1 + t % 3) + n, :], Um[:, 0, k, NC + t * P:NC + (t + 1) * P], wo[1][:, k, n * CH:(n + 1) * CH],
                                    start=(k == 0), stop=(k == RT - 1))
                last.then_inc(S["pr_done"], 1)
            pe.wait_ge(S["ld_wr"], 32)
            for t in range(TL):
                pe.wait_ge(S["h_ready"], t + 1)
                if t == 0:
                    pe.wait_ge(S["pr_read"], TL)
                if t >= 2:
                    pe.wait_ge(S["ht_copied"], t - 1)
                for k in range(KD):
                    last = nc.tensor.transpose(pair(1 + t % 2)[:, k * P:(k + 1) * P], h_sb[:, t, k * P:(k + 1) * P], ident)
                    if k % 4 == 3:
                        last.then_inc(S["ht_done"], 1)
                pe.wait_ge(S["ht_copied"], t + 1)
                for k in range(KD):
                    last = MMUL(ps[:, 0, t * NE:(t + 1) * NE], hT2[:, k, :], wr[:, k, :], start=(k == 0), stop=(k == KD - 1))
                last.then_inc(S["lg_done"], 1)
            pe.wait_ge(S["bf_ready"], 1)
            pe.wait_ge(S["mask_ready"], 1)
            for t in range(TL):
                for u in range(t):
                    MMUL(ps[:, 1, t * NE:(t + 1) * NE], onesb[:, :], mskb[:, u, :], start=(u == 0), stop=False)
                MMUL(ps[:, 1, t * NE:(t + 1) * NE], beforeb[:, :], mskb[:, t, :], start=(t == 0), stop=True)
            for t in range(TL):
                last = MMUL(ps[:, 2, 0:NE], onesb[:, :], mskb[:, t, :], start=(t == 0), stop=(t == TL - 1))
            last.then_inc(S["pos_done"], 1)

            def slots_meta(v):
                pe.wait_ge(S["sel_ready"], v)
                for t in range(TL):
                    last = MMUL(ps[:, 7, 0:5], sel[:, t, :], metab[:, t, :], start=(t == 0), stop=(t == TL - 1))
                last.then_inc(S["meta_done"], 1)

            def rows_to_channels(v):
                pe.wait_ge(S["gathered"], v)
                for k in range(KD):
                    last = nc.tensor.transpose(ps[:, k // 4, (k % 4) * P:(k % 4 + 1) * P], xg[:, k * P:(k + 1) * P], ident)
                    if k % 4 == 3:
                        last.then_inc(S["xt_done"], 1)

            slots_meta(1)
            rows_to_channels(16)
            pe.wait_ge(S["bias_ready"], 1)

            def bias(bank, n0):
                return MMUL(ps[:, bank, :], pick[:, :], bias_w[:, n0:n0 + CH], start=True, stop=False)

            def products(b, i0, i1):
                for i in range(i0, i1):
                    pool, count = lo_count(i)
                    if pool:
                        pe.wait_ge(S["lo_by_pool"], LO_POOL * b + count)
                    else:
                        pe.wait_ge(S["lo_by_dve"], LO_DVE * b + count)
                    hi, lo = w_hi[i % RS], w_lo[i % RS]
                    for q in range(PIECE // CH):
                        c = slice(q * CH, (q + 1) * CH)
                        if i < 4 * PPC:
                            k, bank, rows_t = 2 * (i % PPC) + q, i // PPC, xT
                            stop = k == KD - 1
                        else:
                            k, bank, rows_t = i - 4 * PPC, 4 + q, aT
                            stop = k == FF // P - 1
                        MMUL(ps[:, bank, :], rows_t[0][:, k, :], hi[:, c], start=False, stop=False)
                        MMUL(ps[:, bank, :], rows_t[0][:, k, :], lo[:, c], start=False, stop=False)
                        last = MMUL(ps[:, bank, :], rows_t[1][:, k, :], hi[:, c], start=False, stop=stop)
                    last.then_inc(S["piece_used"], 1)

            def act_to_channels(j, b):
                pe.wait_ge(S["act_ready"], 2 * b + 1 + j)
                if j:
                    pe.wait_ge(S["aT_lo_ready"], 2 * b + 1)
                for k in range(4):
                    last = nc.tensor.transpose(ps[:, 6, k * P:(k + 1) * P], ab[:, k * P:(k + 1) * P], ident)
                last.then_inc(S["at_done"], 1)

            n = pe.value_load(n_items[0:1, 0:1], min_val=NE, max_val=NI)
            with pe.Fori(0, NI) as b:
                with pe.If(b < n):
                    pe.wait_ge(S["xT_lo_ready"], 2 * b + 2)
                    pe.wait_ge(S["pick_ready"], b + 1)
                    bias(0, 0)
                    bias(1, FF)
                    products(b, 0, 8)
                    bias(2, CH)
                    bias(3, FF + CH)
                    pe.wait_ge(S["gate_free"], b + 1)
                    slots_meta(b + 2)
                    products(b, 8, 12)
                    act_to_channels(0, b)
                    products(b, 12, 16)
                    pe.wait_ge(S["o_copied"], 2 * b + 2)
                    bias(4, 2 * FF)
                    bias(5, 2 * FF + CH).then_inc(S["bias_used"], 1)
                    pe.wait_ge(S["aT_lo_ready"], 2 * b + 1)
                    products(b, 16, 19)
                    act_to_channels(1, b)
                    products(b, 19, 20)
                    rows_to_channels(16 * b + 32)
                    pe.wait_ge(S["aT_lo_ready"], 2 * b + 2)
                    products(b, 20, 24)


_PERM = serpentine_order()


def kernel(x, c, ctx, c_ctx, w_mod, b_mod, g_norm_mix, g_norm_ffn, w_in, w_fourier, conv_w,
           conv_b, rg_w_a, rg_b_a, rg_w_x, rg_b_x, rg_lam, g_out_fourier, g_out_rg, w_out,
           w_router, b_router, w_gate_up, b_gate_up, w_down, b_down, g_final):
    import concourse.bacc as bacc
    from concourse.bass_utils import run_bass_kernel_spmd

    a = lambda t: np.ascontiguousarray(np.asarray(t))
    tiles = lambda v: np.asarray(v).reshape(-1, P).T
    bm = np.asarray(b_mod)[0]
    cols = {"c": tiles(c), "c_ctx": tiles(c_ctx), "g_mix": tiles(g_norm_mix), "b_shift": tiles(bm[:D]),
            "b_scale": tiles(bm[D:2 * D]), "conv_w": tiles(conv_w), "conv_b": tiles(conv_b), "b_a": tiles(rg_b_a),
            "b_x": tiles(rg_b_x), "lam": tiles(rg_lam), "g_f": tiles(g_out_fourier), "g_r": tiles(g_out_rg)}
    cst, dft = constants()
    arrays = {
        "x": a(np.asarray(x)[0][_PERM]), "ctx": a(ctx)[0], "w_mod": a(w_mod)[0], "b_mod": a(bm), "w_in": a(w_in)[0],
        "w_fourier": a(w_fourier)[0], "rg_w_a": a(rg_w_a)[0], "rg_w_x": a(rg_w_x)[0], "w_out": a(w_out)[0],
        "w_router": a(w_router)[0], "b_router": a(b_router)[0], "w_gate_up": a(w_gate_up)[0],
        "b_gate_up": a(b_gate_up)[0], "w_down": a(w_down)[0], "b_down": a(b_down)[0],
        "g_norm_ffn": a(g_norm_ffn)[0], "g_final": a(g_final),
        "cols": a(np.concatenate([cols[k] for k in COLS], axis=1)), "cst": cst, "dft": dft,
    }
    nc = bacc.Bacc("TRN2", target_bir_lowering=False, num_devices=1)
    args = [nc.dram_tensor(f"in_{k}", v.shape, mybir.dt.from_np(v.dtype), kind="ExternalInput").ap()
            for k, v in arrays.items()]
    out = nc.dram_tensor("out_rows", (NL, D), F32, kind="ExternalOutput").ap()
    build(nc, *args, out)
    r = run_bass_kernel_spmd(nc, [{f"in_{k}": v for k, v in arrays.items()}], core_ids=[0])
    got = np.empty((1, NL, D), np.float32)
    got[0, _PERM] = r.results[0]["out_rows"]
    return got
```

```python
import numpy as np
import concourse.bass as bass
from concourse import mybir
from contextlib import ExitStack

F32 = mybir.dt.float32
F32R = mybir.dt.float32r
BF16 = mybir.dt.bfloat16
I32 = mybir.dt.int32
U32 = mybir.dt.uint32
ALU = mybir.AluOpType
ACT = mybir.ActivationFunctionType
AX = mybir.AxisListType

P = 128
D = 1024
KD = D // P
NL, NC = 512, 256
TL, TC = NL // P, NC // P
DF = 512
DR = 512
GT = DF // P
RT = DR // P
GRID_W = 64
TAPS, PAD_LO = 4, 2
NE, TOPK = 32, 4
FF = 1024
CH = 512
EPS = 1e-6
LIMIT, ALPHA = 7.0, 1.702
RG_C = 8.0
NS = (NL * TOPK - 1) // P
NI = NE + NS
PIECE = 1024
NPC = 6 * 8 * CH // PIECE
PPC = 8 * CH // PIECE
RS = 4
BY_POOL = (5, 11, 17, 23)
LO_POOL = len(BY_POOL)
LO_DVE = NPC - LO_POOL


def lo_count(i):
    pool = i in BY_POOL
    return pool, sum((j in BY_POOL) == pool for j in range(i + 1))
OUT_OF_RANGE = 4096
KB = 1024

COLS = {}
_at = 0
for _name, _n in (("c", KD), ("c_ctx", KD), ("g_mix", KD), ("b_shift", KD), ("b_scale", KD),
                  ("conv_w", TAPS * RT), ("conv_b", RT), ("b_a", 2 * RT), ("b_x", 2 * RT),
                  ("lam", 2 * RT), ("g_f", GT), ("g_r", RT)):
    COLS[_name] = (_at, _at + _n)
    _at += _n
NCOL = _at

CST = {}
_at = 0
for _name, _n in (("ident", P), ("cd", P), ("neg_sd", P), ("ones", P), ("slot", P), ("before", P),
                  ("expert", NE), ("expert_of_row", 1), ("token", 2 * TL)):
    CST[_name] = (_at, _at + _n)
    _at += _n
NCST = _at


def serpentine_order():
    t = np.arange(NL).reshape(NL // GRID_W, GRID_W)
    t[1::2] = t[1::2, ::-1]
    return t.reshape(-1)


def constants():
    p = np.arange(P)
    c = np.zeros((P, NCST), np.float32)

    def put(name, a):
        c[:, CST[name][0]:CST[name][1]] = a

    put("ident", np.eye(P))
    ang = 2 * np.pi * ((p[:, None] * p[None]) % P) / P
    put("cd", np.cos(ang) / np.sqrt(P))
    put("neg_sd", -np.sin(ang) / np.sqrt(P))
    put("ones", 1.0)
    put("slot", p[None])
    put("before", (p[:, None] < p[None]).astype(np.float32))
    put("expert", np.arange(NE)[None])
    put("expert_of_row", (p % NE)[:, None])
    put("token", np.stack([np.tile(p[:, None], (1, TL)), np.tile(P * np.arange(TL) - OUT_OF_RANGE, (P, 1))], 2).reshape(P, 2 * TL))
    n = serpentine_order()
    ang = 2 * np.pi * ((n[:, None] * n[None]) % NL) / NL
    dft = np.stack([np.cos(ang), np.sin(ang)]) / np.sqrt(NL)
    return c, dft.astype(np.float32)


def build(nc, x, ctx, w_mod, b_mod, w_in, w_fourier, rg_w_a, rg_w_x, w_out, w_router, b_router,
          w_gate_up, b_gate_up, w_down, b_down, g_norm_ffn, g_final, cols, cst, dft, out):
    h_dram = nc.dram_tensor("h_rows", (NL, D), F32, kind="Internal").ap()
    y_dram = nc.dram_tensor("y_rows", (NL, D), F32, kind="Internal").ap()

    with ExitStack() as stack:
        base = 16512
        RING = base
        SLOT = [RING + 16 * KB * i for i in range(6)]
        ZA = RING + 96 * KB
        ZB = ZA + 24 * KB
        ZD = ZB + 22 * KB
        ZX = ZD + 32 * KB
        SM = ZX + 16 * KB
        STAGE_LAST = 229344 - 4 * KB

        def at(name, shape, off, dt=F32):
            return nc.alloc_sbuf_tensor_at(name, shape, dt, offset=off)

        small_at = [SM]

        def small(name, shape, dt=F32):
            n = int(np.prod(shape[1:])) * mybir.dt.size(dt)
            t = at(name, shape, small_at[0], dt)
            small_at[0] += -(-n // 32) * 32
            assert small_at[0] <= STAGE_LAST, name
            return t

        ps = stack.enter_context(nc.psum_tensor("ps", [P, 8, 512], F32))

        def sem(name):
            return stack.enter_context(nc.semaphore(name))

        wm_first = [at("wm_0", [P, KD, CH], ZD), at("wm_1", [P, KD, CH], ZD + 16 * KB),
                    at("wm_2", [P, KD, CH], SLOT[3]), at("wm_3", [P, KD, CH], SLOT[4])]
        wm_rest = [at("wm_a", [P, KD, CH], ZD), at("wm_b", [P, KD, CH], ZD + 16 * KB)]
        x_in = at("x_in", [P, TL, D], ZX)
        c_in = at("c_in", [P, TC, D], ZB)
        xs_c = at("xs_c", [P, TC, D], ZB + 8 * KB)
        junk = at("junk", [P, D], ZB + 16 * KB)
        wf = at("wf", [P, GT, P], ZB + 20 * KB)
        xs_l = at("xs_l", [P, TL, D], SLOT[5])
        win = [at(f"win_{i}", [P, KD, CH], SLOT[(4, 1, 2)[i]]) for i in range(3)]
        hT_l = at("hT_l", [P, KD, NL], ZA)
        hT_c = at("hT_c", [P, KD, NC], ZA + 16 * KB)
        hT_l_hi = at("hT_l_hi", [P, KD, NL], SLOT[0], F32R)
        hT_l_lo = at("hT_l_lo", [P, KD, NL], ZA, F32R)
        hT_c_hi = at("hT_c_hi", [P, KD, NC], SLOT[5], F32R)
        hT_c_lo = at("hT_c_lo", [P, KD, NC], ZA + 16 * KB, F32R)
        win_hi = [at(f"win_hi_{i}", [P, KD, P], SLOT[3] + 4 * KB * i, F32R) for i in range(4)]
        win_lo = [at(f"win_lo_{i}", [P, KD, CH], SLOT[(4, 1, 2)[i]], F32R) for i in range(3)]
        gnf = at("gnf", [P, D], SLOT[5] + 12 * KB)
        bc = at("bc", [P, 4, D], ZX)
        mod_rows = at("mod_rows", [2, 2 * D], ZB)
        fT = at("fT", [P, GT, NL], SLOT[5])
        dft_sb = at("dft_sb", [P, 2, TL, NL], SLOT[4])
        Y = at("Y", [P, TL, 2, DF], ZA)
        catF = [at("catF_hi", [P, GT, NL], SLOT[5], F32R), at("catF_lo", [P, GT, NL], ZB, F32R)]
        NX = PAD_LO + NC + 1 + PAD_LO + NL + 1
        LAT0 = NC + 3
        xp = [at(f"xp_{i}", [P, NX], ZB + 3200 * i) for i in range(2)]
        cv = at("cv", [P, NX - 3], ZB + 6400)
        NB = NC + NL
        xc = at("xc", [P, RT, NB], ZB + 9600)
        gelu = at("gelu", [P, RT, NL], ZA + 16 * KB)
        Am = at("Am", [P, 2, RT, NB], SLOT[0])
        Um = at("Um", [P, 2, RT, NB], SLOT[1] + 8 * KB)
        Rm = at("Rm", [P, RT, NB], SLOT[3])
        Qm = [at(f"Qm_{i}", [P, NB], ZB + 3200 * i) for i in range(2)]
        sqF = at("sqF", [P, GT, NL], ZB + 9600)
        wo = [at("wo_f", [P, GT, D], ZD), at("wo_r", [P, RT, D], ZD + 16 * KB)]
        wo_hi = [at("wo_f_hi", [P, 2, GT, CH], SLOT[3], F32R), at("wo_r_hi", [P, 2, RT, CH], SLOT[0], F32R)]
        wo_lo = [at("wo_f_lo", [P, GT, D], ZD, F32R), at("wo_r_lo", [P, RT, D], ZD + 16 * KB, F32R)]
        catR = [at("catR_hi", [P, RT, NL], ZA + 16 * KB, F32R), at("catR_lo", [P, 2, RT, NB], SLOT[1] + 8 * KB, F32R)]
        xl = at("xl", [P, TL, D], ZA)
        Fb = at("Fb", [P, TL, D], SLOT[4])
        h_sb = at("h_sb", [P, TL, D], SLOT[4])
        hT2 = [at(f"hT2_{i}", [P, KD, P], SLOT[5] + 4 * KB * i) for i in range(2)]
        junk2 = at("junk2", [P, D], SLOT[5] + 8 * KB)
        RA = ZD
        lg = at("lg", [P, TL, NE], RA)
        ex = at("ex", [P, TL, NE], RA + 512)
        one = at("one", [P, TL, NE], RA + 1024)
        msk = at("msk", [P, TL, NE], RA + 1536)
        gts = at("gts", [P, TL, NE], RA + 2048)
        gtr = at("gtr", [P, TL, NE], RA + 2560)
        mskb = at("mskb", [P, TL, NE], RA + 3072, BF16)
        gtb = at("gtb", [P, TL, NE], RA + 3328, BF16)
        m8 = at("m8", [P, TL, 8], RA + 3584)
        i8 = at("i8", [P, TL, 8], RA + 3712, U32)
        if8 = at("if8", [P, TL, 8], RA + 3840)
        cnt = at("cnt", [P, NE], RA + 3968)
        ovf = at("ovf", [P, NE], RA + 4096)
        end = at("end", [P, NE], RA + 4224)
        beg = at("beg", [P, NE], RA + 4352)
        rs8 = at("rs8", [P, 8], RA + 4480)
        lgT = at("lgT", [NE, NL], RA + 5 * KB)
        blocks = at("blocks", [NE, 1], RA + 4640)
        ends = at("ends", [NE, 1], RA + 4672)
        ended = at("ended", [NE, 2, NI], RA + 4704)
        slots = [at(f"slot_{i}", [P, 8 * CH], SLOT[i]) for i in range(6)]
        xg = at("xg", [P, D], ZB + 16 * KB)
        bias_raw = at("bias_raw", [2 * NE, 3 * D], SLOT[2] + 4 * KB)
        bias_w = at("bias_w", [P, 3 * D], ZB, F32R)
        gfin = at("gfin", [P, D], SLOT[3])
        osb = at("osb", [P, D], ZD + 28 * KB)
        gb = at("gb", [P, CH], ZD)
        ub = at("ub", [P, CH], ZD + 2 * KB)
        sg = at("sg", [P, CH], ZD + 4 * KB)
        ab = at("ab", [P, CH], ZD + 6 * KB)
        aT = [at("aT_hi", [P, 8, P], ZD + 8 * KB, F32R), at("aT_lo", [P, 8, P], ZD + 24 * KB, F32R)]
        xT = [at("xT_hi", [P, KD, P], ZX, F32R), at("xT_lo", [P, KD, P], ZX + 4 * KB, F32R)]
        stage_at = [ZD + 12 * KB, ZD + 16 * KB, ZD + 20 * KB, ZB + 12 * KB, ZA + 16 * KB, ZA + 20 * KB, ZX + 8 * KB, STAGE_LAST]
        w_hi = [at(f"w_hi_{i}", [P, PIECE], stage_at[2 * i], F32R) for i in range(RS)]
        w_lo = [at(f"w_lo_{i}", [P, PIECE], stage_at[2 * i + 1], F32R) for i in range(RS)]
        y_sb = at("y_sb", [P, TL, D], SLOT[0])
        o_sb = at("o_sb", [P, TL, D], SLOT[1])
        junk3 = at("junk3", [P, D], SLOT[2])
        zero = at("zero", [P, D], ZB + 18 * KB)

        wbd_at = small_at[0]
        wbd = small("wbd", [P, 2, 2 * RT, P])
        csb = small("csb", [P, NCST])
        pc = small("pc", [P, NCOL])
        MM = at("MM", [P, GT, 2, P], SLOT[5] + 12 * KB)
        csil = small("csil", [P, KD, 2])
        sh = small("sh", [P, KD, 2])
        sc = small("sc", [P, KD, 2])
        ss = small("ss", [P, 6])
        nsp = small("nsp", [P, 3, 2 * RT])
        sp_t = small("sp_t", [P, 6, 2 * RT])
        rsf = small("rsf", [P, 4, TL])
        wr = small("wr", [P, KD, NE])
        br = small("br", [P, NE])
        beforeb = small("beforeb", [P, P], BF16)
        onesb = small("onesb", [P, P], BF16)
        small_at[0], keep = wbd_at, small_at[0]
        posm = small("posm", [P, TL, NE])
        meta = small("meta", [P, TL, NE, 5], BF16)
        item_e = small("item_e", [P, NI + 1])
        item_o = small("item_o", [P, NI + 1])
        item_i = small("item_i", [P, NI + 1], I32)
        before_i = small("before_i", [P, NE], I32)
        n_items = small("n_items", [P, 1], I32)
        sel = small("sel", [P, TL, P], BF16)
        metab = small("metab", [P, TL, 5], BF16)
        pick = small("pick", [P, P], F32R)
        msb = small("msb", [P, 5])
        idx_n = small("idx_n", [P, 1], I32)
        idx_c = small("idx_c", [P, 1], I32)
        table_kept = small("table_kept", [P, 1])
        gate_n = small("gate_n", [P, 1])
        gate_c = small("gate_c", [P, 1])
        assert small_at[0] <= wbd_at + 8 * KB
        small_at[0] = keep

        def col(name):
            a, b = COLS[name]
            return pc[:, a:b]

        def const(name):
            a, b = CST[name]
            return csb[:, a:b]

        ident, ones = const("ident"), const("ones")
        item_no = const("slot")[:, 0:NI]

        wm_v = w_mod.rearrange("(k p) n -> p k n", p=P)
        win_v = w_in.rearrange("(k p) n -> p k n", p=P)
        wo_v = w_out.rearrange("(k p) n -> p k n", p=P)
        wgu_v = w_gate_up.rearrange("e (k p) n -> e p k n", p=P)
        wd_v = w_down.rearrange("e (k p) n -> e p k n", p=P)
        rows = lambda a: a.rearrange("(t p) d -> p t d", p=P)

        names = """ld_cols ld_cst ld_wf ld_ctx ld_x ld_wm0 ld_wm1 ld_wm2 ld_wm3 ld_win0 ld_win1 ld_win2 ld_wbd
            ld_zm0 ld_zm1 ld_dft ld_bc ld_gnf ld_wo0 ld_wo1 ld_xl ld_wr ld_bias ld_gfin dve_step act_step
            pool_step csil_ready mod_done mod_copied mod_turned bc_zero t_done t_by_act t_by_dve mean_in
            root_in mean_ffn film_ready edges_zero wbd_zero bf_ready ssq_in xs_ready hl_by_act hl_by_dve
            hc_hi hc_t hc_lo hl_t win_hi_ready win_lo_ready mm_done mm_copied xr_done xr_copied conv_done
            gr_done gelu_done f_done f_copied gate_mm sig_done z_ready z_done bc_ready y_done y_copied
            dft_done cf_copied ssf_done sp_ready ix_ready a_ready th_ready q_ready w_ready root_ready
            rg_ready sqr_ready ssr_done mean_heads root_heads rsf_ready cf_lo catR_hi_ready catR_lo_ready
            wo_hi_ready wo_lo_ready pf_done pf_copied pr_done pr_read x2_ready ssq_ffn rt_ffn h_scaled
            h_ready h_stored blocks_ready begin_done ended_ready items_done ht_done ht_copied lg_done
            lg_copied lg_turned m8_ready ex_ready mask_ready pos_done table_ready y_zero bias_ready
            gate_free xg_zero dve_u hi_ready lo_by_dve lo_by_pool piece_used meta_done at_done xt_done
            bias_used g_ready act_ready sel_ready idx_ready cur_ready pick_ready s_sig aT_hi_ready
            aT_lo_ready xT_hi_ready xT_lo_ready o_copied gathered scattered y_gated x_out mean_out ssq_out
            rt_out out_ready stored"""
        S = {n: sem(n) for n in names.split()}
        y_ld = [sem(f"y_loaded_{t}") for t in range(TL)]
        w_ld = [sem(f"w_loaded_{c}") for c in range(6)]

        def chunk_src(c, e):
            if c < 4:
                n0 = (c % 2) * FF + (c // 2) * CH
                return wgu_v[e, :, :, n0:n0 + CH]
            return wd_v[e, :, (c - 4) * 4:(c - 3) * 4, :]

        def chunk_dst(c):
            return slots[c][:, :].rearrange("p (k n) -> p k n", k=8 if c < 4 else 4)

        def raw_piece(i):
            q = i % PPC
            return slots[i // PPC][:, q * PIECE:(q + 1) * PIECE]

        def pair(i):
            return ps[:, 2 * i:2 * i + 2, :].rearrange("p b n -> p (b n)")

        TC_U, TU = KD // 2, KD // 2 + KD

        def T_unit(u):
            if u < TC_U:
                return hT_c[:, 2 * u:2 * u + 2, :].rearrange("p k n -> p (k n)")
            return hT_l[:, u - TC_U, :]

        def lg_bank(t):
            return 2 if t == TL - 1 else 0

        def win_tile(j):
            i = (1, 2, 0)[j // 4]
            cols_j = slice((j % 4) * P, (j % 4 + 1) * P)
            return win[i][:, :, cols_j], win_hi[j % 4], win_lo[i][:, :, cols_j]

        block = stack.enter_context(nc.Block())

        @block.sync
        def _(sp):
            def load(dst, src, name):
                sp.dma_start(dst, src).then_inc(S[name], 16)

            load(pc[:, :], cols, "ld_cols")
            load(csb[:, :], cst, "ld_cst")
            load(c_in[:, :, :], rows(ctx), "ld_ctx")
            load(x_in[:, :, :], rows(x), "ld_x")
            for i in range(4):
                load(wm_first[i][:, :, :], wm_v[:, :, i * CH:(i + 1) * CH], f"ld_wm{i}")
            load(win[1][:, :, :], win_v[:, :, CH:2 * CH], "ld_win1")
            load(wf[:, :, :], w_fourier.rearrange("g i j -> i g j"), "ld_wf")
            sp.wait_ge(S["bc_zero"], 1)
            load(bc[0:1, :, :].rearrange("p a d -> p (a d)"), b_mod[2 * D:6 * D].partition_broadcast(1), "ld_bc")
            for i in range(8):
                if i < 2:
                    sp.wait_ge(S["mod_done"], i + 1)
                else:
                    sp.wait_ge(S["z_ready"], i - 1)
                load(wm_rest[i % 2][:, :, :], wm_v[:, :, (4 + i) * CH:(5 + i) * CH], f"ld_zm{i % 2}")
                if i == 1:
                    load(win[2][:, :, :], win_v[:, :, 2 * CH:3 * CH], "ld_win2")
                    sp.wait_ge(S["wbd_zero"], 1)
                    for a, w in enumerate((rg_w_a, rg_w_x)):
                        v = w.rearrange("d (t s) i j -> s i (d t) j", s=2)
                        for h in range(2):
                            load(wbd[64 * h:64 * h + 64, a, :, 64 * h:64 * h + 64], v[h], "ld_wbd")
                if i == 2:
                    sp.wait_ge(S["mod_done"], 4)
                    load(win[0][:, :, :], win_v[:, :, 0:CH], "ld_win0")
                    load(wr[:, :, :], w_router.rearrange("(k p) e -> p k e", p=P), "ld_wr")
                    load(br[:, :], b_router.partition_broadcast(P), "ld_wr")
            for i in range(2):
                sp.wait_ge(S["z_ready"], 7 + i)
                load(wo[i][:, :, :], wo_v[:, 4 * i:4 * i + 4, :], f"ld_wo{i}")
            sp.wait_ge(S["f_done"], GT)
            load(dft_sb[:, 0, :, :], dft[0].rearrange("(m p) n -> p m n", p=P), "ld_dft")
            load(dft_sb[:, 1, :, :], dft[1].rearrange("(m p) n -> p m n", p=P), "ld_dft")
            sp.wait_ge(S["y_done"], TL)
            load(gnf[:, :], g_norm_ffn.partition_broadcast(P), "ld_gnf")
            sp.wait_ge(S["dft_done"], GT)
            load(xl[:, :, :], rows(x), "ld_xl")
            sp.wait_ge(S["pf_done"], TL)
            sp.dma_start(chunk_dst(3), chunk_src(3, 0)).then_inc(w_ld[3], 16)
            sp.wait_ge(S["ssr_done"], 1)
            load(bias_raw[0:NE, 0:2 * FF], b_gate_up, "ld_bias")
            load(bias_raw[NE:2 * NE, 0:2 * FF], b_gate_up, "ld_bias")
            load(bias_raw[0:NE, 2 * FF:], b_down, "ld_bias")
            load(bias_raw[NE:2 * NE, 2 * FF:], b_down, "ld_bias")
            sp.wait_ge(S["pr_done"], TL)
            sp.dma_start(chunk_dst(0), chunk_src(0, 0)).then_inc(w_ld[0], 16)
            sp.dma_start(chunk_dst(1), chunk_src(1, 0)).then_inc(w_ld[1], 16)
            for t in range(TL):
                sp.wait_ge(S["h_ready"], t + 1)
                sp.dma_start(h_dram[t * P:(t + 1) * P, :], h_sb[:, t, :]).then_inc(S["h_stored"], 16)
            sp.wait_ge(S["bias_ready"], 1)
            sp.dma_start(chunk_dst(2), chunk_src(2, 0)).then_inc(w_ld[2], 16)
            sp.wait_ge(S["lg_done"], TL)
            sp.dma_start(chunk_dst(5), chunk_src(5, 0)).then_inc(w_ld[5], 16)
            sp.wait_ge(S["h_stored"], 16 * TL)
            sp.wait_ge(S["gathered"], 16)
            sp.dma_start(chunk_dst(4), chunk_src(4, 0)).then_inc(w_ld[4], 16)
            sp.wait_ge(S["table_ready"], 1)
            n = sp.value_load(n_items[0:1, 0:1], min_val=NE, max_val=NI)
            with sp.Fori(1, NE) as e:
                before = sp.value_load(before_i[0:1, bass.ds(e, 1)], min_val=0, max_val=NI)
                for c in range(6):
                    mine = [i for i in range(PPC * c, PPC * (c + 1)) if i not in BY_POOL]
                    sp.wait_ge(S["lo_by_dve"], LO_DVE * before + lo_count(mine[-1])[1])
                    sp.nop(nofuse=True)
                    theirs = [i for i in range(PPC * c, PPC * (c + 1)) if i in BY_POOL]
                    if theirs:
                        sp.wait_ge(S["lo_by_pool"], LO_POOL * before + lo_count(theirs[-1])[1])
                        sp.nop(nofuse=True)
                    sp.dma_start(chunk_dst(c), chunk_src(c, e)).then_inc(w_ld[c], 16)
            sp.wait_ge(S["lo_by_dve"], LO_DVE * n)
            sp.nop(nofuse=True)
            load(gfin[:, :], g_final.partition_broadcast(P), "ld_gfin")
            sp.wait_ge(S["gathered"], 16 * (n + 1))
            sp.wait_ge(S["scattered"], 16 * (n + 2))
            for t in range(TL):
                sp.dma_start(y_sb[:, t, :], y_dram[t * P:(t + 1) * P, :]).then_inc(y_ld[t], 16)
            for t in range(TL):
                sp.wait_ge(S["out_ready"], t + 1)
                sp.dma_start(out[t * P:(t + 1) * P, :], o_sb[:, t, :]).then_inc(S["stored"], 16)
            sp.wait_ge(S["stored"], 16 * TL)

        @block.gpsimd
        def _(pool):
            nc.gpsimd.memset(wbd[:, :, :, :], 0.0).then_inc(S["wbd_zero"], 1)
            pool.wait_ge(S["ld_cst"], 16)
            nc.gpsimd.tensor_copy(beforeb[:, :], const("before"))
            nc.gpsimd.tensor_copy(onesb[:, :], ones).then_inc(S["bf_ready"], 1)
            pool.wait_ge(S["xs_ready"], TC + TL)
            nc.gpsimd.memset(bc[:, :, :], 0.0).then_inc(S["bc_zero"], 1)
            def win_part(j):
                pool.wait_ge(S["win_hi_ready"], j + 1)
                raw, hi, lo = win_tile(j)
                nc.gpsimd.tensor_tensor(lo, raw, hi[:, :, :].bitcast(F32), ALU.subtract).then_inc(S["win_lo_ready"], 1)

            for j in range(4):
                win_part(j)
            pool.wait_ge(S["film_ready"], 1)
            for i in range(2):
                nc.gpsimd.memset(xp[i][:, 0:PAD_LO], 0.0)
                nc.gpsimd.memset(xp[i][:, PAD_LO + NC:PAD_LO + NC + 3], 0.0)
                last = nc.gpsimd.memset(xp[i][:, NX - 1:NX], 0.0)
            last.then_inc(S["edges_zero"], 1)
            for k in range(KD):
                pool.wait_ge(S["hc_hi"], k + 1)
                nc.gpsimd.tensor_scalar(hT_c[:, k, :], hT_c[:, k, :], sc[:, k, 1:2], sh[:, k, 1:2], ALU.mult, ALU.add).then_inc(S["hc_t"], 1)
            for k in range(KD):
                pool.wait_ge(S["hc_t"], k + 1)
                last = nc.gpsimd.tensor_tensor(hT_c_lo[:, k, :], hT_c[:, k, :], hT_c_hi[:, k, :].bitcast(F32), ALU.subtract)
            last.then_inc(S["hc_lo"], 1)
            for j in range(4, 12):
                win_part(j)
            for n in range(2 * RT):
                d, t = n // RT, n % RT
                pool.wait_ge(S["a_ready"], n + 1)
                if n == 0:
                    pool.wait_ge(S["conv_done"], RT)
                if n >= 2:
                    pool.wait_ge(S["w_ready"], n - 1)
                nc.gpsimd.tensor_tensor(Qm[n % 2][:, :], Am[:, d, t, :], Am[:, d, t, :], ALU.mult).then_inc(S["q_ready"], 1)
            def wo_part(i, n):
                pool.wait_ge(S["wo_hi_ready"], 2 * i + n + 1)
                nc.gpsimd.tensor_tensor(wo_lo[i][:, :, n * CH:(n + 1) * CH], wo[i][:, :, n * CH:(n + 1) * CH],
                                        wo_hi[i][:, n, :, :].bitcast(F32), ALU.subtract).then_inc(S["wo_lo_ready"], 1)

            wo_part(0, 0)
            wo_part(0, 1)
            pool.wait_ge(S["ix_ready"], 3 * RT)
            nc.gpsimd.memset(zero[:, :], 0.0).then_inc(S["y_zero"], 1)
            pool.wait_ge(S["y_zero"], 1)
            pool.dma_start(rows(y_dram), zero[:, :].unsqueeze(1).to_broadcast([P, TL, D])).then_inc(S["scattered"], 16)
            wo_part(1, 0)
            wo_part(1, 1)
            pool.wait_ge(S["pf_done"], TL)
            pool.wait_ge(S["scattered"], 16)
            nc.gpsimd.memset(xg[:, :], 0.0).then_inc(S["xg_zero"], 1)
            pool.wait_ge(S["xg_zero"], 1)
            pool.wait_ge(S["ld_bias"], 64)
            nc.gpsimd.memset(bias_w[2 * NE:P, :].bitcast(F32), 0.0).then_inc(S["pool_step"], 1)
            nc.gpsimd.tensor_copy(bias_w[0:2 * NE, :], bias_raw[:, :]).then_inc(S["pool_step"], 1)
            pool.wait_ge(S["pool_step"], 2)
            for t in range(TL - 1):
                pool.wait_ge(S["h_scaled"], t + 1)
                nc.gpsimd.tensor_tensor(h_sb[:, t, :], h_sb[:, t, :], bc[:, 1, :], ALU.add).then_inc(S["h_ready"], 1)
            pool.wait_ge(S["h_ready"], TL - 1)
            nc.gpsimd.tensor_tensor(bias_w[NE:2 * NE, :], bias_raw[NE:2 * NE, :], bias_w[NE:2 * NE, :].bitcast(F32),
                                    ALU.subtract).then_inc(S["bias_ready"], 1)
            pool.wait_ge(S["bias_ready"], 1)
            pool.wait_ge(S["h_stored"], 16 * TL)

            last_row = pool.to_reg(NL - 1)

            def gather():
                pool.indirect_dma_start(xg[:, :], None, h_dram, bass.IndirectOffsetOnAxis(ap=idx_n[:, 0:1], axis=0),
                                        bounds_check=last_row, oob_is_err=False).then_inc(S["gathered"], 16)

            pool.wait_ge(S["idx_ready"], 1)
            gather()
            pool.wait_ge(S["table_ready"], 1)
            n = pool.value_load(n_items[0:1, 0:1], min_val=NE, max_val=NI)
            def lo_part(b, i):
                pool.wait_ge(S["hi_ready"], NPC * b + i + 1)
                nc.gpsimd.tensor_tensor(w_lo[i % RS][:, :], raw_piece(i), w_hi[i % RS][:, :].bitcast(F32), ALU.subtract
                                        ).then_inc(S["lo_by_pool"], 1)

            def scatter(b):
                pool.wait_ge(S["cur_ready"], b + 1)
                pool.wait_ge(S["o_copied"], 2 * b + 2)
                pool.wait_ge(S["scattered"], 16 * b + 16)
                pool.nop(nofuse=True)
                pool.indirect_dma_start(y_dram, bass.IndirectOffsetOnAxis(ap=idx_c[:, 0:1], axis=0), osb[:, :], None,
                                        bounds_check=last_row, oob_is_err=False, compute_op=ALU.add
                                        ).then_inc(S["scattered"], 16)

            with pool.Fori(0, NI + 1) as b:
                with pool.If(b <= n):
                    with pool.If(b < n):
                        lo_part(b, BY_POOL[0])
                        scatter(b)
                        lo_part(b, BY_POOL[1])
                        pool.wait_ge(S["idx_ready"], b + 2)
                        pool.wait_ge(S["xt_done"], 2 * b + 2)
                        pool.nop(nofuse=True)
                        gather()
                        lo_part(b, BY_POOL[2])
                        lo_part(b, BY_POOL[3])
                    with pool.If(b == n):
                        scatter(b)
            for t in range(TL // 2, TL):
                pool.wait_ge(y_ld[t], 16)
                nc.gpsimd.tensor_tensor(y_sb[:, t, :], y_sb[:, t, :], bc[:, 3, :], ALU.mult).then_inc(S["y_gated"], 1)

        @block.scalar
        def _(act):
            A = nc.scalar.activation
            act.wait_ge(S["ld_cols"], 16)
            a0 = COLS["c"][0]
            A(sp_t[:, 0:2, :].rearrange("p a b -> p (a b)"), pc[:, a0:a0 + 2 * KD], ACT.Sigmoid).then_inc(S["act_step"], 1)
            def norm(t0, t1, src, name):
                act.wait_ge(S[name], 16)
                for t in range(t0, t1):
                    if t:
                        act.wait_ge(S["ssq_in"], t)
                    A(junk[:, :], src[:, t - t0, :], ACT.Square, accum_out=ss[:, t:t + 1]).then_inc(S["ssq_in"], 1)
                act.wait_ge(S["mean_in"], 1 + (t0 > 0))
                A(ss[:, t0:t1], ss[:, t0:t1], ACT.Sqrt).then_inc(S["root_in"], 1)

            norm(0, TC, c_in, "ld_ctx")
            norm(TC, TC + TL, x_in, "ld_x")

            def evac_T(u):
                act.wait_ge(S["t_done"], u + 1)
                A(T_unit(u), ps[:, u % 4, :], ACT.Copy).then_inc(S["t_by_act"], 1)

            for u in range(0, TU, 2):
                evac_T(u)
            def win_part(j):
                if j % 4 == 0:
                    act.wait_ge(S[f"ld_win{(1, 2, 0)[j // 4]}"], 16)
                if j == 0:
                    act.wait_ge(S["mod_done"], 3)
                if j >= 4:
                    act.wait_ge(S[("xr_done", "gr_done")[j // 4 - 1]], j % 4 + 1)
                raw, hi, lo = win_tile(j)
                A(hi[:, :, :], raw, ACT.Copy).then_inc(S["win_hi_ready"], 1)

            for j in range(4):
                win_part(j)
            act.wait_ge(S["film_ready"], 1)
            act.wait_ge(S["t_by_dve"], TU // 2)
            act.wait_ge(S["t_by_act"], TU // 2)
            for k in range(KD):
                A(hT_l_hi[:, k, :], hT_l[:, k, :], ACT.Identity, bias=sh[:, k, 0:1], scale=sc[:, k, 0:1]).then_inc(S["hl_by_act"], 1)
            for k in range(KD):
                A(hT_c_hi[:, k, :], hT_c[:, k, :], ACT.Identity, bias=sh[:, k, 1:2], scale=sc[:, k, 1:2]).then_inc(S["hc_hi"], 1)
            act.wait_ge(S["edges_zero"], 1)
            for t in range(RT):
                act.wait_ge(S["xr_done"], t + 1)
                if t >= 2:
                    act.wait_ge(S["conv_done"], t - 1)
                A(xp[t % 2][:, PAD_LO:PAD_LO + NC], ps[:, t % 2, 0:NC], ACT.Copy)
                A(xp[t % 2][:, NC + 5:NC + 5 + NL], ps[:, 2 + t % 2, :], ACT.Copy).then_inc(S["xr_copied"], 1)
                win_part(4 + t)
            for t in range(RT):
                act.wait_ge(S["gr_done"], t + 1)
                win_part(8 + t)
                A(gelu[:, t, :], ps[:, 4 + t, :], ACT.Gelu_apprx_tanh).then_inc(S["gelu_done"], 1)
            act.wait_ge(S["sp_ready"], 1)
            A(sp_t[:, 2, :], sp_t[:, 1, :], ACT.Exp, scale=-1.0).then_inc(S["sp_ready"], 1)
            for d in range(2):
                for t in range(RT):
                    n = 2 * (RT * d + t)
                    act.wait_ge(S["gate_mm"], n + 1)
                    if d == 1 and t == 0:
                        act.wait_ge(S["root_ready"], RT)
                        act.wait_ge(S["ix_ready"], 2 * RT)
                    A(Rm[:, t, :], pair(n % 2)[:, NC:NC + NB], ACT.Sigmoid,
                      bias=pc[:, COLS["b_a"][0] + RT * d + t:COLS["b_a"][0] + RT * d + t + 1]).then_inc(S["sig_done"], 1)
                    act.wait_ge(S["gate_mm"], n + 2)
                    A(Um[:, d, t, :], pair((n + 1) % 2)[:, NC:NC + NB], ACT.Sigmoid,
                      bias=pc[:, COLS["b_x"][0] + RT * d + t:COLS["b_x"][0] + RT * d + t + 1]).then_inc(S["sig_done"], 1)
                if d == 0:
                    act.wait_ge(S["sp_ready"], 3)
                for t in range(RT):
                    m = RT * d + t
                    act.wait_ge(S["sig_done"], 2 * m + 1)
                    A(Am[:, d, t, :], Rm[:, t, :], ACT.Exp, scale=nsp[:, 0, m:m + 1]).then_inc(S["a_ready"], 1)
                for t in range(RT):
                    m = RT * d + t
                    act.wait_ge(S["a_ready"], m + 1)
                    A(Rm[:, t, :], Rm[:, t, :], ACT.Tanh, scale=nsp[:, 1, m:m + 1]).then_inc(S["th_ready"], 1)
                for t in range(RT):
                    m = RT * d + t
                    act.wait_ge(S["w_ready"], m + 1)
                    A(Rm[:, t, :], Rm[:, t, :], ACT.Sqrt).then_inc(S["root_ready"], 1)
            act.wait_ge(S["ix_ready"], 3 * RT)
            for g in range(GT):
                act.wait_ge(S["dft_done"], g + 1)
                A(sqF[:, g, :], ps[:, 4 + g, :], ACT.Square)
                A(catF[0][:, g, :], ps[:, 4 + g, :], ACT.Copy, scale=pc[:, COLS["g_f"][0] + g:COLS["g_f"][0] + g + 1]).then_inc(S["cf_copied"], 1)
            for i in range(8):
                act.wait_ge(S["z_done"], i + 1)
                A(bc[:, i // 2, (i % 2) * CH:(i % 2 + 1) * CH], ps[:, 2 + i % 2, :], ACT.Copy).then_inc(S["bc_ready"], 1)
            act.wait_ge(S["rg_ready"], RT)
            for t in range(RT):
                A(Um[:, 1, t, NC:], Um[:, 0, t, NC:], ACT.Square).then_inc(S["sqr_ready"], 1)
                A(catR[0][:, t, :], Um[:, 0, t, NC:], ACT.Copy, scale=pc[:, COLS["g_r"][0] + t:COLS["g_r"][0] + t + 1]).then_inc(S["catR_hi_ready"], 1)

            def root_heads(i):
                act.wait_ge(S["mean_heads"], i + 1)
                A(rsf[:, 2 + i, :], rsf[:, i, :], ACT.Sqrt).then_inc(S["root_heads"], 1)
                act.wait_ge(S["rsf_ready"], i + 1)

            root_heads(0)
            for t in range(TL):
                act.wait_ge(S["pf_done"], t + 1)
                A(Fb[:, t, :], pair(1 + t % 3), ACT.Copy, scale=rsf[:, 0, t:t + 1]).then_inc(S["pf_copied"], 1)
            root_heads(1)
            def square_x2(t):
                act.wait_ge(S["x2_ready"], t + 1)
                if t:
                    act.wait_ge(S["ssq_ffn"], t)
                A(junk2[:, :], xl[:, t, :], ACT.Square, accum_out=ss[:, t:t + 1]).then_inc(S["ssq_ffn"], 1)

            def root_x2(t):
                act.wait_ge(S["mean_ffn"], t + 1)
                A(rsf[:, 3, t:t + 1], rsf[:, 2, t:t + 1], ACT.Sqrt).then_inc(S["rt_ffn"], 1)

            def copy_hT2(t):
                act.wait_ge(S["ht_done"], 2 * t + 2)
                if t >= 2:
                    act.wait_ge(S["lg_done"], t - 1)
                A(hT2[t % 2][:, :, :].rearrange("p k n -> p (k n)"), pair(2 + t % 2), ACT.Copy).then_inc(S["ht_copied"], 1)

            square_x2(0)
            square_x2(1)
            root_x2(0)
            square_x2(2)
            root_x2(1)
            root_x2(2)
            copy_hT2(0)
            square_x2(3)
            root_x2(3)
            for t in range(1, TL):
                copy_hT2(t)
            act.wait_ge(S["m8_ready"], 1)
            for t in range(TL):
                last = A(ex[:, t, :], lg[:, t, :], ACT.Exp, bias=rs8[:, t:t + 1])
            last.then_inc(S["ex_ready"], 1)

            def split_xT(h, v):
                act.wait_ge(S["xt_done"], v)
                A(xT[0][:, 4 * h:4 * h + 4, :].rearrange("p k n -> p (k n)"), ps[:, h, :], ACT.Copy).then_inc(S["xT_hi_ready"], 1)

            def split_aT(j, b):
                act.wait_ge(S["at_done"], 2 * b + 1 + j)
                A(aT[0][:, 4 * j:4 * j + 4, :].rearrange("p k n -> p (k n)"), ps[:, 6, :], ACT.Copy).then_inc(S["aT_hi_ready"], 1)

            def hi_parts(b, e, i0, i1):
                for i in range(i0, i1):
                    if i % PPC == 0:
                        act.wait_ge(w_ld[i // PPC], 16 * e + 16)
                    act.wait_ge(S["piece_used"], NPC * b + i + 1)
                    A(w_hi[i % RS][:, :], raw_piece(i), ACT.Copy).then_inc(S["hi_ready"], 1)

            def gated_outputs(b):
                act.wait_ge(S["cur_ready"], b + 1)
                act.wait_ge(S["scattered"], 16 * b + 16)
                act.wait_ge(S["piece_used"], NPC * b + RS)
                for h in range(2):
                    A(osb[:, h * CH:(h + 1) * CH], ps[:, 4 + h, :], ACT.Copy, scale=gate_c[:, 0:1]).then_inc(S["o_copied"], 1)

            def sigmoid(j, b):
                act.wait_ge(S["g_ready"], 2 * b + 1 + j)
                A(sg[:, :], gb[:, :], ACT.Sigmoid, scale=ALPHA).then_inc(S["s_sig"], 1)

            split_xT(0, 1)
            split_xT(1, 2)
            act.wait_ge(S["table_ready"], 1)
            n = act.value_load(n_items[0:1, 0:1], min_val=NE, max_val=NI)
            with act.Fori(0, NI + 1) as b:
                with act.If(b <= n):
                    with act.If(b < n):
                        e = act.value_load(item_i[0:1, bass.ds(b, 1)], min_val=0, max_val=NE - 1)
                        A(table_kept[:, :], ones[:, 0:1], ACT.Sigmoid)
                        hi_parts(b, e, 0, 4)
                        gated_outputs(b)
                        hi_parts(b, e, 4, 12)
                        sigmoid(0, b)
                        hi_parts(b, e, 12, 16)
                        split_aT(0, b)
                        hi_parts(b, e, 16, 20)
                        sigmoid(1, b)
                        hi_parts(b, e, 20, 23)
                        split_aT(1, b)
                        hi_parts(b, e, 23, 24)
                        split_xT(0, 2 * b + 3)
                        split_xT(1, 2 * b + 4)
                    with act.If(b == n):
                        gated_outputs(b)
            def square_out(t):
                act.wait_ge(S["x_out"], t + 1)
                if t:
                    act.wait_ge(S["ssq_out"], t)
                A(junk3[:, :], xl[:, t, :], ACT.Square, accum_out=ss[:, t:t + 1]).then_inc(S["ssq_out"], 1)

            def root_out(t):
                act.wait_ge(S["mean_out"], t + 1)
                A(rsf[:, 1, t:t + 1], rsf[:, 0, t:t + 1], ACT.Sqrt).then_inc(S["rt_out"], 1)

            for t in range(TL):
                square_out(t)
                root_out(t)

        @block.vector
        def _(dve):
            V = nc.vector
            steps = [0]

            def link(ins):
                steps[0] += 1
                ins.then_inc(S["dve_step"], 1)
                dve.wait_ge(S["dve_step"], steps[0])

            dve.wait_ge(S["act_step"], 1)
            for s, name in enumerate(("c", "c_ctx")):
                last = V.tensor_tensor(csil[:, :, s], col(name), sp_t[:, s, :], ALU.mult)
            last.then_inc(S["csil_ready"], 1)
            dve.wait_ge(S["csil_ready"], 1)
            link(V.tensor_scalar(sp_t[:, 0, :], col("lam"), -1.0, None, ALU.mult))
            V.tensor_tensor(sp_t[:, 1, :], sp_t[:, 0, :], col("lam"), ALU.max).then_inc(S["sp_ready"], 1)
            def norm(t0, t1, i, src, dst):
                dve.wait_ge(S["ssq_in"], t1)
                V.tensor_scalar(ss[:, t0:t1], ss[:, t0:t1], 1.0 / D, EPS, ALU.mult, ALU.add).then_inc(S["mean_in"], 1)
                dve.wait_ge(S["root_in"], i + 1)
                link(V.reciprocal(ss[:, t0:t1], ss[:, t0:t1]))
                for t in range(t0, t1):
                    V.tensor_scalar(dst[:, t - t0, :], src[:, t - t0, :], ss[:, t:t + 1], None, ALU.mult).then_inc(S["xs_ready"], 1)

            def evac_T(u):
                dve.wait_ge(S["t_done"], u + 1)
                V.tensor_copy(T_unit(u), ps[:, u % 4, :]).then_inc(S["t_by_dve"], 1)

            norm(0, TC, 0, c_in, xs_c)
            norm(TC, TC + TL, 1, x_in, xs_l)
            for u in range(1, TU, 2):
                evac_T(u)
            for q in range(4):
                dve.wait_ge(S["mod_done"], q + 1)
                V.tensor_copy(mod_rows[:, q * CH:(q + 1) * CH], ps[0:2, 6 + q % 2, :]).then_inc(S["mod_copied"], 1)
            dve.wait_ge(S["mod_turned"], 1)
            mod = ps[:, 5, 0:4 * KD].rearrange("p (m s) -> p m s", s=2)
            for s in range(2):
                V.tensor_tensor(sh[:, :, s], mod[:, 0:KD, s], col("b_shift"), ALU.add)
                link(V.tensor_tensor(sc[:, :, s], mod[:, KD:2 * KD, s], col("b_scale"), ALU.add))
                last = V.scalar_tensor_tensor(sc[:, :, s], sc[:, :, s], 1.0, col("g_mix"), ALU.add, ALU.mult)
            last.then_inc(S["film_ready"], 1)
            dve.wait_ge(S["film_ready"], 1)
            dve.wait_ge(S["t_by_act"], TU // 2)
            dve.wait_ge(S["t_by_dve"], TU // 2)
            for k in range(KD):
                dve.wait_ge(S["hl_by_act"], k + 1)
                V.tensor_scalar(hT_l[:, k, :], hT_l[:, k, :], sc[:, k, 0:1], sh[:, k, 0:1], ALU.mult, ALU.add).then_inc(S["hl_t"], 1)
                dve.wait_ge(S["hl_t"], k + 1)
                V.tensor_tensor(hT_l_lo[:, k, :], hT_l[:, k, :], hT_l_hi[:, k, :].bitcast(F32), ALU.subtract).then_inc(S["hl_by_dve"], 1)
            dve.wait_ge(S["mm_done"], 1)
            for s in range(2):
                last = V.tensor_copy(MM[:, :, s, :], ps[:, 6 + s, :].rearrange("p (g j) -> p g j", g=GT))
            last.then_inc(S["mm_copied"], 1)
            def z_chunk(i):
                dve.wait_ge(S[f"ld_zm{i % 2}"], 16 * (i // 2 + 1))
                if i == 0:
                    dve.wait_ge(S["ld_bc"], 16)
                W, Z = wm_rest[i % 2], bc[:, i // 2, (i % 2) * CH:(i % 2 + 1) * CH]
                for k in range(KD):
                    ins = V.scalar_tensor_tensor(Z, W[:, k, :], csil[:, k, 0:1], Z, ALU.mult, ALU.add)
                    if k < KD - 1:
                        link(ins)
                ins.then_inc(S["z_ready"], 1)

            z_chunk(0)
            z_chunk(1)
            for t in range(RT):
                if t:
                    z_chunk(t + 1)
                dve.wait_ge(S["xr_copied"], t + 1)
                w = [pc[:, COLS["conv_w"][0] + RT * k + t:COLS["conv_w"][0] + RT * k + t + 1] for k in range(TAPS)]
                X = xp[t % 2]
                link(V.tensor_scalar(cv[:, :], X[:, 0:NX - 3], w[0], pc[:, COLS["conv_b"][0] + t:COLS["conv_b"][0] + t + 1], ALU.mult, ALU.add))
                for k in (1, 2):
                    link(V.scalar_tensor_tensor(cv[:, :], X[:, k:k + NX - 3], w[k], cv[:, :], ALU.mult, ALU.add))
                V.scalar_tensor_tensor(xc[:, t, 0:NC], X[:, 3:3 + NC], w[3], cv[:, 0:NC], ALU.mult, ALU.add)
                V.scalar_tensor_tensor(xc[:, t, NC:], X[:, 3 + LAT0:3 + LAT0 + NL], w[3], cv[:, LAT0:LAT0 + NL], ALU.mult, ALU.add
                                       ).then_inc(S["conv_done"], 1)
                dve.wait_ge(S["conv_done"], t + 1)
            for i in range(RT + 1, 8):
                z_chunk(i)
            dve.wait_ge(S["sp_ready"], 2)
            e_, s_, s2, q_ = sp_t[:, 2, :], sp_t[:, 3, :], sp_t[:, 4, :], sp_t[:, 5, :]
            link(V.tensor_scalar(s_, e_, 2.0, None, ALU.add))
            link(V.reciprocal(s_, s_))
            link(V.tensor_tensor(s_, s_, e_, ALU.mult))
            link(V.tensor_tensor(s2, s_, s_, ALU.mult))
            link(V.tensor_scalar(q_, s2, 1.0 / 17, None, ALU.mult))
            for k in (15, 13, 11, 9, 7, 5, 3):
                link(V.scalar_tensor_tensor(q_, q_, 1.0 / k, s2, ALU.add, ALU.mult))
            link(V.scalar_tensor_tensor(q_, q_, 1.0, s_, ALU.add, ALU.mult))
            link(V.tensor_scalar(s_, sp_t[:, 0, :], 0.0, None, ALU.max))
            link(V.scalar_tensor_tensor(q_, q_, 2.0, s_, ALU.mult, ALU.add))
            V.tensor_scalar(nsp[:, 0, :], q_, -RG_C, None, ALU.mult)
            V.tensor_scalar(nsp[:, 1, :], q_, RG_C, None, ALU.mult).then_inc(S["sp_ready"], 1)
            def f_copy(g):
                dve.wait_ge(S["f_done"], g + 1)
                V.tensor_copy(fT[:, g, :], ps[:, 4 + g, :]).then_inc(S["f_copied"], 1)

            def y_copy(m):
                dve.wait_ge(S["y_done"], m + 1)
                v = pair(2 + m % 2).rearrange("p (g s j) -> p g s j", g=GT, s=2)
                for s in range(2):
                    last = V.tensor_copy(Y[:, m, s, :].rearrange("p (g j) -> p g j", g=GT), v[:, :, s, :])
                last.then_inc(S["y_copied"], 1)

            def ix(d):
                for t in range(RT):
                    dve.wait_ge(S["sig_done"], 2 * (RT * d + t) + 2)
                    V.tensor_tensor(Um[:, d, t, :], Um[:, d, t, :], xc[:, t, :], ALU.mult).then_inc(S["ix_ready"], 1)

            def drive(d):
                for t in range(RT):
                    m = RT * d + t
                    dve.wait_ge(S["q_ready"], m + 1)
                    dve.wait_ge(S["th_ready"], m + 1)
                    V.scalar_tensor_tensor(Rm[:, t, :], Qm[m % 2][:, :], 1.0, Rm[:, t, :], ALU.add, ALU.mult).then_inc(S["w_ready"], 1)
                for t in range(RT):
                    m = RT * d + t
                    dve.wait_ge(S["root_ready"], m + 1)
                    V.tensor_tensor(Um[:, d, t, :], Um[:, d, t, :], Rm[:, t, :], ALU.mult).then_inc(S["ix_ready"], 1)

            def scan(d):
                for t in range(RT):
                    a, u = Am[:, d, t, :], Um[:, d, t, :]
                    if t == 0:
                        dve.wait_ge(S["ix_ready"], 2 * RT * (d + 1))
                        if d == 1:
                            dve.wait_ge(S["a_ready"], 2 * RT)
                    if d == 0:
                        link(V.tensor_tensor_scan(u[:, 0:NC], a[:, 0:NC], u[:, 0:NC], 0.0, ALU.mult, ALU.add))
                        link(V.tensor_tensor_scan(u[:, NC:], a[:, NC:], u[:, NC:], u[:, NC - 1:NC], ALU.mult, ALU.add))
                    else:
                        link(V.tensor_tensor_scan(u[:, 0:NC][:, ::-1], a[:, 0:NC][:, ::-1], u[:, 0:NC][:, ::-1], 0.0, ALU.mult, ALU.add))
                        link(V.tensor_tensor_scan(u[:, NC:][:, ::-1], a[:, NC:][:, ::-1], u[:, NC:][:, ::-1], u[:, 0:1], ALU.mult, ALU.add))

            for g in range(GT):
                f_copy(g)
            ix(0)
            for m in range(TL):
                y_copy(m)
            drive(0)
            scan(0)
            ix(1)
            drive(1)

            def round_wo(i):
                dve.wait_ge(S[f"ld_wo{i}"], 16)
                for n in range(2):
                    V.tensor_copy(wo_hi[i][:, n, :, :], wo[i][:, :, n * CH:(n + 1) * CH]).then_inc(S["wo_hi_ready"], 1)

            dve.wait_ge(S["ix_ready"], 4 * RT)
            round_wo(0)
            for g in range(GT):
                dve.wait_ge(S["cf_copied"], g + 1)
                V.scalar_tensor_tensor(catF[1][:, g, :], ps[:, 4 + g, :], pc[:, COLS["g_f"][0] + g:COLS["g_f"][0] + g + 1],
                                       catF[0][:, g, :].bitcast(F32), ALU.mult, ALU.subtract).then_inc(S["cf_lo"], 1)
            scan(1)
            for t in range(RT):
                link(V.tensor_tensor(Um[:, 0, t, NC:], Um[:, 0, t, NC:], Um[:, 1, t, NC:], ALU.add))
                V.tensor_tensor(Um[:, 0, t, NC:], Um[:, 0, t, NC:], gelu[:, t, :], ALU.mult).then_inc(S["rg_ready"], 1)

            def rstd_heads(i, name):
                dve.wait_ge(S[name], 1)
                V.tensor_scalar(rsf[:, i, :], ps[:, 0, TL * i:TL * (i + 1)], 1.0 / DF, EPS, ALU.mult, ALU.add).then_inc(S["mean_heads"], 1)
                dve.wait_ge(S["root_heads"], i + 1)
                V.reciprocal(rsf[:, i, :], rsf[:, 2 + i, :]).then_inc(S["rsf_ready"], 1)

            round_wo(1)
            rstd_heads(0, "ssf_done")
            for t in range(RT):
                dve.wait_ge(S["catR_hi_ready"], t + 1)
                V.scalar_tensor_tensor(catR[1][:, 0, t, NC:], Um[:, 0, t, NC:], pc[:, COLS["g_r"][0] + t:COLS["g_r"][0] + t + 1],
                                       catR[0][:, t, :].bitcast(F32), ALU.mult, ALU.subtract).then_inc(S["catR_lo_ready"], 1)
            dve.wait_ge(S["bc_ready"], 8)
            dve.wait_ge(S["ld_gnf"], 16)
            V.scalar_tensor_tensor(bc[:, 2, :], bc[:, 2, :], 1.0, gnf[:, :], ALU.add, ALU.mult).then_inc(S["bc_ready"], 1)
            rstd_heads(1, "ssr_done")
            dve.wait_ge(S["rsf_ready"], 2)
            dve.wait_ge(S["ld_xl"], 16)
            dve.wait_ge(S["bc_ready"], 9)
            def residual(t):
                dve.wait_ge(S["pr_done"], t + 1)
                dve.wait_ge(S["pf_copied"], t + 1)
                V.scalar_tensor_tensor(Fb[:, t, :], pair(1 + t % 3), rsf[:, 1, t:t + 1], Fb[:, t, :], ALU.mult, ALU.add).then_inc(S["pr_read"], 1)
                dve.wait_ge(S["pr_read"], t + 1)
                link(V.tensor_tensor(Fb[:, t, :], Fb[:, t, :], bc[:, 0, :], ALU.mult))
                V.tensor_tensor(xl[:, t, :], xl[:, t, :], Fb[:, t, :], ALU.add).then_inc(S["x2_ready"], 1)

            def ffn_norm(t):
                dve.wait_ge(S["ssq_ffn"], t + 1)
                V.tensor_scalar(rsf[:, 2, t:t + 1], ss[:, t:t + 1], 1.0 / D, EPS, ALU.mult, ALU.add).then_inc(S["mean_ffn"], 1)
                dve.wait_ge(S["rt_ffn"], t + 1)
                link(V.reciprocal(rsf[:, 3, t:t + 1], rsf[:, 3, t:t + 1]))
                V.scalar_tensor_tensor(h_sb[:, t, :], xl[:, t, :], rsf[:, 3, t:t + 1], bc[:, 2, :], ALU.mult, ALU.mult).then_inc(S["h_scaled"], 1)
                if t == TL - 1:
                    dve.wait_ge(S["h_scaled"], t + 1)
                    dve.wait_ge(S["h_ready"], t)
                    V.tensor_tensor(h_sb[:, t, :], h_sb[:, t, :], bc[:, 1, :], ALU.add).then_inc(S["h_ready"], 1)

            residual(0)
            residual(1)
            ffn_norm(0)
            residual(2)
            ffn_norm(1)
            ffn_norm(2)
            residual(3)
            ffn_norm(3)
            def pick_tokens(b, e):
                V.tensor_copy(metab[:, :, :], meta[:, :, bass.ds(e, 1), :].rearrange("p t e s -> p t (e s)"))
                V.scalar_tensor_tensor(sel[:, :, :], const("slot").unsqueeze(1).to_broadcast([P, TL, P]),
                                       item_o[:, bass.ds(b, 1)], posm[:, :, bass.ds(e, 1)].to_broadcast([P, TL, P]),
                                       ALU.add, ALU.is_equal).then_inc(S["sel_ready"], 1)

            def pick_expert(b):
                V.tensor_tensor(pick[:, :], const("expert_of_row").to_broadcast([P, P]),
                                item_e[:, bass.ds(b, 1)].to_broadcast([P, P]), ALU.is_equal).then_inc(S["pick_ready"], 1)

            def numbers(v):
                dve.wait_ge(S["meta_done"], v)
                V.tensor_copy(msb[:, :], ps[:, 7, 0:5]).then_inc(S["gate_free"], 1)
                dve.wait_ge(S["gate_free"], v)
                V.tensor_reduce(gate_n[:, :], msb[:, 2:5], AX.X, ALU.add)
                V.scalar_tensor_tensor(idx_n[:, :], msb[:, 0:1], float(OUT_OF_RANGE), msb[:, 1:2], ALU.add, ALU.add).then_inc(S["idx_ready"], 1)

            dve.wait_ge(S["ld_wr"], 32)
            for t0, t1 in ((0, TL - 1), (TL - 1, TL)):
                dve.wait_ge(S["lg_done"], t1)
                V.tensor_copy(lgT[:, t0 * P:t1 * P], ps[0:NE, lg_bank(t0), t0 * P:t1 * P]).then_inc(S["lg_copied"], 1)
            dve.wait_ge(S["lg_turned"], 1)
            link(V.tensor_tensor(lg[:, :, :], ps[:, 1, 0:TL * NE].rearrange("p (t e) -> p t e", t=TL),
                                 br[:, :].unsqueeze(1).to_broadcast([P, TL, NE]), ALU.add))
            for t in range(TL):
                link(V.max(m8[:, t, :], lg[:, t, :]))
                last = V.max_index(i8[:, t, :], m8[:, t, :], lg[:, t, :])
            V.tensor_scalar(rs8[:, 0:TL], m8[:, :, 0], -1.0, None, ALU.mult).then_inc(S["m8_ready"], 1)
            dve.wait_ge(S["m8_ready"], 1)
            link(V.tensor_copy(if8[:, :, :], i8[:, :, :]))
            exp_bc = const("expert").unsqueeze(1).to_broadcast([P, TL, NE])
            link(V.tensor_tensor(msk[:, :, :], exp_bc, if8[:, :, 0:1].to_broadcast([P, TL, NE]), ALU.is_equal))
            for k in range(1, TOPK):
                link(V.tensor_tensor(one[:, :, :], exp_bc, if8[:, :, k:k + 1].to_broadcast([P, TL, NE]), ALU.is_equal))
                link(V.tensor_tensor(msk[:, :, :], msk[:, :, :], one[:, :, :], ALU.add))
            V.tensor_copy(mskb[:, :, :], msk[:, :, :]).then_inc(S["mask_ready"], 1)
            dve.wait_ge(S["ex_ready"], 1)
            link(V.tensor_tensor(ex[:, :, :], ex[:, :, :], msk[:, :, :], ALU.mult))
            link(V.tensor_reduce(rs8[:, 4:4 + TL], ex[:, :, :], AX.X, ALU.add))
            link(V.reciprocal(rs8[:, 4:4 + TL], rs8[:, 4:4 + TL]))
            link(V.tensor_tensor(gts[:, :, :], ex[:, :, :], rs8[:, 4:4 + TL].unsqueeze(2).to_broadcast([P, TL, NE]), ALU.mult))
            link(V.tensor_copy(meta[:, :, :, 2], gts[:, :, :]))
            link(V.tensor_tensor(gtr[:, :, :], gts[:, :, :], meta[:, :, :, 2], ALU.subtract))
            link(V.tensor_copy(meta[:, :, :, 3], gtr[:, :, :]))
            link(V.tensor_tensor(gts[:, :, :], gtr[:, :, :], meta[:, :, :, 3], ALU.subtract))
            link(V.tensor_copy(meta[:, :, :, 4], gts[:, :, :]))
            tok = const("token").rearrange("p (t s) -> p t s", s=2).unsqueeze(2).to_broadcast([P, TL, NE, 2])
            link(V.tensor_copy(meta[:, :, :, 0:2], tok))
            dve.wait_ge(S["pos_done"], 1)
            link(V.scalar_tensor_tensor(posm[:, :, :], ps[:, 1, 0:TL * NE].rearrange("p (t e) -> p t e", t=TL), 1.0,
                                        msk[:, :, :], ALU.add, ALU.mult))
            link(V.tensor_scalar(posm[:, :, :], posm[:, :, :], -1.0, None, ALU.add))
            link(V.tensor_scalar(blocks[:, :], ps[0:NE, 3, 0:1], float(P), 1.0, ALU.is_gt, ALU.add))
            for j in range(2, NL // P):
                last = V.scalar_tensor_tensor(blocks[:, :], ps[0:NE, 3, 0:1], float(P * j), blocks[:, :], ALU.is_gt, ALU.add)
                if j < NL // P - 1:
                    link(last)
            last.then_inc(S["blocks_ready"], 1)
            V.memset(gate_c[:, :], 0.0)
            V.memset(idx_c[:, :], OUT_OF_RANGE).then_inc(S["cur_ready"], 1)
            V.memset(item_e[:, 0:1], 0.0)
            link(V.memset(item_o[:, 0:1], 0.0))
            pick_tokens(0, 0)
            pick_expert(0)
            dve.wait_ge(S["begin_done"], 1)
            link(V.tensor_tensor(ends[:, :], ps[0:NE, 4, 0:1], blocks[:, :], ALU.add))
            link(V.tensor_scalar(ended[:, 0, :], item_no[0:NE, :], ends[:, 0:1], None, ALU.is_ge))
            V.tensor_scalar(ended[:, 1, :], ended[:, 0, :], blocks[:, 0:1], None, ALU.mult).then_inc(S["ended_ready"], 1)
            numbers(1)
            link(V.tensor_copy(cnt[:, :], ps[:, 2, 0:NE]))
            link(V.tensor_scalar(ovf[:, :], cnt[:, :], float(P), 1.0, ALU.is_gt, ALU.add))
            for j in range(2, NL // P):
                link(V.scalar_tensor_tensor(ovf[:, :], cnt[:, :], float(P * j), ovf[:, :], ALU.is_gt, ALU.add))
            link(V.tensor_tensor_scan(end[:, :], ones[:, 0:NE], ovf[:, :], 0.0, ALU.mult, ALU.add))
            V.scalar_tensor_tensor(before_i[:, :], end[:, :], -1.0, ovf[:, :], ALU.add, ALU.subtract)
            V.memset(item_e[:, NI:], 0.0)
            V.memset(item_o[:, NI:], 0.0)
            dve.wait_ge(S["pick_ready"], 1)
            dve.wait_ge(S["sel_ready"], 1)
            dve.wait_ge(S["items_done"], 1)
            link(V.tensor_scalar(item_e[:, 0:NI], ps[:, 5, 0:NI], float(NE - 1), None, ALU.min))
            link(V.scalar_tensor_tensor(item_o[:, 0:NI], ps[:, 5, NI:2 * NI], -1.0, item_no, ALU.mult, ALU.add))
            link(V.tensor_scalar(item_o[:, 0:NI], item_o[:, 0:NI], float(P), None, ALU.mult))
            V.tensor_copy(item_i[:, :], item_e[:, :])
            V.tensor_copy(n_items[:, :], end[:, NE - 1:NE]).then_inc(S["table_ready"], 1)
            dve.wait_ge(S["table_ready"], 1)

            def split_xT(h, v):
                dve.wait_ge(S["xT_hi_ready"], v)
                V.tensor_tensor(xT[1][:, 4 * h:4 * h + 4, :].rearrange("p k n -> p (k n)"), ps[:, h, :],
                                xT[0][:, 4 * h:4 * h + 4, :].rearrange("p k n -> p (k n)").bitcast(F32), ALU.subtract
                                ).then_inc(S["xT_lo_ready"], 1)

            def split_aT(j, b):
                dve.wait_ge(S["aT_hi_ready"], 2 * b + 1 + j)
                V.tensor_tensor(aT[1][:, 4 * j:4 * j + 4, :].rearrange("p k n -> p (k n)"), ps[:, 6, :],
                                aT[0][:, 4 * j:4 * j + 4, :].rearrange("p k n -> p (k n)").bitcast(F32), ALU.subtract
                                ).then_inc(S["aT_lo_ready"], 1)

            def lo_parts(b, i0, i1):
                for i in range(i0, i1):
                    if i not in BY_POOL:
                        dve.wait_ge(S["hi_ready"], NPC * b + i + 1)
                        V.tensor_tensor(w_lo[i % RS][:, :], raw_piece(i), w_hi[i % RS][:, :].bitcast(F32), ALU.subtract
                                        ).then_inc(S["lo_by_dve"], 1)

            dve.wait_ge(S["scattered"], 16)
            V.memset(rs8[:, :], 0.0).then_inc(S["piece_used"], RS)
            split_xT(0, 1)
            split_xT(1, 2)

            def swiglu(j, b):
                dve.wait_ge(S["piece_used"], NPC * b + 2 * PPC * (j + 1) + RS)
                V.tensor_scalar(gb[:, :], ps[:, 2 * j, :], LIMIT, None, ALU.min).then_inc(S["g_ready"], 1)
                V.tensor_scalar(ub[:, :], ps[:, 2 * j + 1, :], LIMIT, -LIMIT, ALU.min, ALU.max).then_inc(S["dve_u"], 1)
                dve.wait_ge(S["g_ready"], 2 * b + 1 + j)
                dve.wait_ge(S["dve_u"], 4 * b + 2 * j + 1)
                V.scalar_tensor_tensor(ub[:, :], ub[:, :], 1.0, gb[:, :], ALU.add, ALU.mult).then_inc(S["dve_u"], 1)
                dve.wait_ge(S["dve_u"], 4 * b + 2 * j + 2)
                dve.wait_ge(S["s_sig"], 2 * b + 1 + j)
                V.tensor_tensor(ab[:, :], ub[:, :], sg[:, :], ALU.mult).then_inc(S["act_ready"], 1)

            n = dve.value_load(n_items[0:1, 0:1], min_val=NE, max_val=NI)
            with dve.Fori(0, NI) as b:
                with dve.If(b < n):
                    e = dve.value_load(item_i[0:1, bass.ds(b + 1, 1)], min_val=0, max_val=NE - 1)
                    lo_parts(b, 0, 4)
                    dve.wait_ge(S["meta_done"], b + 1)
                    pick_tokens(b + 1, e)
                    lo_parts(b, 4, 12)
                    swiglu(0, b)
                    lo_parts(b, 12, 13)
                    dve.wait_ge(S["scattered"], 16 * b + 32)
                    dve.wait_ge(S["o_copied"], 2 * b + 2)
                    V.tensor_copy(idx_c[:, :], idx_n[:, :])
                    V.tensor_copy(gate_c[:, :], gate_n[:, :]).then_inc(S["cur_ready"], 1)
                    dve.wait_ge(S["cur_ready"], b + 2)
                    dve.wait_ge(S["gathered"], 16 * b + 16)
                    numbers(b + 2)
                    lo_parts(b, 13, 16)
                    split_aT(0, b)
                    lo_parts(b, 16, 20)
                    swiglu(1, b)
                    lo_parts(b, 20, 23)
                    split_aT(1, b)
                    lo_parts(b, 23, 24)
                    dve.wait_ge(S["bias_used"], b + 1)
                    pick_expert(b + 1)
                    split_xT(0, 2 * b + 3)
                    split_xT(1, 2 * b + 4)
            dve.wait_ge(S["ld_gfin"], 16)

            def add_y(t):
                if t < TL // 2:
                    dve.wait_ge(y_ld[t], 16)
                    link(V.tensor_tensor(y_sb[:, t, :], y_sb[:, t, :], bc[:, 3, :], ALU.mult))
                else:
                    dve.wait_ge(S["y_gated"], t - TL // 2 + 1)
                V.tensor_tensor(xl[:, t, :], xl[:, t, :], y_sb[:, t, :], ALU.add).then_inc(S["x_out"], 1)

            def mean(t):
                dve.wait_ge(S["ssq_out"], t + 1)
                V.tensor_scalar(rsf[:, 0, t:t + 1], ss[:, t:t + 1], 1.0 / D, EPS, ALU.mult, ALU.add).then_inc(S["mean_out"], 1)

            def scaled(t):
                dve.wait_ge(S["rt_out"], t + 1)
                link(V.reciprocal(rsf[:, 1, t:t + 1], rsf[:, 1, t:t + 1]))
                V.scalar_tensor_tensor(o_sb[:, t, :], xl[:, t, :], rsf[:, 1, t:t + 1], gfin[:, :], ALU.mult, ALU.mult).then_inc(S["out_ready"], 1)

            add_y(0)
            for t in range(1, TL):
                add_y(t)
                mean(t - 1)
                if t > 1:
                    scaled(t - 2)
            scaled(TL - 2)
            mean(TL - 1)
            scaled(TL - 1)

        @block.tensor
        def _(pe):
            MMUL = nc.tensor.matmul
            pe.wait_ge(S["ld_cst"], 16)
            pe.wait_ge(S["csil_ready"], 1)

            def turn(u):
                if u < TC_U:
                    pe.wait_ge(S["xs_ready"], TC)
                else:
                    pe.wait_ge(S["xs_ready"], TC + TL)
                if u >= 4:
                    pe.wait_ge(S[("t_by_act", "t_by_dve")[u % 2]], (u - 4) // 2 + 1)
                if u < TC_U:
                    parts = [(xs_c, t, 2 * u + k) for k in range(2) for t in range(TC)]
                else:
                    parts = [(xs_l, t, u - TC_U) for t in range(TL)]
                for i, (src, t, k) in enumerate(parts):
                    last = nc.tensor.transpose(ps[:, u % 4, i * P:(i + 1) * P], src[:, t, k * P:(k + 1) * P], ident)
                last.then_inc(S["t_done"], 1)

            def mod_chunk(q):
                pe.wait_ge(S[f"ld_wm{q}"], 16)
                if q >= 2:
                    pe.wait_ge(S["mod_copied"], q - 1)
                for k in range(KD):
                    last = MMUL(ps[0:2, 6 + q % 2, :], csil[:, k, :], wm_first[q][:, k, :], start=(k == 0), stop=(k == KD - 1))
                last.then_inc(S["mod_done"], 1)

            for u in range(TU):
                turn(u)
            for q in range(4):
                mod_chunk(q)
            pe.wait_ge(S["mod_copied"], 4)
            for m in range(2 * KD):
                last = nc.tensor.transpose(ps[:, 5, 2 * m:2 * m + 2], mod_rows[:, m * P:(m + 1) * P], ident[0:2, 0:2])
            last.then_inc(S["mod_turned"], 1)
            pe.wait_ge(S["ld_wf"], 16)
            for s, name in enumerate(("cd", "neg_sd")):
                last = MMUL(ps[:, 6 + s, :], const(name), wf[:, :, :].rearrange("p g j -> p (g j)"), start=True, stop=True)
            last.then_inc(S["mm_done"], 1)
            def project(j, bank, h_hi, h_lo, n, waits=False):
                raw, hi, lo = win_tile(j)
                pe.wait_ge(S["win_lo_ready"], j + 1)
                for k in range(KD):
                    if waits:
                        pe.wait_ge(S["hl_by_dve"], k + 1)
                    MMUL(ps[:, bank, 0:n], hi[:, k, :], h_hi[:, k, :], start=(k == 0), stop=False)
                    MMUL(ps[:, bank, 0:n], hi[:, k, :], h_lo[:, k, :], start=False, stop=False)
                    last = MMUL(ps[:, bank, 0:n], lo[:, k, :], h_hi[:, k, :], start=False, stop=(k == KD - 1))
                return last

            def latents(j, bank, waits=False):
                return project(j, bank, hT_l_hi, hT_l_lo, NL, waits)

            def context(j, bank):
                return project(j, bank, hT_c_hi, hT_c_lo, NC)

            latents(0, 2, True)
            latents(1, 3)
            pe.wait_ge(S["hc_lo"], 1)
            for t in range(RT):
                if t >= 2:
                    pe.wait_ge(S["xr_copied"], t - 1)
                    latents(t, 2 + t % 2)
                context(t, t % 2).then_inc(S["xr_done"], 1)
            pe.wait_ge(S["mm_copied"], 1)
            for t in range(RT):
                latents(4 + t, 4 + t).then_inc(S["gr_done"], 1)
            for g in range(GT):
                pe.wait_ge(S["gelu_done"], g + 1)
                latents(8 + g, 4 + g).then_inc(S["f_done"], 1)

            def gates(d):
                for t in range(RT):
                    for a in range(2):
                        n = 2 * (RT * d + t) + a
                        if n == 0:
                            pe.wait_ge(S["ld_wbd"], 64)
                            pe.wait_ge(S["conv_done"], RT)
                            pe.wait_ge(S["xr_copied"], RT)
                        if n >= 2:
                            pe.wait_ge(S["sig_done"], n - 1)
                        v = pair(n % 2)
                        MMUL(v[:, NC:2 * NC], wbd[:, a, RT * d + t, :], xc[:, t, 0:NC], start=True, stop=True)
                        MMUL(v[:, 2 * NC:], wbd[:, a, RT * d + t, :], xc[:, t, NC:], start=True, stop=True).then_inc(S["gate_mm"], 1)

            def z_sum(i):
                if i >= 2:
                    pe.wait_ge(S["bc_ready"], i - 1)
                pe.wait_ge(S["z_ready"], i + 1)
                MMUL(ps[:, 2 + i % 2, :], ones, bc[:, i // 2, (i % 2) * CH:(i % 2 + 1) * CH], start=True, stop=True).then_inc(S["z_done"], 1)

            gates(0)
            pe.wait_ge(S["f_copied"], GT)
            for m in range(TL):
                if m >= 2:
                    pe.wait_ge(S["y_copied"], m - 1)
                for g in range(GT):
                    last = MMUL(pair(2 + m % 2)[:, g * 2 * P:(g + 1) * 2 * P], fT[:, g, m * P:(m + 1) * P],
                                MM[:, g, :, :].rearrange("p s j -> p (s j)"), start=True, stop=True)
                last.then_inc(S["y_done"], 1)
            pe.wait_ge(S["y_copied"], TL)
            pe.wait_ge(S["ld_dft"], 32)
            for g in range(GT):
                for m in range(TL):
                    for s in range(2):
                        last = MMUL(ps[:, 4 + g, :], Y[:, m, s, g * P:(g + 1) * P], dft_sb[:, s, m, :],
                                    start=(m == 0 and s == 0), stop=(m == TL - 1 and s == 1))
                last.then_inc(S["dft_done"], 1)
                if g == 1:
                    gates(1)
            pe.wait_ge(S["sig_done"], 4 * RT)
            for i in range(8):
                z_sum(i)
            def square_sums(i, sq, name):
                for t in range(TL):
                    for g in range(GT):
                        last = MMUL(ps[:, 0, TL * i + t:TL * i + t + 1], sq(g, t), ones[:, 0:1], start=(g == 0), stop=(g == GT - 1))
                last.then_inc(S[name], 1)

            def project_out(i, t, heads, name):
                for n in range(2):
                    if t == 0:
                        pe.wait_ge(S["wo_lo_ready"], 2 * i + n + 1)
                    for k in range(GT):
                        hi, lo = heads(k, t)
                        w_h, w_l = wo_hi[i][:, n, k, :], wo_lo[i][:, k, n * CH:(n + 1) * CH]
                        bank = ps[:, 2 * (1 + t % 3) + n, :]
                        MMUL(bank, hi, w_h, start=(k == 0), stop=False)
                        MMUL(bank, hi, w_l, start=False, stop=False)
                        last = MMUL(bank, lo, w_h, start=False, stop=(k == GT - 1))
                last.then_inc(S[name], 1)

            pe.wait_ge(S["cf_copied"], GT)
            square_sums(0, lambda g, t: sqF[:, g, t * P:(t + 1) * P], "ssf_done")
            pe.wait_ge(S["bc_ready"], 8)
            pe.wait_ge(S["cf_lo"], GT)
            for t in range(TL):
                if t >= 3:
                    pe.wait_ge(S["pf_copied"], t - 2)
                project_out(0, t, lambda k, t: [c[:, k, t * P:(t + 1) * P] for c in catF], "pf_done")
            pe.wait_ge(S["sqr_ready"], RT)
            square_sums(1, lambda g, t: Um[:, 1, g, NC + t * P:NC + (t + 1) * P], "ssr_done")
            pe.wait_ge(S["catR_lo_ready"], RT)
            pe.wait_ge(S["ld_wr"], 32)
            for t in range(TL):
                pe.wait_ge(S["pf_copied"], (TL, 2, 3)[t] if t < 3 else TL)
                if t >= 3:
                    pe.wait_ge(S["pr_read"], t - 2)
                project_out(1, t, lambda k, t: [catR[0][:, k, t * P:(t + 1) * P], catR[1][:, 0, k, NC + t * P:NC + (t + 1) * P]], "pr_done")

            def turn_h(t):
                pe.wait_ge(S["h_ready"], t + 1)
                pe.wait_ge(S["pr_read"], min(TL, t + 2))
                if t >= 2:
                    pe.wait_ge(S["ht_copied"], t - 1)
                for k in range(KD):
                    last = nc.tensor.transpose(pair(2 + t % 2)[:, k * P:(k + 1) * P], h_sb[:, t, k * P:(k + 1) * P], ident)
                    if k % 4 == 3:
                        last.then_inc(S["ht_done"], 1)

            def route(t):
                pe.wait_ge(S["ht_copied"], t + 1)
                for k in range(KD):
                    last = MMUL(ps[0:NE, lg_bank(t), t * P:(t + 1) * P], wr[:, k, :], hT2[t % 2][:, k, :], start=(k == 0), stop=(k == KD - 1))
                last.then_inc(S["lg_done"], 1)

            for t in range(TL):
                turn_h(t)
                if t:
                    route(t - 1)
            route(TL - 1)
            for t in range(TL):
                pe.wait_ge(S["lg_copied"], 1 + (t == TL - 1))
                last = nc.tensor.transpose(ps[:, 1, t * NE:(t + 1) * NE], lgT[:, t * P:(t + 1) * P], ident[0:NE, 0:NE])
            last.then_inc(S["lg_turned"], 1)
            pe.wait_ge(S["bf_ready"], 1)
            pe.wait_ge(S["mask_ready"], 1)
            for t in range(TL):
                for u in range(t):
                    MMUL(ps[:, 1, t * NE:(t + 1) * NE], onesb[:, :], mskb[:, u, :], start=(u == 0), stop=False)
                MMUL(ps[:, 1, t * NE:(t + 1) * NE], beforeb[:, :], mskb[:, t, :], start=(t == 0), stop=True)
            for t in range(TL):
                MMUL(ps[:, 2, 0:NE], onesb[:, :], mskb[:, t, :], start=(t == 0), stop=(t == TL - 1))
            for t in range(TL):
                last = MMUL(ps[0:NE, 3, 0:1], mskb[:, t, :], onesb[:, 0:1], start=(t == 0), stop=(t == TL - 1))
            last.then_inc(S["pos_done"], 1)
            pe.wait_ge(S["blocks_ready"], 1)
            MMUL(ps[0:NE, 4, 0:1], const("before")[0:NE, 0:NE], blocks[:, :], start=True, stop=True).then_inc(S["begin_done"], 1)

            def slots_meta(v):
                pe.wait_ge(S["sel_ready"], v)
                for t in range(TL):
                    last = MMUL(ps[:, 7, 0:5], sel[:, t, :], metab[:, t, :], start=(t == 0), stop=(t == TL - 1))
                last.then_inc(S["meta_done"], 1)

            def rows_to_channels(v):
                pe.wait_ge(S["gathered"], v)
                for k in range(KD):
                    last = nc.tensor.transpose(ps[:, k // 4, (k % 4) * P:(k % 4 + 1) * P], xg[:, k * P:(k + 1) * P], ident)
                    if k % 4 == 3:
                        last.then_inc(S["xt_done"], 1)

            slots_meta(1)
            pe.wait_ge(S["ended_ready"], 1)
            MMUL(ps[:, 5, 0:2 * NI], ones[0:NE, :], ended[:, :, :].rearrange("p a q -> p (a q)"), start=True, stop=True).then_inc(S["items_done"], 1)
            rows_to_channels(16)
            pe.wait_ge(S["bias_ready"], 1)

            def bias(bank, n0):
                return MMUL(ps[:, bank, :], pick[:, :], bias_w[:, n0:n0 + CH], start=True, stop=False)

            def products(b, i0, i1):
                for i in range(i0, i1):
                    pool, count = lo_count(i)
                    if pool:
                        pe.wait_ge(S["lo_by_pool"], LO_POOL * b + count)
                    else:
                        pe.wait_ge(S["lo_by_dve"], LO_DVE * b + count)
                    hi, lo = w_hi[i % RS], w_lo[i % RS]
                    for q in range(PIECE // CH):
                        c = slice(q * CH, (q + 1) * CH)
                        if i < 4 * PPC:
                            k, bank, rows_t = 2 * (i % PPC) + q, i // PPC, xT
                            stop = k == KD - 1
                        else:
                            k, bank, rows_t = i - 4 * PPC, 4 + q, aT
                            stop = k == FF // P - 1
                        MMUL(ps[:, bank, :], rows_t[0][:, k, :], hi[:, c], start=False, stop=False)
                        MMUL(ps[:, bank, :], rows_t[0][:, k, :], lo[:, c], start=False, stop=False)
                        last = MMUL(ps[:, bank, :], rows_t[1][:, k, :], hi[:, c], start=False, stop=stop)
                    last.then_inc(S["piece_used"], 1)

            def act_to_channels(j, b):
                pe.wait_ge(S["act_ready"], 2 * b + 1 + j)
                if j:
                    pe.wait_ge(S["aT_lo_ready"], 2 * b + 1)
                for k in range(4):
                    last = nc.tensor.transpose(ps[:, 6, k * P:(k + 1) * P], ab[:, k * P:(k + 1) * P], ident)
                last.then_inc(S["at_done"], 1)

            pe.wait_ge(S["table_ready"], 1)
            n = pe.value_load(n_items[0:1, 0:1], min_val=NE, max_val=NI)
            with pe.Fori(0, NI) as b:
                with pe.If(b < n):
                    pe.wait_ge(S["xT_lo_ready"], 2 * b + 2)
                    pe.wait_ge(S["pick_ready"], b + 1)
                    bias(0, 0)
                    bias(1, FF)
                    products(b, 0, 8)
                    bias(2, CH)
                    bias(3, FF + CH)
                    pe.wait_ge(S["gate_free"], b + 1)
                    slots_meta(b + 2)
                    products(b, 8, 12)
                    act_to_channels(0, b)
                    products(b, 12, 16)
                    pe.wait_ge(S["o_copied"], 2 * b + 2)
                    bias(4, 2 * FF)
                    bias(5, 2 * FF + CH).then_inc(S["bias_used"], 1)
                    pe.wait_ge(S["aT_lo_ready"], 2 * b + 1)
                    products(b, 16, 19)
                    act_to_channels(1, b)
                    products(b, 19, 20)
                    rows_to_channels(16 * b + 32)
                    pe.wait_ge(S["aT_lo_ready"], 2 * b + 2)
                    products(b, 20, 24)


_PERM = serpentine_order()


def kernel(x, c, ctx, c_ctx, w_mod, b_mod, g_norm_mix, g_norm_ffn, w_in, w_fourier, conv_w,
           conv_b, rg_w_a, rg_b_a, rg_w_x, rg_b_x, rg_lam, g_out_fourier, g_out_rg, w_out,
           w_router, b_router, w_gate_up, b_gate_up, w_down, b_down, g_final):
    import concourse.bacc as bacc
    from concourse.bass_utils import run_bass_kernel_spmd

    a = lambda t: np.ascontiguousarray(np.asarray(t))
    tiles = lambda v: np.asarray(v).reshape(-1, P).T
    bm = np.asarray(b_mod)[0]
    cols = {"c": tiles(c), "c_ctx": tiles(c_ctx), "g_mix": tiles(g_norm_mix), "b_shift": tiles(bm[:D]),
            "b_scale": tiles(bm[D:2 * D]), "conv_w": tiles(conv_w), "conv_b": tiles(conv_b), "b_a": tiles(rg_b_a),
            "b_x": tiles(rg_b_x), "lam": tiles(rg_lam), "g_f": tiles(g_out_fourier), "g_r": tiles(g_out_rg)}
    cst, dft = constants()
    arrays = {
        "x": a(np.asarray(x)[0][_PERM]), "ctx": a(ctx)[0], "w_mod": a(w_mod)[0], "b_mod": a(bm), "w_in": a(w_in)[0],
        "w_fourier": a(w_fourier)[0], "rg_w_a": a(rg_w_a)[0], "rg_w_x": a(rg_w_x)[0], "w_out": a(w_out)[0],
        "w_router": a(w_router)[0], "b_router": a(b_router)[0], "w_gate_up": a(w_gate_up)[0],
        "b_gate_up": a(b_gate_up)[0], "w_down": a(w_down)[0], "b_down": a(b_down)[0],
        "g_norm_ffn": a(g_norm_ffn)[0], "g_final": a(g_final),
        "cols": a(np.concatenate([cols[k] for k in COLS], axis=1)), "cst": cst, "dft": dft,
    }
    nc = bacc.Bacc("TRN2", target_bir_lowering=False, num_devices=1)
    args = [nc.dram_tensor(f"in_{k}", v.shape, mybir.dt.from_np(v.dtype), kind="ExternalInput").ap()
            for k, v in arrays.items()]
    out = nc.dram_tensor("out_rows", (NL, D), F32, kind="ExternalOutput").ap()
    build(nc, *args, out)
    r = run_bass_kernel_spmd(nc, [{f"in_{k}": v for k, v in arrays.items()}], core_ids=[0])
    got = np.empty((1, NL, D), np.float32)
    got[0, _PERM] = r.results[0]["out_rows"]
    return got
```
